# Optimizing a Trainium2 kernel written in Bass

```python
import math
import jax, jax.numpy as jnp
from jax import lax
import numpy as np

D_MODEL = 1024
BATCH = 1
SEQ = 1024
DEPTH = 1

MIX_WIDTH = D_MODEL
ATT_WIDTH = MIX_WIDTH // 2
SSD_WIDTH = MIX_WIDTH - ATT_WIDTH

DA_HEADS = 4
DA_HEAD_DIM = ATT_WIDTH // (2 * DA_HEADS)
DA_V_DIM = 2 * DA_HEAD_DIM
ROPE_THETA = 10000.0
Q_BLOCK = 128

SSD_HEAD_DIM = 64
SSD_HEADS = SSD_WIDTH // SSD_HEAD_DIM
SSD_GROUPS = 2
SSD_STATE = 128
SSD_CONV = 4
SSD_CHUNK = 128

PEER_HEADS = 8
PEER_NKEYS = 128
PEER_EXPERTS = PEER_NKEYS * PEER_NKEYS
PEER_TOPK = 16
PEER_DKEY = 256
PEER_TOKEN_BLOCK = 128

LN_EPS = 1e-5
RMS_EPS = 1e-5

QK_COLS = DA_HEADS * 2 * DA_HEAD_DIM
V_COLS = DA_HEADS * DA_V_DIM
SSD_BC = SSD_GROUPS * SSD_STATE
CONV_CH = SSD_WIDTH + 2 * SSD_BC
SPLIT_SIZES = [QK_COLS, QK_COLS, V_COLS, SSD_WIDTH, CONV_CH, SSD_HEADS]
IN_COLS = sum(SPLIT_SIZES)

kernel_name = 'hymba_diffattn_ssd_peer_deepnorm'

def layer_norm(x, g, b):
    xf = x.astype(jnp.float32)
    mu = xf.mean(-1, keepdims=True)
    var = jnp.square(xf - mu).mean(-1, keepdims=True)
    return ((xf - mu) * lax.rsqrt(var + LN_EPS) * g + b).astype(x.dtype)

def rms_norm(x, g):
    xf = x.astype(jnp.float32)
    ms = jnp.square(xf).mean(-1, keepdims=True)
    return (xf * lax.rsqrt(ms + RMS_EPS) * g).astype(x.dtype)

def rope_tables(positions):
    inv_freq = ROPE_THETA ** (-jnp.arange(0, DA_HEAD_DIM, 2, dtype=jnp.float32) / DA_HEAD_DIM)
    ang = positions.astype(jnp.float32)[..., None] * inv_freq
    return jnp.cos(ang)[:, :, None, None, :], jnp.sin(ang)[:, :, None, None, :]

def apply_rope(x, cos, sin):
    half = x.shape[-1] // 2
    x1, x2 = x[..., :half], x[..., half:]
    return jnp.concatenate([x1 * cos - x2 * sin, x2 * cos + x1 * sin], axis=-1).astype(x.dtype)

def diff_attention(q, k, v, lam, lambda_init, subln_g):
    b, s = q.shape[0], q.shape[1]
    qh = q.transpose(0, 2, 3, 1, 4)
    kh = k.transpose(0, 2, 3, 1, 4)
    vh = v.transpose(0, 2, 1, 3)
    scale = DA_HEAD_DIM ** -0.5
    outs = []
    for i in range(s // Q_BLOCK):
        lo, hi = i * Q_BLOCK, (i + 1) * Q_BLOCK
        sc = jnp.einsum('bhcqd,bhckd->bhcqk', qh[:, :, :, lo:hi], kh[:, :, :, :hi]).astype(jnp.float32) * scale
        qpos = lo + jnp.arange(Q_BLOCK)
        kpos = jnp.arange(hi)
        sc = jnp.where(kpos[None, :] <= qpos[:, None], sc, -jnp.inf)
        p = jax.nn.softmax(sc, axis=-1)
        w = p[:, :, 0] - lam * p[:, :, 1]
        outs.append(jnp.einsum('bhqk,bhkv->bqhv', w.astype(vh.dtype), vh[:, :, :hi]))
    o = jnp.concatenate(outs, axis=1)
    o = rms_norm(o, subln_g) * (1.0 - lambda_init)
    return o.reshape(b, s, DA_HEADS * DA_V_DIM)

def causal_depthwise_conv(u, w, bias):
    out = lax.conv_general_dilated(u, w[:, None, :], window_strides=(1,), padding=[(SSD_CONV - 1, 0)],
                                   dimension_numbers=('NWC', 'WIO', 'NWC'), feature_group_count=u.shape[-1])
    return out + bias

def segsum_exp(a):
    t = a.shape[-1]
    cs = jnp.cumsum(a, axis=-1)
    diff = cs[..., :, None] - cs[..., None, :]
    mask = jnp.tril(jnp.ones((t, t), dtype=bool))
    return jnp.exp(jnp.where(mask, diff, -jnp.inf))

def ssd_scan(x, dt, A, Bm, Cm):
    b, s, h, p = x.shape
    g, n, l = SSD_GROUPS, SSD_STATE, SSD_CHUNK
    r, c = h // g, s // l
    xd = (x.astype(jnp.float32) * dt[..., None]).reshape(b, c, l, g, r, p)
    a = (dt * A).reshape(b, c, l, g, r).transpose(0, 3, 4, 1, 2)
    Bc = Bm.astype(jnp.float32).reshape(b, c, l, g, n)
    Cc = Cm.astype(jnp.float32).reshape(b, c, l, g, n)
    a_cs = jnp.cumsum(a, axis=-1)
    Lm = segsum_exp(a)
    CB = jnp.einsum('bclgn,bcsgn->bcgls', Cc, Bc)
    y_diag = jnp.einsum('bcgls,bgrcls,bcsgrp->bclgrp', CB, Lm, xd)
    decay = jnp.exp(a_cs[..., -1:] - a_cs)
    states = jnp.einsum('bclgn,bgrcl,bclgrp->cbgrpn', Bc, decay, xd)
    chunk_decay = jnp.exp(a_cs[..., -1]).transpose(3, 0, 1, 2)

    def step(hstate, inp):
        st, dec = inp
        return hstate * dec[..., None, None] + st, hstate

    h0 = jnp.zeros((b, g, r, p, n), jnp.float32)
    _, prev = lax.scan(step, h0, (states, chunk_decay))
    y_off = jnp.einsum('bclgn,cbgrpn,bgrcl->bclgrp', Cc, prev, jnp.exp(a_cs))
    return (y_diag + y_off).reshape(b, s, h, p)

def ssd_mixer(z, xbc, dt_raw, conv_w, conv_b, dt_bias, a_log, d_skip, norm_g):
    b, s = z.shape[0], z.shape[1]
    xbc = jax.nn.silu(causal_depthwise_conv(xbc, conv_w, conv_b))
    xs, Bm, Cm = jnp.split(xbc, [SSD_WIDTH, SSD_WIDTH + SSD_BC], axis=-1)
    dt = jax.nn.softplus(dt_raw.astype(jnp.float32) + dt_bias)
    A = -jnp.exp(a_log.astype(jnp.float32))
    x4 = xs.reshape(b, s, SSD_HEADS, SSD_HEAD_DIM)
    y = ssd_scan(x4, dt, A, Bm.reshape(b, s, SSD_GROUPS, SSD_STATE), Cm.reshape(b, s, SSD_GROUPS, SSD_STATE))
    y = y + d_skip.astype(jnp.float32)[:, None] * x4.astype(jnp.float32)
    y = y.reshape(b, s, SSD_WIDTH) * jax.nn.silu(z.astype(jnp.float32))
    y = rms_norm(y.reshape(b, s, SSD_GROUPS, SSD_WIDTH // SSD_GROUPS), 1.0).reshape(b, s, SSD_WIDTH) * norm_g
    return y.astype(z.dtype)

def peer_ffn(h, w_q, sub_keys, u_tab, v_tab):
    b, s, d = h.shape
    q = jnp.einsum('bsd,dk->bsk', h, w_q).reshape(b, s, PEER_HEADS, 2, PEER_DKEY // 2)
    scores = jnp.einsum('bshcd,hcnd->bshcn', q, sub_keys).astype(jnp.float32)
    s1, i1 = lax.top_k(scores[..., 0, :], PEER_TOPK)
    s2, i2 = lax.top_k(scores[..., 1, :], PEER_TOPK)
    cand = (s1[..., :, None] + s2[..., None, :]).reshape(b, s, PEER_HEADS, PEER_TOPK * PEER_TOPK)
    cand_ids = (i1[..., :, None] * PEER_NKEYS + i2[..., None, :]).reshape(b, s, PEER_HEADS, PEER_TOPK * PEER_TOPK)
    top_s, pos = lax.top_k(cand, PEER_TOPK)
    ids = jnp.take_along_axis(cand_ids, pos, axis=-1)
    gates = jax.nn.softmax(top_s, axis=-1)
    nblk = (b * s) // PEER_TOKEN_BLOCK
    kk = PEER_HEADS * PEER_TOPK
    hb = h.reshape(nblk, PEER_TOKEN_BLOCK, d)
    idb = ids.reshape(nblk, PEER_TOKEN_BLOCK, kk)
    gb = gates.reshape(nblk, PEER_TOKEN_BLOCK, kk).astype(h.dtype)

    def apply(args):
        hx, idx, g = args
        act = jax.nn.gelu(jnp.einsum('td,tkd->tk', hx, u_tab[idx]), approximate=False) * g
        return jnp.einsum('tk,tkd->td', act, v_tab[idx])

    return lax.map(apply, (hb, idb, gb)).reshape(b, s, d)

def setup_inputs(seed: int = 0) -> dict:
    key = jax.random.key(seed)
    ks = jax.random.split(key, 24)
    beta = (8.0 * DEPTH) ** -0.25
    f32 = jnp.float32
    nrm = lambda k, shp: jax.random.normal(k, shp, f32)
    x = nrm(ks[0], (BATCH, SEQ, D_MODEL))
    offs = jax.random.randint(ks[1], (BATCH, 1), 0, 4096, dtype=jnp.int32)
    positions = offs + jnp.arange(SEQ, dtype=jnp.int32)[None, :]
    col_scale = jnp.ones((IN_COLS,), f32)
    col_scale = col_scale.at[2 * QK_COLS:2 * QK_COLS + V_COLS].set(beta)
    xs0 = 2 * QK_COLS + V_COLS + SSD_WIDTH
    col_scale = col_scale.at[xs0:xs0 + SSD_WIDTH].set(beta)
    w_in = nrm(ks[2], (DEPTH, D_MODEL, IN_COLS)) * (D_MODEL ** -0.5) * col_scale
    w_out = nrm(ks[3], (DEPTH, MIX_WIDTH, D_MODEL)) * (MIX_WIDTH ** -0.5) * beta
    lambda_q1 = nrm(ks[4], (DEPTH, DA_HEAD_DIM)) * 0.1
    lambda_k1 = nrm(ks[5], (DEPTH, DA_HEAD_DIM)) * 0.1
    lambda_q2 = nrm(ks[6], (DEPTH, DA_HEAD_DIM)) * 0.1
    lambda_k2 = nrm(ks[7], (DEPTH, DA_HEAD_DIM)) * 0.1
    subln_g = 1.0 + 0.02 * nrm(ks[8], (DEPTH, DA_V_DIM))
    conv_w = jax.random.uniform(ks[9], (DEPTH, SSD_CONV, CONV_CH), f32, -0.5, 0.5)
    conv_b = 0.02 * nrm(ks[10], (DEPTH, CONV_CH))
    dt0 = jnp.exp(jax.random.uniform(ks[11], (DEPTH, SSD_HEADS), f32, math.log(1e-3), math.log(1e-1)))
    dt_bias = dt0 + jnp.log(-jnp.expm1(-dt0))
    a_log = jnp.log(jax.random.uniform(ks[12], (DEPTH, SSD_HEADS), f32, 1.0, 16.0))
    d_skip = 1.0 + 0.1 * nrm(ks[13], (DEPTH, SSD_HEADS))
    ssd_norm_g = 1.0 + 0.02 * nrm(ks[14], (DEPTH, SSD_WIDTH))
    ln1_g = 1.0 + 0.02 * nrm(ks[15], (DEPTH, D_MODEL))
    ln1_b = 0.02 * nrm(ks[16], (DEPTH, D_MODEL))
    peer_wq = nrm(ks[17], (DEPTH, D_MODEL, PEER_HEADS * PEER_DKEY)) * (D_MODEL ** -0.5)
    peer_keys = nrm(ks[18], (DEPTH, PEER_HEADS, 2, PEER_NKEYS, PEER_DKEY // 2)) * ((PEER_DKEY // 2) ** -0.5)
    peer_u = nrm(ks[19], (DEPTH, PEER_EXPERTS, D_MODEL)) * (D_MODEL ** -0.5) * beta
    peer_v = nrm(ks[20], (DEPTH, PEER_EXPERTS, D_MODEL)) * beta
    ln2_g = 1.0 + 0.02 * nrm(ks[21], (DEPTH, D_MODEL))
    ln2_b = 0.02 * nrm(ks[22], (DEPTH, D_MODEL))
    return {'x': x, 'positions': positions, 'w_in': w_in, 'w_out': w_out,
            'lambda_q1': lambda_q1, 'lambda_k1': lambda_k1, 'lambda_q2': lambda_q2, 'lambda_k2': lambda_k2,
            'subln_g': subln_g, 'conv_w': conv_w, 'conv_b': conv_b, 'dt_bias': dt_bias, 'a_log': a_log,
            'd_skip': d_skip, 'ssd_norm_g': ssd_norm_g, 'ln1_g': ln1_g, 'ln1_b': ln1_b,
            'peer_wq': peer_wq, 'peer_keys': peer_keys, 'peer_u': peer_u, 'peer_v': peer_v,
            'ln2_g': ln2_g, 'ln2_b': ln2_b}

def reference(x, positions, w_in, w_out, lambda_q1, lambda_k1, lambda_q2, lambda_k2, subln_g,
              conv_w, conv_b, dt_bias, a_log, d_skip, ssd_norm_g, ln1_g, ln1_b,
              peer_wq, peer_keys, peer_u, peer_v, ln2_g, ln2_b):
    b, s, _ = x.shape
    alpha = (2.0 * DEPTH) ** 0.25
    cos, sin = rope_tables(positions)
    split_at = np.cumsum(SPLIT_SIZES)[:-1].tolist()
    for l in range(DEPTH):
        lambda_init = 0.8 - 0.6 * math.exp(-0.3 * l)
        proj = jnp.einsum('bsd,dk->bsk', x, w_in[l])
        q, k, v, z, xbc, dt_raw = jnp.split(proj, split_at, axis=-1)
        q = apply_rope(q.reshape(b, s, DA_HEADS, 2, DA_HEAD_DIM), cos, sin)
        k = apply_rope(k.reshape(b, s, DA_HEADS, 2, DA_HEAD_DIM), cos, sin)
        v = v.reshape(b, s, DA_HEADS, DA_V_DIM)
        lam = (jnp.exp(jnp.sum(lambda_q1[l].astype(jnp.float32) * lambda_k1[l]))
               - jnp.exp(jnp.sum(lambda_q2[l].astype(jnp.float32) * lambda_k2[l])) + lambda_init)
        att = diff_attention(q, k, v, lam, lambda_init, subln_g[l])
        ssd = ssd_mixer(z, xbc, dt_raw, conv_w[l], conv_b[l], dt_bias[l], a_log[l], d_skip[l], ssd_norm_g[l])
        mix = jnp.einsum('bsk,kd->bsd', jnp.concatenate([att, ssd], axis=-1), w_out[l])
        x = layer_norm(alpha * x + mix, ln1_g[l], ln1_b[l])
        ffn = peer_ffn(x, peer_wq[l], peer_keys[l], peer_u[l], peer_v[l])
        x = layer_norm(alpha * x + ffn, ln2_g[l], ln2_b[l])
    return x


_drawn_inputs = setup_inputs


def setup_inputs(seed=0):
    import zlib

    import numpy as np

    out = dict(_drawn_inputs(seed))
    spreads = {}
    factors = {'lambda_k1': 3.598,
     'lambda_q2': 3.764,
     'subln_g': 12.931,
     'ssd_norm_g': 11.707,
     'ln2_g': 7.521,
     'ln2_b': 7.756}
    for name, (base, spread) in spreads.items():
        noise = np.random.default_rng([zlib.crc32(name.encode()), seed]).standard_normal(out[name].shape)
        drawn = base * np.exp(spread * noise) if base else spread * noise
        out[name] = __import__('jax').numpy.asarray(drawn.astype(out[name].dtype))
    for name, factor in factors.items():
        out[name] = (out[name] * factor).astype(out[name].dtype)
    return out
```

```python
import math
from contextlib import ExitStack

import numpy as np

import concourse.bass as bass
from concourse import mybir

F32 = mybir.dt.float32
U32 = mybir.dt.uint32
I32 = mybir.dt.int32
ALU = mybir.AluOpType
ACT = mybir.ActivationFunctionType
AX = mybir.AxisListType

P = 128
ATT = SSD = 512
DA_HEADS = 4
DA_DIM = 64
DA_V = 128
HALF = DA_DIM // 2
SSD_HEADS = 8
SSD_DIM = 64
CONV = 4
LAMBDA_INIT = 0.8 - 0.6 * math.exp(-0.3 * 0)
RMS_EPS = 1e-5
FAR = -1.0e30
INV_FREQ = np.float32(10000.0) ** (-np.arange(0, DA_DIM, 2, dtype=np.float32) / np.float32(DA_DIM))
TURN = 2 * math.pi
TURN_PARTS = (6.28125, 2029 * 2.0 ** -20, TURN - 6.28125 - 2029 * 2.0 ** -20)
PI_BELOW = 3.1415925
ROUND = 1.5 * 2.0 ** 23
D = 1024
T = 1024
NT = T // P
KC = D // P
HEADS = 8
NKEYS = 128
DKEY = 256
TOPK = 16
SLOTS = HEADS * TOPK
RING = 8
DIAGS = 8
ALPHA = 2.0 ** 0.25
LN_EPS = 1e-5
NEG = -3.0e38



def build_mixer(nc, x, x_t, positions, w_in, w_out, lambdas, subln_g, conv_w, conv_b, dt_bias, a_log,
                d_skip, ssd_norm_g, ln1_g, ln1_b, x1_dram, x1t_dram):
    vec, act_, mm = nc.vector, nc.scalar, nc.tensor
    with ExitStack() as ctx:
        def sb(name, shape, dt=F32, to=None):
            return (to or ctx).enter_context(nc.sbuf_tensor(name, shape, dt))

        def sem(name):
            return ctx.enter_context(nc.semaphore(name))

        bank = [ctx.enter_context(nc.psum_tensor(f"bank{i}", [P, 512], F32)) for i in range(4)]
        wide = [ctx.enter_context(nc.psum_tensor(f"wide{i}", [P, 1024], F32)) for i in range(2)]
        bank += [w[:, i * 512:(i + 1) * 512] for w in wide for i in range(2)]

        ident = sb("ident", [P, P])
        upper = sb("upper", [P, P])
        ones = sb("ones", [P, P])
        mask_sl = sb("mask_sl", [P, 4, P])
        mask_qk = sb("mask_qk", [P, P])
        q_t = sb("q_t", [P, DA_HEADS, T])
        k_t = sb("k_t", [P, DA_HEADS, T])
        val = sb("val1", [P, NT, ATT])
        xt = sb("xt", [P, KC, T])
        w_ring = sb("w_ring", [P, 2, KC, 512])
        half_neg = sb("half_neg", [P, 4])
        lam = sb("lam", [P, 1])
        minus_lam = sb("minus_lam", [P, 1])

        const_ready = sem("const_ready")
        w_out_in = sem("w_out_in")
        step = sem("pool_step1")

        ssd = ctx.enter_context(ExitStack())
        z = sb("z", [P, NT, SSD], to=ssd)
        xbc = sb("xbc", [P, KC, CONV - 1 + T], to=ssd)
        dt_raw = sb("dt_raw", [P, NT * SSD_HEADS], to=ssd)
        proj = ExitStack()
        w_dt = sb("w_dt", [P, KC, SSD_HEADS], to=proj)
        cw = sb("cw", [P, KC, CONV], to=proj)
        cb = sb("cb", [P, KC], to=proj)
        conv = sb("conv", [P, 2, T], to=proj)
        lam_in = sb("lam_in", [P, 4, DA_DIM], to=proj)
        lam_dot = sb("lam_dot", [P, 2], to=proj)
        lam_exp = sb("lam_exp", [P, 2], to=proj)
        pos_i = sb("pos_i", [P, NT], I32, to=proj)
        pos_f = sb("pos_f", [P, NT], to=proj)
        freq = sb("freq", [P, HALF], to=proj)
        ang = sb("ang", [P, NT, HALF], to=proj)
        turns = sb("turns", [P, 2, NT, HALF], to=proj)
        trig = sb("trig", [P, 2, NT, HALF], to=proj)
        roped = sb("roped", [P, 2, ATT], to=proj)
        prod = sb("prod", [P, 2, ATT // 2], to=proj)

        chunk_in = [sem(f"chunk_in{i}") for i in range(KC)]
        w_landed = [sem(f"w_landed{i}") for i in range(2)]
        w_free = sem("w_free")
        dt_in = sem("dt_in")
        small_in = sem("small_in")
        act_group = sem("act_group")
        dve_group = sem("dve_group")
        bank_free = [sem(f"bank_free{i}") for i in range(4)]
        dt_done = sem("dt_done")
        xbc_ready = sem("xbc_ready")
        conv_ready = sem("conv_ready")
        conv_free = sem("conv_free")
        turns_ready = sem("turns_ready")
        trig_ready = sem("trig_ready")
        lam_ready = sem("lam_ready")
        lam_exped = sem("lam_exped")
        roped_ready = sem("roped_ready")
        roped_free = sem("roped_free")
        turned = sem("turned")
        turned_free = [sem(f"turned_free{i}") for i in range(2)]

        cols = {"xbc": 2048, "z": 1536, "v": 1024, "k": 512, "q": 0}
        blocks = [("xbc", 2048), ("xbc", 2560), ("z", 1536), ("v", 1024), ("k", 512), ("q", 0)]

        with nc.Block() as block:
            @block.sync
            def _(sp):
                def load(dst, n, c):
                    return sp.dma_start(dst, w_in[c * P:(c + 1) * P, blocks[n][1]:blocks[n][1] + 512])
                for c in range(KC):
                    sp.dma_start(xt[:, c, :], x_t[c * P:(c + 1) * P, :]).then_inc(chunk_in[c], 16)
                    load(w_ring[:, 0, c, :], 0, c).then_inc(chunk_in[c], 16)
                for n in range(1, len(blocks)):
                    if n >= 2:
                        sp.wait_ge(w_free, 1).then_inc(w_free, -1)
                    at = blocks[n][1]
                    sp.dma_start(w_ring[:, n % 2, :, :], w_in[:, at:at + 512].rearrange("(c p) n -> p c n", p=P))\
                        .then_inc(w_landed[n % 2], 16)

            @block.gpsimd
            def _(pool):
                pool.memset(ident[:], 0.0).then_inc(step, 1)
                pool.memset(upper[:], 1.0).then_inc(step, 1)
                pool.memset(ones[:], 1.0).then_inc(step, 1)
                pool.memset(mask_sl[:], 0.0).then_inc(step, 1)
                pool.memset(mask_qk[:], 0.0).then_inc(step, 1)
                pool.wait_ge(step, 5).then_inc(step, -5)
                pool.affine_select(out=ident[:], in_=ident[:], compare_op=ALU.not_equal, fill=1.0, base=0,
                                   pattern=[[-1, P]], channel_multiplier=1).then_inc(const_ready, 1)
                pool.affine_select(out=upper[:], in_=upper[:], compare_op=ALU.is_ge, fill=0.0, base=0,
                                   pattern=[[1, P]], channel_multiplier=-1).then_inc(const_ready, 1)
                pool.affine_select(out=mask_sl[:], in_=mask_sl[:], compare_op=ALU.is_ge, fill=FAR, base=0,
                                   pattern=[[0, 4], [1, P]], channel_multiplier=-1).then_inc(const_ready, 1)
                pool.affine_select(out=mask_qk[:], in_=mask_qk[:], compare_op=ALU.is_ge, fill=FAR, base=0,
                                   pattern=[[-1, P]], channel_multiplier=1).then_inc(const_ready, 1)

            @block.tensor
            def _(pe):
                pe.wait_ge(const_ready, 4)

                def turn(n):
                    pe.wait_ge(roped_ready, 1).then_inc(roped_ready, -1)
                    pe.wait_ge(turned_free[n % 2], 1).then_inc(turned_free[n % 2], -1)
                    for h in range(DA_HEADS):
                        last = mm.transpose(bank[5 + n % 2][:, h * P:(h + 1) * P], roped[:, n % 2, h * P:(h + 1) * P], ident[:])
                    last.then_inc(turned, 1)

                group = 0
                for n, (kind, _) in enumerate(blocks):
                    slot = n % 2
                    if n:
                        pe.wait_ge(w_landed[slot], 16).then_inc(w_landed[slot], -16)
                    for i in range(8):
                        b = group % 4
                        pe.wait_ge(bank_free[b], 1).then_inc(bank_free[b], -1)
                        for c in range(KC):
                            if n == 0 and i == 0:
                                pe.wait_ge(chunk_in[c], 32)
                            if kind == "xbc":
                                lhs = w_ring[:, slot, c, (i // 2) * P:(i // 2 + 1) * P]
                                rhs = xt[:, c, (i % 2) * 512:(i % 2 + 1) * 512]
                            else:
                                lhs, rhs = xt[:, c, i * P:(i + 1) * P], w_ring[:, slot, c, :]
                            last = mm.matmul(bank[b][:], lhs, rhs, start=(c == 0), stop=(c == KC - 1))
                            if n and i == 0 and c == 0:
                                last.then_inc(w_free, 1)
                        last.then_inc(dve_group if kind in "kq" else act_group, 1)
                        group += 1
                        if kind in "kq" and (kind == "q" or i):
                            turn((kind == "q") * 8 + i - 1)
                    if n == 1:
                        pe.wait_ge(dt_in, 16).then_inc(dt_in, -16)
                        for t in range(NT):
                            for c in range(KC):
                                last = mm.matmul(bank[4][:, t * SSD_HEADS:(t + 1) * SSD_HEADS], xt[:, c, t * P:(t + 1) * P],
                                                 w_dt[:, c, :], start=(c == 0), stop=(c == KC - 1))
                        last.then_inc(dt_done, 1)
                turn(15)

            @block.scalar
            def _(act):
                act.dma_start(pos_i[:], positions).then_inc(small_in, 16)
                for i in range(4):
                    act.dma_start(lam_in[:, i, :], lambdas[i].partition_broadcast(P)).then_inc(small_in, 16)
                act.dma_start(cw[:], conv_w).then_inc(small_in, 16)
                act.dma_start(cb[:], conv_b).then_inc(small_in, 16)
                act.dma_start(w_dt[:], w_in[:, 3072:3072 + SSD_HEADS].rearrange("(c p) n -> p c n", p=P)).then_inc(dt_in, 16)
                for b in range(4):
                    act.sem_inc(bank_free[b], 1)
                act.sem_inc(turned_free[0], 1)
                act.sem_inc(turned_free[1], 1)
                act.wait_ge(small_in, 16 * 7)
                act.wait_ge(turns_ready, 1).then_inc(turns_ready, -1)
                act_.activation(trig[:], turns[:], ACT.Sin).then_inc(trig_ready, 1)
                act.wait_ge(lam_ready, 1).then_inc(lam_ready, -1)
                act_.activation(lam_exp[:], lam_dot[:], ACT.Exp).then_inc(lam_exped, 1)

                def smooth(ch):
                    act.wait_ge(conv_ready, 1).then_inc(conv_ready, -1)
                    act_.activation(xbc[:, ch, CONV - 1:], conv[:, ch % 2, :], ACT.Silu, bias=cb[:, ch:ch + 1]).then_inc(conv_free, 1)

                group = 0
                for ch in range(KC):
                    for half in range(2):
                        act.wait_ge(act_group, 1).then_inc(act_group, -1)
                        act_.activation(xbc[:, ch, CONV - 1 + half * 512:CONV - 1 + (half + 1) * 512], bank[group % 4][:],
                                        ACT.Copy).then_inc(bank_free[group % 4], 1)
                        group += 1
                    act.drain().then_inc(xbc_ready, 1)
                    if ch:
                        smooth(ch - 1)
                smooth(KC - 1)
                for t in range(NT):
                    act.wait_ge(act_group, 1).then_inc(act_group, -1)
                    act_.activation(z[:, t, :], bank[group % 4][:], ACT.Silu).then_inc(bank_free[group % 4], 1)
                    group += 1
                for t in range(NT):
                    act.wait_ge(act_group, 1).then_inc(act_group, -1)
                    act_.activation(val[:, t, :], bank[group % 4][:], ACT.Copy).then_inc(bank_free[group % 4], 1)
                    group += 1
                for n in range(2 * NT):
                    act.wait_ge(turned, 1).then_inc(turned, -1)
                    act.sem_inc(roped_free, 1)
                    dst = (k_t if n < NT else q_t)[:, :, (n % NT) * P:(n % NT + 1) * P]
                    act_.activation(dst, bank[5 + n % 2][:].rearrange("p (h n) -> p h n", h=DA_HEADS), ACT.Copy)\
                        .then_inc(turned_free[n % 2], 1)

            @block.vector
            def _(dve):
                dve.sem_inc(conv_free, 2)
                for i in range(HALF):
                    vec.memset(freq[:, i:i + 1], float(INV_FREQ[i]))
                vec.memset(xbc[:, :, 0:CONV - 1], 0.0)
                dve.wait_ge(small_in, 16 * 7)
                vec.tensor_copy(pos_f[:], pos_i[:])
                for i in range(2):
                    vec.tensor_tensor_reduce(lam_in[:, 2 * i, :], lam_in[:, 2 * i, :], lam_in[:, 2 * i + 1, :], 1.0, 0.0,
                                             ALU.mult, ALU.add, lam_dot[:, i:i + 1])
                dve.drain().then_inc(lam_ready, 1)
                full = [P, NT, HALF]
                vec.tensor_tensor(ang[:], pos_f[:].unsqueeze(2).broadcast_to(full), freq[:].unsqueeze(1).broadcast_to(full), ALU.mult)
                dve.drain()
                for i, quarter in enumerate((0.25, 0.0)):
                    t, n = turns[:, i], trig[:, i]
                    vec.tensor_scalar(n, ang[:], 1 / TURN, quarter, ALU.mult, ALU.add)
                    dve.drain()
                    vec.tensor_scalar(n, n, ROUND, None, ALU.add)
                    dve.drain()
                    vec.tensor_scalar(n, n, ROUND, None, ALU.subtract)
                    dve.drain()
                    vec.tensor_copy(t, ang[:])
                    for part in TURN_PARTS:
                        dve.drain()
                        vec.scalar_tensor_tensor(out=t, in0=n, scalar=-part, in1=t, op0=ALU.mult, op1=ALU.add)
                    dve.drain()
                    vec.tensor_scalar(t, t, quarter * TURN, PI_BELOW, ALU.add, ALU.min)
                    dve.drain()
                    vec.tensor_scalar(t, t, -PI_BELOW, None, ALU.max)
                dve.drain().then_inc(turns_ready, 1)
                dve.wait_ge(lam_exped, 1).then_inc(lam_exped, -1)
                vec.tensor_tensor(lam[:], lam_exp[:, 0:1], lam_exp[:, 1:2], ALU.subtract)
                dve.drain()
                vec.tensor_scalar(minus_lam[:], lam[:], LAMBDA_INIT, -1.0, ALU.add, ALU.mult)

                for ch in range(KC):
                    dve.wait_ge(xbc_ready, 1).then_inc(xbc_ready, -1)
                    dve.wait_ge(conv_free, 1).then_inc(conv_free, -1)
                    vec.tensor_scalar(conv[:, ch % 2, :], xbc[:, ch, 0:T], cw[:, ch, 0:1], None, ALU.mult)
                    for i in range(1, CONV):
                        dve.drain()
                        vec.scalar_tensor_tensor(out=conv[:, ch % 2, :], in0=xbc[:, ch, i:i + T], scalar=cw[:, ch, i:i + 1],
                                                 in1=conv[:, ch % 2, :], op0=ALU.mult, op1=ALU.add)
                    dve.drain().then_inc(conv_ready, 1)
                dve.wait_ge(dt_done, 1).then_inc(dt_done, -1)
                vec.tensor_copy(dt_raw[:], bank[4][:, 0:NT * SSD_HEADS])
                dve.wait_ge(trig_ready, 1).then_inc(trig_ready, -1)
                dve.sem_inc(roped_free, 2)
                for n in range(2 * NT):
                    t, b = n % NT, n % 4
                    dve.wait_ge(dve_group, 1).then_inc(dve_group, -1)
                    src = bank[b][:].rearrange("p (g two n) -> p g two n", two=2, n=HALF)
                    dst = roped[:, n % 2, :].rearrange("p (g two n) -> p g two n", two=2, n=HALF)
                    part = [P, 2 * DA_HEADS, HALF]
                    cos = trig[:, 0, t, :].unsqueeze(1).broadcast_to(part)
                    sin = trig[:, 1, t, :].unsqueeze(1).broadcast_to(part)
                    p0, p1 = (prod[:, i, :].rearrange("p (g n) -> p g n", n=HALF) for i in range(2))
                    dve.wait_ge(roped_free, 1).then_inc(roped_free, -1)
                    vec.tensor_tensor(p0, src[:, :, 1, :], sin, ALU.mult)
                    vec.tensor_tensor(p1, src[:, :, 0, :], sin, ALU.mult)
                    vec.tensor_tensor(dst[:, :, 0, :], src[:, :, 0, :], cos, ALU.mult)
                    vec.tensor_tensor(dst[:, :, 1, :], src[:, :, 1, :], cos, ALU.mult)
                    dve.drain().then_inc(bank_free[b], 1)
                    vec.tensor_tensor(dst[:, :, 0, :], dst[:, :, 0, :], p0, ALU.subtract)
                    vec.tensor_tensor(dst[:, :, 1, :], dst[:, :, 1, :], p1, ALU.add)
                    dve.drain().then_inc(roped_ready, 1)
        proj.close()

        scan = ExitStack()
        per_head = [P, NT, SSD_HEADS]
        xs = sb("xs", [P, SSD], to=scan)
        bcs = sb("bcs", [P, 4 * P], to=scan)
        xd = sb("xd", [P, SSD], to=scan)
        xd_end = sb("xd_end", [P, SSD], to=scan)
        decay_in = sb("decay_in", [P, SSD_HEADS, P], to=scan)
        decays = sb("decays", [P, SSD_HEADS, P], to=scan)
        mixed = sb("mixed", [P, SSD_HEADS, P], to=scan)
        state = sb("state", [P, SSD], to=scan)
        ys = sb("ys", [P, SSD], to=scan)
        sq = sb("sq", [P, SSD], to=scan)
        ss = sb("ss", [P, 2], to=scan)
        rs = sb("rs", [P, 2], to=scan)
        norm_g = sb("norm_g", [P, SSD], to=scan)
        bias_dt = sb("bias_dt", [P, SSD_HEADS], to=scan)
        log_a = sb("log_a", [P, SSD_HEADS], to=scan)
        skip = sb("skip", [P, SSD_HEADS], to=scan)
        e_dt, u_dt, l_dt, dt, a, cs, ecs, dec, etot = (
            sb(n, per_head, to=scan) for n in ("e_dt", "u_dt", "l_dt", "dt", "a", "cs", "ecs", "dec", "etot"))

        vecs_in = sem("vecs_in")
        prep = sem("prep")
        prep_pe = sem("prep_pe")
        exp_done = sem("exp_done")
        prep_act = sem("prep_act")
        cs_done = sem("cs_done")
        x_done = sem("x_done")
        x_free = sem("x_free")
        bc_done = sem("bc_done")
        bc_free = sem("bc_free")
        l_in_ready = sem("l_in_ready")
        l_in_free = sem("l_in_free")
        l_done = sem("l_done")
        l_free = sem("l_free")
        xs_ready = sem("xs_ready")
        bcs_ready = sem("bcs_ready")
        bcs_for_pe = sem("bcs_for_pe")
        decays_ready = sem("decays_ready")
        chunk_free = sem("chunk_free")
        xd_ready = sem("xd_ready")
        mixed_ready = sem("mixed_ready")
        state_ready = sem("state_ready")
        st_done = sem("st_done")
        y_done = sem("y_done")
        y_banks_free = sem("y_banks_free")
        ss_ready = sem("ss_ready")
        rs_ready = sem("rs_ready")
        ys_ready = sem("ys_ready")
        yt_done = sem("yt_done")
        yt_free = sem("yt_free")
        half_ready = sem("half_ready")
        X, BC, L, YO, ST, YD, YT = bank[0], bank[1], wide[0], bank[2], bank[3], bank[6], bank[7]
        flat = "p c h -> p (c h)"

        def by_head(v):
            return v.unsqueeze(2).broadcast_to([P, SSD_HEADS, SSD_DIM])

        def heads(v):
            return v[:].rearrange("p (h d) -> p h d", d=SSD_DIM)

        with nc.Block() as block:
            @block.sync
            def _(sp):
                for dst, src in ((bias_dt, dt_bias), (log_a, a_log), (skip, d_skip), (norm_g, ssd_norm_g)):
                    sp.dma_start(dst[:], src.partition_broadcast(P)).then_inc(vecs_in, 16)
                for h in range(2):
                    sp.dma_start(w_ring[:, h, :, :], w_out[:, h * 512:(h + 1) * 512].rearrange("(c p) n -> p c n", p=P))\
                        .then_inc(w_out_in, 16)

            @block.gpsimd
            def _(pool):
                pool.memset(half_neg[:], -0.5).then_inc(half_ready, 1)
                pool.wait_ge(half_ready, 1)
                pool.wait_ge(prep, 1).then_inc(prep, -1)
                for c in range(NT):
                    pool.wait_ge(l_in_free, 1).then_inc(l_in_free, -1)
                    pool.tensor_tensor(decay_in[:], a[:, c, :].unsqueeze(2).broadcast_to([P, SSD_HEADS, P]),
                                       upper[:].unsqueeze(1).broadcast_to([P, SSD_HEADS, P]), ALU.mult).then_inc(l_in_ready, 1)
                    if c:
                        pool.wait_ge(ss_ready, 1).then_inc(ss_ready, -1)
                        pool.tensor_tensor(rs[:], ss[:], half_neg[:, 0:2], ALU.pow).then_inc(rs_ready, 1)
                pool.wait_ge(ss_ready, 1).then_inc(ss_ready, -1)
                pool.tensor_tensor(rs[:], ss[:], half_neg[:, 0:2], ALU.pow).then_inc(rs_ready, 1)

            @block.tensor
            def _(pe):
                def channels(c, i):
                    return xbc[:, i, CONV - 1 + c * P:CONV - 1 + (c + 1) * P]

                def front(c):
                    pe.wait_ge(x_free, 1).then_inc(x_free, -1)
                    for i in range(4):
                        last = mm.transpose(X[:, i * P:(i + 1) * P], channels(c, i), ident[:])
                    last.then_inc(x_done, 1)
                    pe.wait_ge(bc_free, 1).then_inc(bc_free, -1)
                    for g in range(2):
                        mm.transpose(BC[:, g * P:(g + 1) * P], channels(c, 4 + g), ident[:])
                    for g in range(2):
                        last = mm.matmul(BC[:, (2 + g) * P:(3 + g) * P], channels(c, 4 + g), channels(c, 6 + g), start=True, stop=True)
                    last.then_inc(bc_done, 1)
                    pe.wait_ge(l_free, 1).then_inc(l_free, -1)
                    pe.wait_ge(l_in_ready, 1).then_inc(l_in_ready, -1)
                    for i in range(2):
                        out = L[:, i * 512:(i + 1) * 512]
                        mm.matmul(out, ones[:], decay_in[:, 4 * i:4 * i + 4, :].rearrange("p h l -> p (h l)"), start=True, stop=False)
                        last = mm.matmul(out, ident[:], mask_sl[:].rearrange("p h l -> p (h l)"), start=False, stop=True)
                    last.then_inc(l_done, 1)

                def back(c):
                    pe.wait_ge(y_banks_free, 1).then_inc(y_banks_free, -1)
                    pe.wait_ge(state_ready, 1).then_inc(state_ready, -1)
                    for g in range(2):
                        mm.matmul(YO[:, g * 256:(g + 1) * 256], channels(c, 6 + g), state[:, g * 256:(g + 1) * 256], start=True, stop=True)
                    pe.wait_ge(xd_ready, 1).then_inc(xd_ready, -1)
                    pe.wait_ge(bcs_for_pe, 1).then_inc(bcs_for_pe, -1)
                    for g in range(2):
                        last = mm.matmul(ST[:, g * 256:(g + 1) * 256], bcs[:, g * P:(g + 1) * P], xd_end[:, g * 256:(g + 1) * 256],
                                         start=True, stop=True)
                    last.then_inc(st_done, 1)
                    pe.wait_ge(mixed_ready, 1).then_inc(mixed_ready, -1)
                    for h in range(SSD_HEADS):
                        last = mm.matmul(YD[:, h * SSD_DIM:(h + 1) * SSD_DIM], mixed[:, h, :], xd[:, h * SSD_DIM:(h + 1) * SSD_DIM],
                                         start=True, stop=True)
                    last.then_inc(y_done, 1)

                def turn(c):
                    pe.wait_ge(ys_ready, 1).then_inc(ys_ready, -1)
                    pe.wait_ge(yt_free, 1).then_inc(yt_free, -1)
                    for i in range(4):
                        last = mm.transpose(YT[:, i * P:(i + 1) * P], ys[:, i * P:(i + 1) * P], ident[:])
                    last.then_inc(yt_done, 1)

                pe.wait_ge(prep_pe, 1).then_inc(prep_pe, -1)
                mm.matmul(YD[:, 0:64], upper[:], a[:].rearrange(flat), start=True, stop=True)
                mm.matmul(YD[:, 64:128], ones[:], a[:].rearrange(flat), start=True, stop=True).then_inc(cs_done, 1)
                front(0)
                for c in range(NT):
                    back(c)
                    if c + 1 < NT:
                        front(c + 1)
                    turn(c)

            @block.scalar
            def _(act):
                for s in (x_free, bc_free, l_free, yt_free):
                    act.sem_inc(s, 1)
                act.wait_ge(vecs_in, 64)
                act.wait_ge(prep_act, 1).then_inc(prep_act, -1)
                act_.activation(e_dt[:], e_dt[:], ACT.Exp)
                act_.activation(log_a[:], log_a[:], ACT.Exp)
                act.drain().then_inc(exp_done, 1)
                act.wait_ge(prep_act, 1).then_inc(prep_act, -1)
                act_.activation(l_dt[:], u_dt[:], ACT.Ln).then_inc(exp_done, 1)
                act.wait_ge(prep_act, 1).then_inc(prep_act, -1)
                act_.activation(ecs[:], cs[:], ACT.Exp)
                act_.activation(dec[:], dec[:], ACT.Exp)
                act_.activation(etot[:], etot[:], ACT.Exp)
                act.drain().then_inc(exp_done, 1)
                act.wait_ge(prep_act, 1).then_inc(prep_act, -1)
                for c in range(NT):
                    act.wait_ge(x_done, 1).then_inc(x_done, -1)
                    act.wait_ge(chunk_free, 1).then_inc(chunk_free, -1)
                    act_.activation(xs[:], X[:], ACT.Copy)
                    act.drain().then_inc(xs_ready, 1)
                    act.sem_inc(x_free, 1)
                    act.wait_ge(bc_done, 1).then_inc(bc_done, -1)
                    act_.activation(bcs[:], BC[:], ACT.Copy)
                    act.drain().then_inc(bcs_for_pe, 1)
                    act.sem_inc(bc_free, 1)
                    act.wait_ge(l_done, 1).then_inc(l_done, -1)
                    for h in range(SSD_HEADS):
                        act_.activation(decays[:, h, :], L[:, h * P:(h + 1) * P], ACT.Exp, bias=cs[:, c, h:h + 1])
                    act.drain().then_inc(decays_ready, 1)
                    act.sem_inc(l_free, 1)
                    act.sem_inc(l_in_free, 1)
                    act.wait_ge(yt_done, 1).then_inc(yt_done, -1)
                    act_.activation(xt[:, 4:8, c * P:(c + 1) * P], YT[:].rearrange("p (i n) -> p i n", i=4), ACT.Copy).then_inc(yt_free, 1)

            @block.vector
            def _(dve):
                vec.memset(state[:], 0.0).then_inc(state_ready, 1)
                dve.sem_inc(l_in_free, 1)
                dve.sem_inc(chunk_free, 1)
                dve.sem_inc(y_banks_free, 1)
                dve.wait_ge(vecs_in, 64)
                raw = dt_raw[:].rearrange("p (c h) -> p c h", h=SSD_HEADS)
                vec.tensor_tensor(raw, raw, bias_dt[:].unsqueeze(1).broadcast_to(per_head), ALU.add)
                dve.drain()
                vec.tensor_scalar(u_dt[:], raw, -1.0, None, ALU.mult)
                dve.drain()
                vec.tensor_tensor(e_dt[:], raw, u_dt[:], ALU.min)
                dve.drain().then_inc(prep_act, 1)
                dve.wait_ge(exp_done, 1).then_inc(exp_done, -1)
                vec.tensor_scalar(u_dt[:], e_dt[:], 1.0, None, ALU.add)
                dve.drain().then_inc(prep_act, 1)
                vec.tensor_scalar(dt[:], u_dt[:], -1.0, None, ALU.add)
                dve.drain()
                vec.tensor_tensor(e_dt[:], e_dt[:], dt[:], ALU.subtract)
                dve.wait_ge(exp_done, 1).then_inc(exp_done, -1)
                vec.reciprocal(u_dt[:], u_dt[:])
                dve.drain()
                vec.tensor_tensor(e_dt[:], e_dt[:], u_dt[:], ALU.mult)
                vec.tensor_scalar(dt[:], raw, 0.0, None, ALU.max)
                dve.drain()
                vec.tensor_tensor(dt[:], dt[:], e_dt[:], ALU.add)
                dve.drain()
                vec.tensor_tensor(dt[:], dt[:], l_dt[:], ALU.add)
                vec.tensor_scalar(log_a[:], log_a[:], -1.0, None, ALU.mult)
                dve.drain()
                vec.tensor_tensor(a[:], dt[:], log_a[:].unsqueeze(1).broadcast_to(per_head), ALU.mult)
                dve.drain().then_inc(prep, 1)
                dve.sem_inc(prep_pe, 1)
                dve.wait_ge(cs_done, 1).then_inc(cs_done, -1)
                both = YD[:, 0:128].rearrange("p (k c h) -> p k c h", k=2, h=SSD_HEADS)
                vec.tensor_copy(cs[:], both[:, 0])
                vec.tensor_copy(etot[:], both[:, 1])
                dve.drain()
                vec.tensor_tensor(dec[:], etot[:], cs[:], ALU.subtract)
                dve.drain().then_inc(prep_act, 1)
                dve.wait_ge(exp_done, 1).then_inc(exp_done, -1)
                vec.tensor_scalar(cs[:], cs[:], -1.0, None, ALU.mult)
                dve.drain().then_inc(prep_act, 1)

                for c in range(NT):
                    dve.wait_ge(xs_ready, 1).then_inc(xs_ready, -1)
                    vec.tensor_tensor(heads(xd), heads(xs), by_head(dt[:, c, :]), ALU.mult)
                    dve.drain()
                    vec.tensor_tensor(heads(xd_end), heads(xd), by_head(dec[:, c, :]), ALU.mult)
                    dve.drain().then_inc(xd_ready, 1)
                    dve.wait_ge(decays_ready, 1).then_inc(decays_ready, -1)
                    for g in range(2):
                        vec.tensor_tensor(mixed[:, 4 * g:4 * g + 4, :], decays[:, 4 * g:4 * g + 4, :],
                                          bcs[:, (2 + g) * P:(3 + g) * P].unsqueeze(1).broadcast_to([P, 4, P]), ALU.mult)
                    dve.drain().then_inc(mixed_ready, 1)
                    dve.wait_ge(st_done, 1).then_inc(st_done, -1)
                    vec.tensor_tensor(heads(state), heads(state), by_head(etot[:, c, :]), ALU.mult)
                    dve.drain()
                    vec.tensor_tensor(state[:], state[:], ST[:], ALU.add)
                    dve.drain().then_inc(state_ready, 1)
                    dve.wait_ge(y_done, 1).then_inc(y_done, -1)
                    vec.tensor_tensor(heads(ys), YO[:].rearrange("p (h d) -> p h d", d=SSD_DIM), by_head(ecs[:, c, :]), ALU.mult)
                    vec.tensor_tensor(heads(sq), heads(xs), by_head(skip[:]), ALU.mult)
                    dve.drain()
                    vec.tensor_tensor(ys[:], ys[:], YD[:], ALU.add)
                    dve.drain().then_inc(y_banks_free, 1)
                    dve.sem_inc(chunk_free, 1)
                    vec.tensor_tensor(ys[:], ys[:], sq[:], ALU.add)
                    dve.drain()
                    vec.tensor_tensor(ys[:], ys[:], z[:, c, :], ALU.mult)
                    dve.drain()
                    for g in range(2):
                        part = slice(g * 256, (g + 1) * 256)
                        vec.tensor_tensor_reduce(sq[:, part], ys[:, part], ys[:, part], 1.0, 0.0, ALU.mult, ALU.add, ss[:, g:g + 1])
                    dve.drain()
                    vec.tensor_scalar(ss[:], ss[:], 1.0 / 256, RMS_EPS, ALU.mult, ALU.add)
                    dve.drain().then_inc(ss_ready, 1)
                    dve.wait_ge(rs_ready, 1).then_inc(rs_ready, -1)
                    for g in range(2):
                        part = slice(g * 256, (g + 1) * 256)
                        vec.scalar_tensor_tensor(out=ys[:, part], in0=ys[:, part], scalar=rs[:, g:g + 1], in1=norm_g[:, part],
                                                 op0=ALU.mult, op1=ALU.mult)
                    dve.drain().then_inc(ys_ready, 1)
        scan.close()
        ssd.close()

        probs = sb("probs", [P, 3, 2, T])
        wt = sb("wt", [P, 2, NT, P])
        xtile = sb("xtile", [P, D])
        res = sb("res", [P, D])
        x1 = sb("x1", [P, D])
        x1t = sb("x1t_out", [P, KC, P])
        g1 = sb("g1", [P, D])
        b1 = sb("b1", [P, D])
        att = sb("att", [P, ATT])
        att_sq = sb("att_sq", [P, ATT])
        sub_g = sb("sub_g", [P, DA_V])
        mx = sb("mx", [P, 2, 2])
        rsum = sb("rsum1", [P, 3, 2])
        rinv = sb("rinv", [P, 2])
        av = sb("av", [P, DA_HEADS])
        ar = sb("ar", [P, DA_HEADS])
        stats = sb("stats1", [P, 2, 6])
        mv = sb("mv1", [P, 2])
        var = sb("var1", [P, 1])
        rstd = sb("rstd1", [P, 1])

        norm_in = sem("norm_in")
        sc_done = [sem(f"sc_done{i}") for i in range(2)]
        sc_free = [sem(f"sc_free{i}1") for i in range(2)]
        mx_ready = [sem(f"mx_ready{i}") for i in range(2)]
        probs_ready = sem("probs_ready")
        w_ready = sem("w_ready")
        t_done = [sem(f"t_done{i}") for i in range(2)]
        t_free = [sem(f"t_free{i}") for i in range(2)]
        wt_ready = sem("wt_ready")
        pv_done = sem("pv_done")
        pv_free = sem("pv_free")
        att_copied = sem("att_copied")
        av_ready = sem("av_ready")
        ar_ready = sem("ar_ready")
        att_ready = sem("att_ready")
        mix_ready = sem("mix_ready")
        op_done = sem("op_done")
        op_free = sem("op_free")
        xtile_in = sem("xtile_in")
        xtile_free = sem("xtile_free")
        var_ready = sem("var_ready1")
        rstd_ready = sem("rstd_ready1")
        x1_ready = sem("x1_ready")
        x1_turn = sem("x1_turn")
        x1_free = sem("x1_free")
        x1_landed = sem("x1_landed")
        x1t_ready = sem("x1t_ready")
        x1t_landed = sem("x1t_landed")
        SC, TP, PV, OP = wide, bank[0:2], bank[2], bank[3]
        items = NT * DA_HEADS
        last_step = items - 1 + 12

        def tail(n, lag):
            t, rest = divmod(n - lag, DA_HEADS)
            return t if rest == 0 and 0 <= t < NT else None

        with nc.Block() as block:
            @block.sync
            def _(sp):
                for dst, src in ((g1, ln1_g), (b1, ln1_b), (sub_g, subln_g)):
                    sp.dma_start(dst[:], src.partition_broadcast(P)).then_inc(norm_in, 16)
                for t in range(NT):
                    sp.wait_ge(xtile_free, 1).then_inc(xtile_free, -1)
                    sp.dma_start(xtile[:], x[t * P:(t + 1) * P, :]).then_inc(xtile_in, 16)
                    sp.wait_ge(x1_ready, 1).then_inc(x1_ready, -1)
                    sp.dma_start(x1_dram[t * P:(t + 1) * P, :], x1[:]).then_inc(x1_landed, 16)
                    sp.wait_ge(x1t_ready, 1).then_inc(x1t_ready, -1)
                    sp.dma_start(x1t_dram[t * P:(t + 1) * P, :], x1t[:].rearrange("p c n -> p (c n)")).then_inc(x1t_landed, 16)
                sp.wait_ge(x1_landed, 16).then_inc(x1_landed, -16)
                sp.wait_ge(x1t_landed, 16).then_inc(x1t_landed, -16)

            @block.gpsimd
            def _(pool):
                for n in range(last_step + 1):
                    if tail(n, 7) is not None:
                        pool.wait_ge(av_ready, 1).then_inc(av_ready, -1)
                        pool.tensor_tensor(ar[:], av[:], half_neg[:], ALU.pow).then_inc(ar_ready, 1)
                    if tail(n, 10) is not None:
                        pool.wait_ge(var_ready, 1).then_inc(var_ready, -1)
                        pool.tensor_tensor(rstd[:], var[:], half_neg[:, 0:1], ALU.pow).then_inc(rstd_ready, 1)

            @block.tensor
            def _(pe):
                pe.wait_ge(w_out_in, 32)

                def scores(n):
                    t, h = divmod(n, DA_HEADS)
                    keys = (t + 1) * P
                    for c in range(2):
                        rows = slice(c * DA_DIM, (c + 1) * DA_DIM)
                        pe.wait_ge(sc_free[c], 1).then_inc(sc_free[c], -1)
                        for k0 in range(0, keys, 512):
                            k1 = min(keys, k0 + 512)
                            diagonal = k1 == keys
                            last = mm.matmul(SC[c][:, k0:k1], q_t[rows, h, t * P:(t + 1) * P], k_t[rows, h, k0:k1],
                                             start=True, stop=not diagonal)
                            if diagonal:
                                last = mm.matmul(SC[c][:, k1 - P:k1], ident[:], mask_qk[:], start=False, stop=True)
                        last.then_inc(sc_done[c], 1)

                def turn(n):
                    t = n // DA_HEADS
                    pe.wait_ge(w_ready, 1).then_inc(w_ready, -1)
                    for b in range(t // 4 + 1):
                        pe.wait_ge(t_free[b], 1).then_inc(t_free[b], -1)
                        for k in range(4 * b, min(4 * b + 4, t + 1)):
                            last = mm.transpose(TP[b][:, (k % 4) * P:(k % 4 + 1) * P], probs[:, n % 3, 0, k * P:(k + 1) * P], ident[:])
                        last.then_inc(t_done[b], 1)

                def weigh(n):
                    t, h = divmod(n, DA_HEADS)
                    if h == 0:
                        pe.wait_ge(pv_free, 1).then_inc(pv_free, -1)
                    pe.wait_ge(wt_ready, 1).then_inc(wt_ready, -1)
                    for k in range(t + 1):
                        last = mm.matmul(PV[:, h * P:(h + 1) * P], wt[:, n % 2, k, :], val[:, k, h * P:(h + 1) * P],
                                         start=(k == 0), stop=(k == t))
                    if h == DA_HEADS - 1:
                        last.then_inc(pv_done, 1)

                for n in range(last_step + 1):
                    if n < items:
                        scores(n)
                    if 2 <= n < items + 2:
                        turn(n - 2)
                    if 3 <= n < items + 3:
                        weigh(n - 3)
                    if tail(n, 9) is not None:
                        pe.wait_ge(att_ready, 1).then_inc(att_ready, -1)
                        pe.wait_ge(t_free[0], 1).then_inc(t_free[0], -1)
                        for i in range(4):
                            last = mm.transpose(TP[0][:, i * P:(i + 1) * P], att[:, i * P:(i + 1) * P], ident[:])
                        last.then_inc(t_done[0], 1)
                    if (t := tail(n, 10)) is not None:
                        pe.wait_ge(mix_ready, 1).then_inc(mix_ready, -1)
                        for half in range(2):
                            pe.wait_ge(op_free, 1).then_inc(op_free, -1)
                            for c in range(KC):
                                last = mm.matmul(OP[:], xt[:, c, t * P:(t + 1) * P], w_ring[:, half, c, :],
                                                 start=(c == 0), stop=(c == KC - 1))
                            last.then_inc(op_done, 1)
                    if tail(n, 12) is not None:
                        pe.wait_ge(x1_turn, 1).then_inc(x1_turn, -1)
                        for b in range(2):
                            pe.wait_ge(t_free[b], 1).then_inc(t_free[b], -1)
                            for i in range(4):
                                at = (4 * b + i) * P
                                last = mm.transpose(TP[b][:, i * P:(i + 1) * P], x1[:, at:at + P], ident[:])
                            last.then_inc(t_done[b], 1)

            @block.scalar
            def _(act):
                for s in (*t_free, *sc_free, pv_free):
                    act.sem_inc(s, 1)
                act.sem_inc(x1t_landed, 16)
                for n in range(last_step + 1):
                    if n < items:
                        keys = (n // DA_HEADS + 1) * P
                        for c in range(2):
                            act.wait_ge(mx_ready[c], 1).then_inc(mx_ready[c], -1)
                            act_.activation(probs[:, n % 3, c, 0:keys], SC[c][:, 0:keys], ACT.Exp, bias=mx[:, n % 2, c:c + 1],
                                            scale=DA_DIM ** -0.5, accum_out=rsum[:, n % 3, c:c + 1])
                            act.drain().then_inc(sc_free[c], 1)
                        act.sem_inc(probs_ready, 1)
                    if 2 <= n < items + 2:
                        m = n - 2
                        t = m // DA_HEADS
                        for b in range(t // 4 + 1):
                            k0, k1 = 4 * b, min(4 * b + 4, t + 1)
                            act.wait_ge(t_done[b], 1).then_inc(t_done[b], -1)
                            act_.activation(wt[:, m % 2, k0:k1, :].rearrange("p k n -> p (k n)"), TP[b][:, 0:(k1 - k0) * P], ACT.Copy)
                            act.drain().then_inc(t_free[b], 1)
                        act.sem_inc(wt_ready, 1)
                    if tail(n, 6) is not None:
                        act.wait_ge(pv_done, 1).then_inc(pv_done, -1)
                        act_.activation(att[:], PV[:], ACT.Copy)
                        act.drain().then_inc(pv_free, 1)
                        act.sem_inc(att_copied, 1)
                    if (t := tail(n, 9)) is not None:
                        act.wait_ge(t_done[0], 1).then_inc(t_done[0], -1)
                        act_.activation(xt[:, 0:4, t * P:(t + 1) * P], TP[0][:].rearrange("p (i n) -> p i n", i=4), ACT.Copy)
                        act.drain().then_inc(t_free[0], 1)
                        act.sem_inc(mix_ready, 1)
                    if tail(n, 12) is not None:
                        act.wait_ge(x1t_landed, 16).then_inc(x1t_landed, -16)
                        for b in range(2):
                            act.wait_ge(t_done[b], 1).then_inc(t_done[b], -1)
                            act_.activation(x1t[:, 4 * b:4 * b + 4, :].rearrange("p i n -> p (i n)"), TP[b][:], ACT.Copy)
                            act.drain().then_inc(t_free[b], 1)
                        act.sem_inc(x1t_ready, 1)
                        act.sem_inc(x1_free, 1)

            @block.vector
            def _(dve):
                dve.sem_inc(op_free, 1)
                dve.sem_inc(xtile_free, 1)
                dve.sem_inc(x1_free, 1)
                dve.sem_inc(x1_landed, 16)
                dve.wait_ge(norm_in, 48)
                vec.tensor_scalar(sub_g[:], sub_g[:], 1.0 - LAMBDA_INIT, None, ALU.mult)
                dve.drain()
                for n in range(last_step + 1):
                    if n < items:
                        keys = (n // DA_HEADS + 1) * P
                        for c in range(2):
                            dve.wait_ge(sc_done[c], 1).then_inc(sc_done[c], -1)
                            vec.tensor_reduce(mx[:, n % 2, c:c + 1], SC[c][:, 0:keys], AX.X, ALU.max)
                            dve.drain()
                            vec.tensor_scalar(mx[:, n % 2, c:c + 1], mx[:, n % 2, c:c + 1], -DA_DIM ** -0.5, None, ALU.mult)
                            dve.drain().then_inc(mx_ready[c], 1)
                    if 1 <= n < items + 1:
                        m = n - 1
                        keys = (m // DA_HEADS + 1) * P
                        p0, p1 = (probs[:, m % 3, c, 0:keys] for c in range(2))
                        dve.wait_ge(probs_ready, 1).then_inc(probs_ready, -1)
                        vec.reciprocal(rinv[:], rsum[:, m % 3, :])
                        dve.drain()
                        vec.tensor_tensor(rinv[:, 1:2], rinv[:, 1:2], minus_lam[:], ALU.mult)
                        vec.tensor_scalar(p0, p0, rinv[:, 0:1], None, ALU.mult)
                        dve.drain()
                        vec.scalar_tensor_tensor(out=p0, in0=p1, scalar=rinv[:, 1:2], in1=p0, op0=ALU.mult, op1=ALU.add)
                        dve.drain().then_inc(w_ready, 1)
                    if tail(n, 7) is not None:
                        dve.wait_ge(att_copied, 1).then_inc(att_copied, -1)
                        vec.tensor_tensor(att_sq[:], att[:], att[:], ALU.mult)
                        dve.drain()
                        vec.tensor_reduce(av[:], att_sq[:].rearrange("p (h n) -> p h n", h=DA_HEADS), AX.X, ALU.add)
                        dve.drain()
                        vec.tensor_scalar(av[:], av[:], 1.0 / DA_V, RMS_EPS, ALU.mult, ALU.add)
                        dve.drain().then_inc(av_ready, 1)
                    if tail(n, 8) is not None:
                        full = [P, DA_HEADS, DA_V]
                        by_head_ = att[:].rearrange("p (h n) -> p h n", h=DA_HEADS)
                        dve.wait_ge(ar_ready, 1).then_inc(ar_ready, -1)
                        vec.tensor_tensor(by_head_, by_head_, ar[:].unsqueeze(2).broadcast_to(full), ALU.mult)
                        dve.drain()
                        vec.tensor_tensor(by_head_, by_head_, sub_g[:].unsqueeze(1).broadcast_to(full), ALU.mult)
                        dve.drain().then_inc(att_ready, 1)
                    if tail(n, 10) is not None:
                        dve.wait_ge(xtile_in, 16).then_inc(xtile_in, -16)
                        for half in range(2):
                            part = slice(half * 512, (half + 1) * 512)
                            dve.wait_ge(op_done, 1).then_inc(op_done, -1)
                            vec.scalar_tensor_tensor(out=res[:, part], in0=xtile[:, part], scalar=ALPHA, in1=OP[:],
                                                     op0=ALU.mult, op1=ALU.add)
                            dve.drain().then_inc(op_free, 1)
                            vec.bn_stats(stats[:, half, :], res[:, part])
                        dve.drain().then_inc(xtile_free, 1)
                        vec.bn_aggr(mv[:], stats[:].rearrange("p a b -> p (a b)"))
                        dve.drain()
                        vec.tensor_scalar(var[:], mv[:, 1:2], LN_EPS, None, ALU.add)
                        dve.drain().then_inc(var_ready, 1)
                    if tail(n, 11) is not None:
                        dve.wait_ge(rstd_ready, 1).then_inc(rstd_ready, -1)
                        dve.wait_ge(x1_landed, 16).then_inc(x1_landed, -16)
                        dve.wait_ge(x1_free, 1).then_inc(x1_free, -1)
                        vec.tensor_scalar(x1[:], res[:], mv[:, 0:1], rstd[:, 0:1], ALU.subtract, ALU.mult)
                        dve.drain()
                        vec.tensor_tensor(x1[:], x1[:], g1[:], ALU.mult)
                        dve.drain()
                        vec.tensor_tensor(x1[:], x1[:], b1[:], ALU.add)
                        dve.drain().then_inc(x1_ready, 1)
                        dve.sem_inc(x1_turn, 1)


def refine_rsqrt(nc, dve, out, var, std, tmp):
    vec = nc.vector
    vec.reciprocal(out, std)
    dve.drain()
    vec.tensor_tensor(tmp, out, out, ALU.mult)
    dve.drain()
    vec.tensor_tensor(tmp, tmp, var, ALU.mult)
    dve.drain()
    vec.tensor_scalar(tmp, tmp, -0.5, 1.5, ALU.mult, ALU.add)
    dve.drain()
    vec.tensor_tensor(out, out, tmp, ALU.mult)
    dve.drain()


def build_experts(nc, x1_dram, x1t_dram, peer_wq, keys_t, peer_u, peer_v, ln2_g, ln2_b, out):
    with ExitStack() as ctx:
        def sb(name, shape, dt=F32):
            return ctx.enter_context(nc.sbuf_tensor(name, shape, dt))

        def ps(name, shape):
            return ctx.enter_context(nc.psum_tensor(name, shape, F32))

        def sem(name):
            return ctx.enter_context(nc.semaphore(name))

        wq = sb("wq", [P, KC, HEADS * DKEY])
        keys = sb("keys", [P, HEADS * 2 * NKEYS])
        u_ring = sb("u_ring", [P, RING, D])
        v_ring = sb("v_ring", [P, RING, D])
        x1t_sel = sb("x1t_sel", [P, KC, P])
        x1_u = sb("x1_u", [P, D])
        x1_v = sb("x1_v", [P, D])
        g2 = sb("g2", [P, D])
        b2 = sb("b2", [P, D])
        y = sb("y", [P, D])
        ids_all = sb("ids_all", [P, NT * SLOTS], U32)
        exp_all = sb("exp_all", [P, NT * SLOTS])
        sum_all = sb("sum_all", [P, NT * HEADS])
        coef_all = sb("coef_all", [P, NT * SLOTS])
        ids_u = sb("ids_u", [P, 2, TOPK], U32)
        ids_v = sb("ids_v", [P, 2, TOPK], U32)
        coef_v = sb("coef_v", [P, 2, TOPK])
        dots = sb("dots", [P, 2, TOPK])
        gelu = sb("gelu", [P, 2, TOPK])
        rsum = sb("rsum", [P, 1])
        zero = sb("zero2", [P, P])
        diag = sb("diag", [P, DIAGS, P])
        ident = sb("ident2", [P, P])
        alpha_ident = sb("alpha_ident", [P, P])
        q_sb = sb("q_sb", [P, DKEY])
        qt_sb = sb("qt_sb", [P, 2, P])
        val = sb("val", [P, 2, TOPK])
        idx = sb("idx", [P, 2, TOPK], U32)
        idx_f = sb("idx_f", [P, 2, TOPK])
        work = sb("work", [P, 2, NKEYS])
        cand = sb("cand", [P, TOPK, TOPK])
        cand2 = sb("cand2", [P, TOPK * TOPK])
        top = sb("top", [P, TOPK])
        neg_max = sb("neg_max", [P, 1])
        pos = sb("pos", [P, TOPK], U32)
        ab = sb("ab", [P, 2, TOPK], U32)
        ab_f = sb("ab_f", [P, 2, TOPK])
        onehot = sb("onehot", [P, 2, TOPK, TOPK])
        picked = sb("picked", [P, 2, TOPK])
        iota16 = sb("iota16", [P, TOPK])
        iota_i = sb("iota_i", [P, TOPK], I32)
        stats = sb("stats", [P, 2, 6])
        mv = sb("mv", [P, 2])
        rstd = sb("rstd", [P, 1])
        var = sb("var2", [P, 1])
        std = sb("std2", [P, 1])
        tmp = sb("tmp2", [P, 1])

        acc = [ps(f"acc{i}", [P, 512]) for i in range(2)]
        q_ps = ps("q_ps", [P, 512])
        qt_ps = ps("qt_ps", [P, 512])
        sc_ps = ps("sc_ps", [P, 512])

        weights_in = sem("weights_in2")
        ln2_in = sem("ln2_in")
        sel_in = sem("sel_in")
        sel_free = sem("sel_free")
        xu_in = sem("xu_in")
        xu_free = sem("xu_free")
        xv_in = sem("xv_in")
        xv_free = sem("xv_free")
        u_landed = [sem(f"u_landed{i}") for i in range(RING)]
        v_landed = [sem(f"v_landed{i}") for i in range(RING)]
        u_free = sem("u_free")
        v_free = sem("v_free")
        ids_ready = sem("ids_ready")
        q_done = sem("q_done")
        q_copied = sem("q_copied")
        qt_done = sem("qt_done")
        qt_copied = sem("qt_copied")
        sc_done = sem("sc_done")
        sc_free = sem("sc_free")
        top_ready = sem("top_ready")
        top_free = sem("top_free")
        dots_ready = sem("dots_ready")
        gelu_ready = sem("gelu_ready")
        coef_ready = sem("coef_ready")
        diag_ready = sem("diag_ready")
        diag_free = sem("diag_free")
        acc_done = sem("acc_done")
        acc_free = sem("acc_free")
        y_ready = sem("y_ready")
        y_free = sem("y_free")
        y_out = sem("y_out")
        var_ready = sem("var_ready2")
        std_ready = sem("std_ready2")
        consts = sem("consts2")
        zero_ready = sem("zero_ready")
        pool_step = sem("pool_step")

        def rounds(eng, body):
            body(0, True, False, False)
            body(1, True, True, False)
            with eng.Fori(2, NT) as r:
                body(r, True, True, True)
            body(NT, False, True, True)
            body(NT + 1, False, False, True)

        def groups(eng, body):
            with eng.Fori(0, HEADS // 2) as half:
                for par in range(2):
                    body(half * 2 + par, par)

        block = ctx.enter_context(nc.Block())

        @block.sync
        def _(sp):
            sp.dma_start(keys[:], keys_t).then_inc(weights_in, 16)
            for c in range(KC):
                sp.dma_start(wq[:, c, :], peer_wq[c * P:(c + 1) * P, :]).then_inc(weights_in, 16)

            def round_(r, sel, u, v, late):
                if sel:
                    sp.wait_ge(sel_free, 1).then_inc(sel_free, -1)
                    sp.dma_start(x1t_sel[:].rearrange("p c n -> p (c n)"),
                                 x1t_dram[bass.ds(r * P, P), :]).then_inc(sel_in, 16)
                if u:
                    sp.wait_ge(xu_free, 1).then_inc(xu_free, -1)
                    sp.dma_start(x1_u[:], x1_dram[bass.ds((r - 1) * P, P), :]).then_inc(xu_in, 16)
                if v:
                    sp.wait_ge(xv_free, 1).then_inc(xv_free, -1)
                    sp.dma_start(x1_v[:], x1_dram[bass.ds((r - 2) * P, P), :]).then_inc(xv_in, 16)
                if late:
                    sp.wait_ge(y_ready, 1).then_inc(y_ready, -1)
                    sp.dma_start(out[bass.ds((r - 3) * P, P), :], y[:]).then_inc(y_free, 16)

            round_(0, True, False, False, False)
            sp.dma_start(g2[:], ln2_g.partition_broadcast(P)).then_inc(ln2_in, 16)
            sp.dma_start(b2[:], ln2_b.partition_broadcast(P)).then_inc(ln2_in, 16)
            round_(1, True, True, False, False)
            round_(2, True, True, True, False)
            with sp.Fori(3, NT) as r:
                round_(r, True, True, True, True)
            round_(NT, False, True, True, True)
            round_(NT + 1, False, False, True, True)
            sp.wait_ge(y_ready, 1).then_inc(y_ready, -1)
            sp.dma_start(out[(NT - 1) * P:NT * P, :], y[:]).then_inc(y_out, 16)
            sp.wait_ge(y_out, 16)

        @block.gpsimd
        def _(pool):
            pool.iota(iota_i[:], [[1, TOPK]], base=0, channel_multiplier=0).then_inc(consts, 1)
            pool.memset(ident[:], 0.0).then_inc(pool_step, 1)
            pool.memset(alpha_ident[:], 0.0).then_inc(pool_step, 1)
            pool.wait_ge(pool_step, 2).then_inc(pool_step, -2)
            for m, diagonal in ((ident, 1.0), (alpha_ident, ALPHA)):
                pool.affine_select(out=m[:], in_=m[:], compare_op=ALU.not_equal, fill=diagonal, base=0,
                                   pattern=[[-1, P]], channel_multiplier=1).then_inc(consts, 1)

            def gather(ring, slot, table, ids, par, j, landed):
                pool.indirect_dma_start(ring[:, slot, :], None, table,
                                        bass.IndirectOffsetOnAxis(ap=ids[:, par, j:j + 1], axis=0))\
                    .then_inc(landed[slot], 16)

            def round_(r, sel, u, v):
                if not (u or v):
                    return

                def group(g, par):
                    if u:
                        pool.wait_ge(ids_ready, 1).then_inc(ids_ready, -1)
                        pool.tensor_copy(ids_u[:, par, :], ids_all[:, bass.ds(((r - 1) * HEADS + g) * TOPK, TOPK)])\
                            .then_inc(pool_step, 1)
                        pool.wait_ge(pool_step, 1).then_inc(pool_step, -1)
                    if v:
                        pool.tensor_copy(ids_v[:, par, :], ids_all[:, bass.ds(((r - 2) * HEADS + g) * TOPK, TOPK)])\
                            .then_inc(pool_step, 1)
                        pool.wait_ge(pool_step, 1).then_inc(pool_step, -1)
                    for j in range(TOPK):
                        slot = j % RING
                        if u:
                            pool.wait_ge(u_free, 1).then_inc(u_free, -1)
                            gather(u_ring, slot, peer_u, ids_u, par, j, u_landed)
                        if v:
                            pool.wait_ge(v_free, 1).then_inc(v_free, -1)
                            gather(v_ring, slot, peer_v, ids_v, par, j, v_landed)
                groups(pool, group)
            rounds(pool, round_)

        @block.tensor
        def _(pe):
            pe.sem_inc(v_free, RING)
            pe.wait_ge(consts, 3)
            pe.wait_ge(zero_ready, 1)
            pe.wait_ge(weights_in, 16 * (KC + 1))

            def round_(r, sel, u, v):
                if sel:
                    pe.wait_ge(sel_in, 16).then_inc(sel_in, -16)
                if v:
                    pe.wait_ge(xv_in, 16).then_inc(xv_in, -16)
                    pe.wait_ge(acc_free, 1).then_inc(acc_free, -1)
                    for c in range(2):
                        nc.tensor.matmul(acc[c][:], alpha_ident[:], x1_v[:, c * 512:(c + 1) * 512],
                                         start=True, stop=False, skip_group_check=True)

                def group(g, par):
                    def add_rows(j0, j1):
                        for j in range(j0, j1):
                            slot = j % RING
                            pe.wait_ge(diag_ready, 1).then_inc(diag_ready, -1)
                            pe.wait_ge(v_landed[slot], (((r - 2) * HEADS + g) * (TOPK // RING) + j // RING + 1) * 16)
                            nc.tensor.matmul(acc[0][:], diag[:, j % DIAGS, :], v_ring[:, slot, 0:512],
                                             start=False, stop=False, skip_group_check=True)\
                                .then_inc(diag_free, 1)
                            nc.tensor.matmul(acc[1][:], diag[:, j % DIAGS, :], v_ring[:, slot, 512:1024],
                                             start=False, stop=False, skip_group_check=True)\
                                .then_inc(v_free, 1)

                    if v:
                        add_rows(0, 4)
                    if sel:
                        for c in range(KC):
                            last = nc.tensor.matmul(q_ps[:, 0:DKEY], x1t_sel[:, c, :], wq[:, c, bass.ds(g * DKEY, DKEY)],
                                                    start=(c == 0), stop=(c == KC - 1))
                        last.then_inc(q_done, 1)
                    if v:
                        add_rows(4, 8)
                    if sel:
                        pe.wait_ge(q_copied, 1).then_inc(q_copied, -1)
                        for c in range(2):
                            last = nc.tensor.transpose(qt_ps[:, c * P:(c + 1) * P], q_sb[:, c * P:(c + 1) * P], ident[:])
                        last.then_inc(qt_done, 1)
                    if v:
                        add_rows(8, 12)
                    if sel:
                        pe.wait_ge(qt_copied, 1).then_inc(qt_copied, -1)
                        pe.wait_ge(sc_free, 1).then_inc(sc_free, -1)
                        for c in range(2):
                            last = nc.tensor.matmul(sc_ps[:, c * NKEYS:(c + 1) * NKEYS], qt_sb[:, c, :],
                                                    keys[:, bass.ds(g * 2 * NKEYS + c * NKEYS, NKEYS)], start=True, stop=True)
                        last.then_inc(sc_done, 1)
                    if v:
                        add_rows(12, 16)
                groups(pe, group)
                if v:
                    for c in range(2):
                        last = nc.tensor.matmul(acc[c][:], zero[:], x1_v[:, c * 512:(c + 1) * 512],
                                                start=False, stop=True, skip_group_check=True)
                    last.then_inc(acc_done, 1)
            rounds(pe, round_)

        @block.scalar
        def _(act):
            act.sem_inc(sel_free, 1)
            act.sem_inc(top_free, 1)
            act.wait_ge(consts, 3)

            def round_(r, sel, u, v):
                def group(g, par):
                    def diagonals(j0, j1):
                        for j in range(j0, j1):
                            act.wait_ge(diag_free, 1).then_inc(diag_free, -1)
                            nc.scalar.activation(diag[:, j % DIAGS, :], ident[:], ACT.Copy,
                                                 scale=coef_v[:, par, j:j + 1]).then_inc(diag_ready, 1)
                    if v:
                        act.wait_ge(coef_ready, 1).then_inc(coef_ready, -1)
                        nc.scalar.activation(coef_v[:, par, :], coef_all[:, bass.ds(((r - 2) * HEADS + g) * TOPK, TOPK)], ACT.Copy)
                        act.drain()
                        diagonals(0, 8)
                    if sel:
                        act.wait_ge(q_done, 1).then_inc(q_done, -1)
                        nc.scalar.activation(q_sb[:], q_ps[:, 0:DKEY], ACT.Copy).then_inc(q_copied, 1)
                    if v:
                        diagonals(8, 12)
                    if sel:
                        act.wait_ge(qt_done, 1).then_inc(qt_done, -1)
                        nc.scalar.activation(qt_sb[:].rearrange("p c n -> p (c n)"), qt_ps[:, 0:2 * P], ACT.Copy).then_inc(qt_copied, 1)
                    if v:
                        diagonals(12, 16)
                    if sel:
                        act.wait_ge(top_ready, 1).then_inc(top_ready, -1)
                        nc.scalar.activation(exp_all[:, bass.ds((r * HEADS + g) * TOPK, TOPK)], top[:], ACT.Exp,
                                             bias=neg_max[:, 0:1]).then_inc(top_free, 1)
                    if u:
                        act.wait_ge(dots_ready, 1).then_inc(dots_ready, -1)
                        nc.scalar.activation(gelu[:, par, :], dots[:, par, :], ACT.Gelu).then_inc(gelu_ready, 1)
                groups(act, group)
                if sel:
                    act.sem_inc(sel_free, 1)
                if v:
                    act.wait_ge(var_ready, 1).then_inc(var_ready, -1)
                    nc.scalar.activation(std[:], var[:], ACT.Sqrt).then_inc(std_ready, 1)
            rounds(act, round_)

        @block.vector
        def _(dve):
            vec = nc.vector
            dve.sem_inc(u_free, RING)
            dve.sem_inc(sc_free, 1)
            dve.sem_inc(xu_free, 1)
            dve.sem_inc(xv_free, 1)
            dve.sem_inc(acc_free, 1)
            dve.sem_inc(diag_free, DIAGS - 1)
            dve.sem_inc(y_free, 16)
            vec.memset(zero[:], 0.0).then_inc(zero_ready, 1)
            dve.wait_ge(consts, 3)
            vec.tensor_copy(iota16[:], iota_i[:])
            dve.drain()

            def choose(r, g):
                dve.wait_ge(sc_done, 1).then_inc(sc_done, -1)
                for c in range(2):
                    s = sc_ps[:, c * NKEYS:(c + 1) * NKEYS]
                    vec.max(val[:, c, 0:8], s)
                dve.drain()
                for c in range(2):
                    s = sc_ps[:, c * NKEYS:(c + 1) * NKEYS]
                    vec.max_index(idx[:, c, 0:8], val[:, c, 0:8], s)
                    vec.match_replace(work[:, c, :], val[:, c, 0:8], s, NEG)
                dve.drain().then_inc(sc_free, 1)
                for c in range(2):
                    vec.max(val[:, c, 8:16], work[:, c, :])
                dve.drain()
                for c in range(2):
                    vec.max_index(idx[:, c, 8:16], val[:, c, 8:16], work[:, c, :])
                vec.tensor_tensor(cand[:], val[:, 0, :].unsqueeze(2).broadcast_to([P, TOPK, TOPK]),
                                  val[:, 1, :].unsqueeze(1).broadcast_to([P, TOPK, TOPK]), ALU.add)
                dve.drain()
                vec.tensor_copy(idx_f[:], idx[:])
                dve.wait_ge(top_free, 1).then_inc(top_free, -1)
                flat = cand[:].rearrange("p a b -> p (a b)")
                vec.max(top[:, 0:8], flat)
                dve.drain()
                vec.max_index(pos[:, 0:8], top[:, 0:8], flat)
                vec.match_replace(cand2[:], top[:, 0:8], flat, NEG)
                dve.drain()
                vec.max(top[:, 8:16], cand2[:])
                vec.tensor_scalar(neg_max[:], top[:, 0:1], -1.0, None, ALU.mult)
                dve.drain().then_inc(top_ready, 1)
                vec.max_index(pos[:, 8:16], top[:, 8:16], cand2[:])
                dve.drain()
                vec.tensor_scalar(ab[:, 0, :], pos[:], 4, None, ALU.logical_shift_right)
                vec.tensor_scalar(ab[:, 1, :], pos[:], TOPK - 1, None, ALU.bitwise_and)
                dve.drain()
                vec.tensor_copy(ab_f[:], ab[:])
                dve.drain()
                full = [P, 2, TOPK, TOPK]
                vec.tensor_tensor(onehot[:], ab_f[:].unsqueeze(3).broadcast_to(full),
                                  iota16[:].unsqueeze(1).unsqueeze(1).broadcast_to(full), ALU.is_equal)
                dve.drain()
                vec.tensor_tensor(onehot[:], onehot[:], idx_f[:].unsqueeze(2).broadcast_to(full), ALU.mult)
                dve.drain()
                vec.tensor_reduce(picked[:], onehot[:], AX.X, ALU.add)
                dve.drain()
                vec.scalar_tensor_tensor(out=ids_all[:, bass.ds((r * HEADS + g) * TOPK, TOPK)], in0=picked[:, 0, :],
                                         scalar=float(NKEYS), in1=picked[:, 1, :], op0=ALU.mult, op1=ALU.add)\
                    .then_inc(ids_ready, 1)

            def round_(r, sel, u, v):
                if u:
                    dve.wait_ge(xu_in, 16).then_inc(xu_in, -16)
                if isinstance(r, int) and r == NT:
                    dve.wait_ge(top_free, 1).then_inc(top_free, -1)

                def group(g, par):
                    for j in range(TOPK):
                        slot = j % RING
                        if sel and j == 13:
                            choose(r, g)
                        if u:
                            dve.wait_ge(u_landed[slot], (((r - 1) * HEADS + g) * (TOPK // RING) + j // RING + 1) * 16)
                            vec.tensor_tensor_reduce(u_ring[:, slot, :], u_ring[:, slot, :], x1_u[:], 1.0, 0.0,
                                                     ALU.mult, ALU.add, dots[:, par, j:j + 1]).then_inc(u_free, 1)
                    if u:
                        dve.drain().then_inc(dots_ready, 1)
                        at = bass.ds(((r - 1) * HEADS + g) * TOPK, TOPK)
                        vec.tensor_reduce(rsum[:], exp_all[:, at], AX.X, ALU.add)
                        dve.drain()
                        vec.reciprocal(rsum[:], rsum[:])
                        dve.drain()
                        dve.wait_ge(gelu_ready, 1).then_inc(gelu_ready, -1)
                        vec.scalar_tensor_tensor(out=coef_all[:, at], in0=gelu[:, par, :], scalar=rsum[:, 0:1],
                                                 in1=exp_all[:, at], op0=ALU.mult, op1=ALU.mult).then_inc(coef_ready, 1)
                if sel or u:
                    groups(dve, group)
                if u:
                    dve.sem_inc(xu_free, 1)
                if v:
                    dve.wait_ge(acc_done, 1).then_inc(acc_done, -1)
                    dve.sem_inc(xv_free, 1)
                    for c in range(2):
                        vec.bn_stats(stats[:, c, :], acc[c][:])
                    dve.drain()
                    vec.bn_aggr(mv[:], stats[:].rearrange("p a b -> p (a b)"))
                    dve.drain()
                    vec.tensor_scalar(var[:], mv[:, 1:2], LN_EPS, None, ALU.add).then_inc(var_ready, 1)
                    dve.wait_ge(std_ready, 1).then_inc(std_ready, -1)
                    refine_rsqrt(nc, dve, rstd[:], var[:], std[:], tmp[:])
                    dve.wait_ge(y_free, 16).then_inc(y_free, -16)
                    for c in range(2):
                        vec.tensor_scalar(y[:, c * 512:(c + 1) * 512], acc[c][:], mv[:, 0:1], rstd[:, 0:1],
                                          ALU.subtract, ALU.mult)
                    dve.drain().then_inc(acc_free, 1)
                    dve.wait_ge(ln2_in, 32)
                    vec.tensor_tensor(y[:], y[:], g2[:], ALU.mult)
                    dve.drain()
                    vec.tensor_tensor(y[:], y[:], b2[:], ALU.add)
                    dve.drain().then_inc(y_ready, 1)
            rounds(dve, round_)


_INS = ['x', 'x_t', 'positions', 'w_in', 'w_out', 'lambda_q1', 'lambda_k1', 'lambda_q2', 'lambda_k2', 'subln_g', 'conv_w',
        'conv_b', 'dt_bias', 'a_log', 'd_skip', 'ssd_norm_g', 'ln1_g', 'ln1_b', 'peer_wq', 'peer_keys', 'peer_u', 'peer_v',
        'ln2_g', 'ln2_b']


def build(nc, x, x_t, positions, w_in, w_out, lambda_q1, lambda_k1, lambda_q2, lambda_k2, subln_g, conv_w, conv_b, dt_bias,
          a_log, d_skip, ssd_norm_g, ln1_g, ln1_b, peer_wq, peer_keys, peer_u, peer_v, ln2_g, ln2_b, out):
    x1_dram = nc.dram_tensor("x1_rows", (T, D), F32).ap()
    x1t_dram = nc.dram_tensor("x1_tiles_t", (T, D), F32).ap()
    build_mixer(nc, x, x_t, positions, w_in, w_out, (lambda_q1, lambda_k1, lambda_q2, lambda_k2), subln_g, conv_w, conv_b,
                dt_bias, a_log, d_skip, ssd_norm_g, ln1_g, ln1_b, x1_dram, x1t_dram)
    build_experts(nc, x1_dram, x1t_dram, peer_wq, peer_keys, peer_u, peer_v, ln2_g, ln2_b, out)


def kernel(**inputs):
    import concourse.bacc as _bacc
    from concourse.bass_utils import run_bass_kernel_spmd as _run

    a = {name: np.asarray(v)[0] for name, v in inputs.items()}
    a["x_t"] = a["x"].T
    a["positions"] = a["positions"].reshape(NT, P).T
    a["conv_w"] = a["conv_w"].reshape(CONV, KC, P).transpose(2, 1, 0)
    a["conv_b"] = a["conv_b"].reshape(KC, P).T
    a["peer_keys"] = a["peer_keys"].transpose(3, 0, 1, 2).reshape(P, HEADS * 2 * NKEYS)

    nc = _bacc.Bacc("TRN2", target_bir_lowering=False, num_devices=1)
    arrays, args = {}, []
    for name in _INS:
        arrays[f"in_{name}_dram"] = np.ascontiguousarray(a[name])
        args.append(nc.dram_tensor(f"in_{name}_dram", a[name].shape, mybir.dt.from_np(a[name].dtype), kind="ExternalInput").ap())
    args.append(nc.dram_tensor("out_0_dram", (T, D), F32, kind="ExternalOutput").ap())
    build(nc, *args)
    r = _run(nc, [arrays], core_ids=[0])
    return r.results[0]["out_0_dram"].reshape(1, T, D)
```

```python
import math
from contextlib import ExitStack

import numpy as np

import concourse.bass as bass
from concourse import mybir

F32 = mybir.dt.float32
U32 = mybir.dt.uint32
I32 = mybir.dt.int32
ALU = mybir.AluOpType
ACT = mybir.ActivationFunctionType
AX = mybir.AxisListType

P = 128
ATT = SSD = 512
DA_HEADS = 4
DA_DIM = 64
DA_V = 128
HALF = DA_DIM // 2
SSD_HEADS = 8
SSD_DIM = 64
CONV = 4
LAMBDA_INIT = 0.8 - 0.6 * math.exp(-0.3 * 0)
RMS_EPS = 1e-5
FAR = -1.0e30
INV_FREQ = np.float32(10000.0) ** (-np.arange(0, DA_DIM, 2, dtype=np.float32) / np.float32(DA_DIM))
TURN = 2 * math.pi
TURN_PARTS = (6.28125, 2029 * 2.0 ** -20, TURN - 6.28125 - 2029 * 2.0 ** -20)
PI_BELOW = 3.1415925
ROUND = 1.5 * 2.0 ** 23
D = 1024
T = 1024
NT = T // P
KC = D // P
HEADS = 8
NKEYS = 128
DKEY = 256
TOPK = 16
SLOTS = HEADS * TOPK
RING = 8
DIAGS = 8
LAG = 2
ALPHA = 2.0 ** 0.25
LN_EPS = 1e-5
NEG = -3.0e38



def build_mixer(nc, x, x_t, positions, w_in, w_out, lambdas, subln_g, conv_w, conv_b, dt_bias, a_log,
                d_skip, ssd_norm_g, ln1_g, ln1_b, x1_dram, x1t_dram):
    vec, act_, mm = nc.vector, nc.scalar, nc.tensor
    with ExitStack() as ctx:
        def sb(name, shape, dt=F32, to=None):
            return (to or ctx).enter_context(nc.sbuf_tensor(name, shape, dt))

        def sem(name):
            return ctx.enter_context(nc.semaphore(name))

        bank = [ctx.enter_context(nc.psum_tensor(f"bank{i}", [P, 512], F32)) for i in range(4)]
        wide = [ctx.enter_context(nc.psum_tensor(f"wide{i}", [P, 1024], F32)) for i in range(2)]
        bank += [w[:, i * 512:(i + 1) * 512] for w in wide for i in range(2)]

        ident = sb("ident", [P, P])
        upper = sb("upper", [P, P])
        ones = sb("ones", [P, P])
        mask_sl = sb("mask_sl", [P, 4, P])
        mask_qk = sb("mask_qk", [P, P])
        q_t = sb("q_t", [P, DA_HEADS, T])
        k_t = sb("k_t", [P, DA_HEADS, T])
        val = sb("val1", [P, NT, ATT])
        xt = sb("xt", [P, KC, T])
        w_ring = sb("w_ring", [P, 2, KC, 512])
        half_neg = sb("half_neg", [P, 4])
        lam = sb("lam", [P, 1])
        minus_lam = sb("minus_lam", [P, 1])

        const_ready = sem("const_ready")
        w_out_in = sem("w_out_in")
        z = sb("z", [P, NT, SSD])
        step = sem("pool_step1")

        scan = ExitStack()
        xbc = sb("xbc", [P, KC, CONV - 1 + T], to=scan)
        dt_raw = sb("dt_raw", [P, NT * SSD_HEADS], to=scan)
        w_dt = sb("w_dt", [P, KC, SSD_HEADS], to=scan)
        cw = sb("cw", [P, KC, CONV], to=scan)
        cb = sb("cb", [P, KC], to=scan)
        conv = sb("conv", [P, T], to=scan)
        lam_in = sb("lam_in", [P, 4, DA_DIM], to=scan)
        lam_dot = sb("lam_dot", [P, 2], to=scan)
        lam_exp = sb("lam_exp", [P, 2], to=scan)
        pos_i = sb("pos_i", [P, NT], I32, to=scan)
        pos_f = sb("pos_f", [P, NT], to=scan)
        freq = sb("freq", [P, HALF], to=scan)
        ang = sb("ang", [P, NT, HALF], to=scan)
        turns = sb("turns", [P, 2, NT, HALF], to=scan)
        trig = sb("trig", [P, 2, NT, HALF], to=scan)
        roped = sb("roped", [P, 2, ATT], to=scan)
        prod = sb("prod", [P, 2, ATT // 2], to=scan)

        per_head = [P, NT, SSD_HEADS]
        xs = sb("xs", [P, SSD], to=scan)
        bcs = sb("bcs", [P, 4 * P], to=scan)
        xd = sb("xd", [P, SSD], to=scan)
        xd_end = sb("xd_end", [P, SSD], to=scan)
        decay_in = sb("decay_in", [P, SSD_HEADS, P], to=scan)
        decays = sb("decays", [P, SSD_HEADS, P], to=scan)
        state = sb("state", [P, SSD], to=scan)
        ys = sb("ys", [P, SSD], to=scan)
        sq = sb("sq", [P, SSD], to=scan)
        ss = sb("ss", [P, 2], to=scan)
        rs = sb("rs", [P, 2], to=scan)
        norm_g = sb("norm_g", [P, SSD], to=scan)
        bias_dt = sb("bias_dt", [P, SSD_HEADS], to=scan)
        log_a = sb("log_a", [P, SSD_HEADS], to=scan)
        skip = sb("skip", [P, SSD_HEADS], to=scan)
        e_dt, u_dt, l_dt, dt, a, cs, ecs, dec, etot = (
            sb(n, per_head, to=scan) for n in ("e_dt", "u_dt", "l_dt", "dt", "a", "cs", "ecs", "dec", "etot"))


        chunk_in = [sem(f"chunk_in{i}") for i in range(KC)]
        w_landed = [sem(f"w_landed{i}") for i in range(2)]
        w_free = sem("w_free")
        dt_in = sem("dt_in")
        small_in = sem("small_in")
        act_group = sem("act_group")
        dve_group = sem("dve_group")
        bank_free = [sem(f"bank_free{i}") for i in range(2)]
        dt_done = sem("dt_done")
        xbc_ready = sem("xbc_ready")
        conv_ready = sem("conv_ready")
        conv_free = sem("conv_free")
        turns_ready = sem("turns_ready")
        trig_ready = sem("trig_ready")
        lam_ready = sem("lam_ready")
        lam_exped = sem("lam_exped")
        roped_ready = sem("roped_ready")
        roped_free = sem("roped_free")

        vecs_in = sem("vecs_in")
        prep = sem("prep")
        prep_pe = sem("prep_pe")
        exp_done = sem("exp_done")
        prep_act = sem("prep_act")
        cs_done = sem("cs_done")
        xt_done = sem("xt_done")
        xt_free = sem("xt_free")
        z_ready = sem("z_ready")
        state_for_pe = sem("state_for_pe")
        bc_done = sem("bc_done")
        bc_free = sem("bc_free")
        l_in_ready = sem("l_in_ready")
        l_in_free = sem("l_in_free")
        l_done = sem("l_done")
        l_free = sem("l_free")
        xs_ready = sem("xs_ready")
        bcs_ready = sem("bcs_ready")
        bcs_for_pe = sem("bcs_for_pe")
        decays_ready = sem("decays_ready")
        chunk_free = sem("chunk_free")
        xd_ready = sem("xd_ready")
        mixed_ready = sem("mixed_ready")
        st_done = sem("st_done")
        y_done = sem("y_done")
        y_banks_free = sem("y_banks_free")
        ss_ready = sem("ss_ready")
        rs_ready = sem("rs_ready")
        XT, BC, L, YO, ST, YD = bank[2], bank[3], bank[4], bank[5], bank[6], bank[7]
        flat = "p c h -> p (c h)"

        def by_head(v):
            return v.unsqueeze(2).broadcast_to([P, SSD_HEADS, SSD_DIM])

        def heads(v):
            return v[:].rearrange("p (h d) -> p h d", d=SSD_DIM)

        blocks = [("xbc", 2048), ("xbc", 2560), ("z", 1536), ("v", 1024), ("k", 512), ("q", 0)]
        steps = 4 * NT

        def stage(step, lag):
            c, rest = divmod(step - 2 - lag, 3)
            return c if rest == 0 and 0 <= c < NT else None

        with nc.Block() as block:
            @block.sync
            def _(sp):
                def load(dst, n, c):
                    return sp.dma_start(dst, w_in[c * P:(c + 1) * P, blocks[n][1]:blocks[n][1] + 512])
                for c in range(KC):
                    sp.dma_start(xt[:, c, :], x_t[c * P:(c + 1) * P, :]).then_inc(chunk_in[c], 16)
                    load(w_ring[:, 0, c, :], 0, c).then_inc(chunk_in[c], 16)
                for n in range(1, len(blocks)):
                    if n >= 2:
                        sp.wait_ge(w_free, 1).then_inc(w_free, -1)
                    at = blocks[n][1]
                    sp.dma_start(w_ring[:, n % 2, :, :], w_in[:, at:at + 512].rearrange("(c p) n -> p c n", p=P))\
                        .then_inc(w_landed[n % 2], 16)
                for h in range(2):
                    sp.wait_ge(w_free, 1).then_inc(w_free, -1)
                    sp.dma_start(w_ring[:, h, :, :], w_out[:, h * 512:(h + 1) * 512].rearrange("(c p) n -> p c n", p=P))\
                        .then_inc(w_out_in, 16)

            @block.gpsimd
            def _(pool):
                pool.memset(ident[:], 0.0).then_inc(step, 1)
                pool.memset(upper[:], 1.0).then_inc(step, 1)
                pool.memset(ones[:], 1.0).then_inc(step, 1)
                pool.memset(mask_sl[:], 0.0).then_inc(step, 1)
                pool.memset(mask_qk[:], 0.0).then_inc(step, 1)
                pool.wait_ge(step, 5).then_inc(step, -5)
                pool.affine_select(out=ident[:], in_=ident[:], compare_op=ALU.not_equal, fill=1.0, base=0,
                                   pattern=[[-1, P]], channel_multiplier=1).then_inc(const_ready, 1)
                pool.affine_select(out=upper[:], in_=upper[:], compare_op=ALU.is_ge, fill=0.0, base=0,
                                   pattern=[[1, P]], channel_multiplier=-1).then_inc(const_ready, 1)
                pool.affine_select(out=mask_sl[:], in_=mask_sl[:], compare_op=ALU.is_ge, fill=FAR, base=0,
                                   pattern=[[0, 4], [1, P]], channel_multiplier=-1).then_inc(const_ready, 1)
                pool.affine_select(out=mask_qk[:], in_=mask_qk[:], compare_op=ALU.is_ge, fill=FAR, base=0,
                                   pattern=[[-1, P]], channel_multiplier=1).then_inc(const_ready, 1)
                pool.memset(half_neg[:], -0.5).then_inc(step, 1)
                pool.wait_ge(step, 1).then_inc(step, -1)
                pool.wait_ge(prep, 1).then_inc(prep, -1)
                for c in range(NT):
                    pool.wait_ge(l_in_free, 1).then_inc(l_in_free, -1)
                    pool.tensor_tensor(decay_in[:], a[:, c, :].unsqueeze(2).broadcast_to([P, SSD_HEADS, P]),
                                       upper[:].unsqueeze(1).broadcast_to([P, SSD_HEADS, P]), ALU.mult).then_inc(l_in_ready, 1)
                    if c:
                        pool.wait_ge(ss_ready, 1).then_inc(ss_ready, -1)
                        pool.tensor_tensor(rs[:], ss[:], half_neg[:, 0:2], ALU.pow).then_inc(rs_ready, 1)
                pool.wait_ge(ss_ready, 1).then_inc(ss_ready, -1)
                pool.tensor_tensor(rs[:], ss[:], half_neg[:, 0:2], ALU.pow).then_inc(rs_ready, 1)

            @block.tensor
            def _(pe):
                pe.wait_ge(const_ready, 4)

                def channels(c, i):
                    return xbc[:, i, CONV - 1 + c * P:CONV - 1 + (c + 1) * P]

                def turn(n):
                    pe.wait_ge(roped_ready, 1).then_inc(roped_ready, -1)
                    pe.wait_ge(xt_free, 1).then_inc(xt_free, -1)
                    for h in range(DA_HEADS):
                        last = mm.transpose(XT[:, h * P:(h + 1) * P], roped[:, n % 2, h * P:(h + 1) * P], ident[:])
                    last.then_inc(xt_done, 1)

                def decay_half(i):
                    pe.wait_ge(l_free, 1).then_inc(l_free, -1)
                    mm.matmul(L[:], ones[:], decay_in[:, 4 * i:4 * i + 4, :].rearrange("p h l -> p (h l)"), start=True, stop=False)
                    mm.matmul(L[:], ident[:], mask_sl[:].rearrange("p h l -> p (h l)"), start=False, stop=True).then_inc(l_done, 1)

                def scan_stages(s):
                    if (c := stage(s, 3)) is not None:
                        pe.wait_ge(mixed_ready, 1).then_inc(mixed_ready, -1)
                        for h in range(SSD_HEADS):
                            last = mm.matmul(YD[:, h * SSD_DIM:(h + 1) * SSD_DIM], decays[:, h, :], xd[:, h * SSD_DIM:(h + 1) * SSD_DIM],
                                             start=True, stop=True)
                        last.then_inc(y_done, 1)
                    if (c := stage(s, 0)) is not None:
                        pe.wait_ge(xt_free, 1).then_inc(xt_free, -1)
                        for i in range(4):
                            last = mm.transpose(XT[:, i * P:(i + 1) * P], channels(c, i), ident[:])
                        last.then_inc(xt_done, 1)
                        pe.wait_ge(bc_free, 1).then_inc(bc_free, -1)
                        for g in range(2):
                            mm.transpose(BC[:, g * P:(g + 1) * P], channels(c, 4 + g), ident[:])
                        for g in range(2):
                            last = mm.matmul(BC[:, (2 + g) * P:(3 + g) * P], channels(c, 4 + g), channels(c, 6 + g), start=True, stop=True)
                        last.then_inc(bc_done, 1)
                        pe.wait_ge(l_in_ready, 1).then_inc(l_in_ready, -1)
                        decay_half(0)
                    if (c := stage(s, 1)) is not None:
                        decay_half(1)
                        pe.wait_ge(y_banks_free, 1).then_inc(y_banks_free, -1)
                        pe.wait_ge(state_for_pe, 1).then_inc(state_for_pe, -1)
                        for g in range(2):
                            mm.matmul(YO[:, g * 256:(g + 1) * 256], channels(c, 6 + g), state[:, g * 256:(g + 1) * 256], start=True, stop=True)
                    if (c := stage(s, 2)) is not None:
                        pe.wait_ge(xd_ready, 1).then_inc(xd_ready, -1)
                        pe.wait_ge(bcs_for_pe, 1).then_inc(bcs_for_pe, -1)
                        for g in range(2):
                            last = mm.matmul(ST[:, g * 256:(g + 1) * 256], bcs[:, g * P:(g + 1) * P], xd_end[:, g * 256:(g + 1) * 256],
                                             start=True, stop=True)
                        last.then_inc(st_done, 1)

                group = 0
                for n, (kind, _) in enumerate(blocks):
                    slot = n % 2
                    if n:
                        pe.wait_ge(w_landed[slot], 16).then_inc(w_landed[slot], -16)
                    for i in range(8):
                        s = group - 2 * NT
                        if s == 1:
                            pe.wait_ge(prep_pe, 1).then_inc(prep_pe, -1)
                            mm.matmul(YD[:, 0:64], upper[:], a[:].rearrange(flat), start=True, stop=True)
                            mm.matmul(YD[:, 64:128], ones[:], a[:].rearrange(flat), start=True, stop=True).then_inc(cs_done, 1)
                        scan_stages(s)
                        b = group % 2
                        pe.wait_ge(bank_free[b], 1).then_inc(bank_free[b], -1)
                        for c in range(KC):
                            if n == 0 and i == 0:
                                pe.wait_ge(chunk_in[c], 32)
                            if kind == "xbc":
                                lhs = w_ring[:, slot, c, (i // 2) * P:(i // 2 + 1) * P]
                                rhs = xt[:, c, (i % 2) * 512:(i % 2 + 1) * 512]
                            else:
                                lhs, rhs = xt[:, c, i * P:(i + 1) * P], w_ring[:, slot, c, :]
                            last = mm.matmul(bank[b][:], lhs, rhs, start=(c == 0), stop=(c == KC - 1))
                            if n and i == 0 and c == 0:
                                last.then_inc(w_free, 1)
                        last.then_inc(dve_group if kind in "kq" else act_group, 1)
                        group += 1
                        if kind in "kq" and (kind == "q" or i):
                            turn((kind == "q") * 8 + i - 1)
                    if n == 1:
                        pe.wait_ge(dt_in, 16).then_inc(dt_in, -16)
                        for t in range(NT):
                            for c in range(KC):
                                last = mm.matmul(BC[:, t * SSD_HEADS:(t + 1) * SSD_HEADS], xt[:, c, t * P:(t + 1) * P],
                                                 w_dt[:, c, :], start=(c == 0), stop=(c == KC - 1))
                        last.then_inc(dt_done, 1)
                turn(15)
                pe.drain().then_inc(w_free, 1)

            @block.scalar
            def _(act):
                act.dma_start(pos_i[:], positions).then_inc(small_in, 16)
                for i in range(4):
                    act.dma_start(lam_in[:, i, :], lambdas[i].partition_broadcast(P)).then_inc(small_in, 16)
                act.dma_start(cw[:], conv_w).then_inc(small_in, 16)
                act.dma_start(cb[:], conv_b).then_inc(small_in, 16)
                act.dma_start(w_dt[:], w_in[:, 3072:3072 + SSD_HEADS].rearrange("(c p) n -> p c n", p=P)).then_inc(dt_in, 16)
                for dst, src in ((bias_dt, dt_bias), (log_a, a_log), (skip, d_skip), (norm_g, ssd_norm_g)):
                    act.dma_start(dst[:], src.partition_broadcast(P)).then_inc(vecs_in, 16)
                for free in (*bank_free, xt_free, l_free):
                    act.sem_inc(free, 1)
                act.wait_ge(small_in, 16 * 7)
                act.wait_ge(vecs_in, 64)
                act.wait_ge(turns_ready, 1).then_inc(turns_ready, -1)
                act_.activation(trig[:], turns[:], ACT.Sin).then_inc(trig_ready, 1)
                act.wait_ge(lam_ready, 1).then_inc(lam_ready, -1)
                act_.activation(lam_exp[:], lam_dot[:], ACT.Exp).then_inc(lam_exped, 1)

                def smooth(ch):
                    act.wait_ge(conv_ready, 1).then_inc(conv_ready, -1)
                    act_.activation(xbc[:, ch, CONV - 1:], conv[:], ACT.Silu, bias=cb[:, ch:ch + 1])
                    act.drain().then_inc(conv_free, 1)

                def evacuate(dst, func, group):
                    act.wait_ge(act_group, 1).then_inc(act_group, -1)
                    act_.activation(dst, bank[group % 2][:], func).then_inc(bank_free[group % 2], 1)

                for ch in range(KC):
                    for half in range(2):
                        at = CONV - 1 + half * 512
                        evacuate(xbc[:, ch, at:at + 512], ACT.Copy, 2 * ch + half)
                    act.drain().then_inc(xbc_ready, 1)
                    if ch:
                        smooth(ch - 1)
                smooth(KC - 1)

                def keep_turned(n):
                    act.wait_ge(xt_done, 1).then_inc(xt_done, -1)
                    act.sem_inc(roped_free, 1)
                    dst = (k_t if n < NT else q_t)[:, :, (n % NT) * P:(n % NT + 1) * P]
                    act_.activation(dst, XT[:].rearrange("p (h n) -> p h n", h=DA_HEADS), ACT.Copy).then_inc(xt_free, 1)

                def dt_exponentials():
                    act.wait_ge(prep_act, 1).then_inc(prep_act, -1)
                    act_.activation(e_dt[:], e_dt[:], ACT.Exp)
                    act_.activation(log_a[:], log_a[:], ACT.Exp)
                    act.drain().then_inc(exp_done, 1)
                    act.wait_ge(prep_act, 1).then_inc(prep_act, -1)
                    act_.activation(l_dt[:], u_dt[:], ACT.Ln).then_inc(exp_done, 1)

                def decay_exponentials(c, i):
                    act.wait_ge(l_done, 1).then_inc(l_done, -1)
                    for h in range(4 * i, 4 * i + 4):
                        act_.activation(decays[:, h, :], L[:, (h % 4) * P:(h % 4 + 1) * P], ACT.Exp, bias=cs[:, c, h:h + 1])
                    act.drain().then_inc(l_free, 1)
                    act.sem_inc(decays_ready, 1)

                for s in range(steps):
                    if s == 0:
                        dt_exponentials()
                    if s == 1:
                        act.wait_ge(prep_act, 1).then_inc(prep_act, -1)
                        act_.activation(ecs[:], cs[:], ACT.Exp)
                        act_.activation(dec[:], dec[:], ACT.Exp)
                        act_.activation(etot[:], etot[:], ACT.Exp)
                        act.drain().then_inc(exp_done, 1)
                        act.wait_ge(prep_act, 1).then_inc(prep_act, -1)
                    if (c := stage(s, 0)) is not None:
                        act.wait_ge(xt_done, 1).then_inc(xt_done, -1)
                        act.wait_ge(chunk_free, 1).then_inc(chunk_free, -1)
                        act_.activation(xs[:], XT[:], ACT.Copy)
                        act.drain().then_inc(xt_free, 1)
                        act.sem_inc(xs_ready, 1)
                        act.wait_ge(bc_done, 1).then_inc(bc_done, -1)
                        act_.activation(bcs[:], BC[:], ACT.Copy)
                        act.drain().then_inc(bc_free, 1)
                        act.sem_inc(bcs_for_pe, 1)
                        decay_exponentials(c, 0)
                    if (c := stage(s, 1)) is not None:
                        decay_exponentials(c, 1)
                        act.sem_inc(l_in_free, 1)
                    if s < NT:
                        evacuate(z[:, s, :], ACT.Silu, s)
                        act.drain().then_inc(z_ready, 1)
                    elif s < 2 * NT:
                        evacuate(val[:, s - NT, :], ACT.Copy, s)
                    n = s - 2 * NT - 1
                    if n >= 0:
                        keep_turned(n)
                keep_turned(2 * NT - 1)

            @block.vector
            def _(dve):
                dve.sem_inc(conv_free, 1)
                for i in range(HALF):
                    vec.memset(freq[:, i:i + 1], float(INV_FREQ[i]))
                vec.memset(xbc[:, :, 0:CONV - 1], 0.0)
                dve.wait_ge(small_in, 16 * 7)
                vec.tensor_copy(pos_f[:], pos_i[:])
                for i in range(2):
                    vec.tensor_tensor_reduce(lam_in[:, 2 * i, :], lam_in[:, 2 * i, :], lam_in[:, 2 * i + 1, :], 1.0, 0.0,
                                             ALU.mult, ALU.add, lam_dot[:, i:i + 1])
                dve.drain().then_inc(lam_ready, 1)
                full = [P, NT, HALF]
                vec.tensor_tensor(ang[:], pos_f[:].unsqueeze(2).broadcast_to(full), freq[:].unsqueeze(1).broadcast_to(full), ALU.mult)
                dve.drain()
                for i, quarter in enumerate((0.25, 0.0)):
                    t, n = turns[:, i], trig[:, i]
                    vec.tensor_scalar(n, ang[:], 1 / TURN, quarter, ALU.mult, ALU.add)
                    dve.drain()
                    vec.tensor_scalar(n, n, ROUND, None, ALU.add)
                    dve.drain()
                    vec.tensor_scalar(n, n, ROUND, None, ALU.subtract)
                    dve.drain()
                    vec.tensor_copy(t, ang[:])
                    for part in TURN_PARTS:
                        dve.drain()
                        vec.scalar_tensor_tensor(out=t, in0=n, scalar=-part, in1=t, op0=ALU.mult, op1=ALU.add)
                    dve.drain()
                    vec.tensor_scalar(t, t, quarter * TURN, PI_BELOW, ALU.add, ALU.min)
                    dve.drain()
                    vec.tensor_scalar(t, t, -PI_BELOW, None, ALU.max)
                dve.drain().then_inc(turns_ready, 1)
                dve.wait_ge(lam_exped, 1).then_inc(lam_exped, -1)
                vec.tensor_tensor(lam[:], lam_exp[:, 0:1], lam_exp[:, 1:2], ALU.subtract)
                dve.drain()
                vec.tensor_scalar(minus_lam[:], lam[:], LAMBDA_INIT, -1.0, ALU.add, ALU.mult)

                for ch in range(KC):
                    dve.wait_ge(xbc_ready, 1).then_inc(xbc_ready, -1)
                    dve.wait_ge(conv_free, 1).then_inc(conv_free, -1)
                    vec.tensor_scalar(conv[:], xbc[:, ch, 0:T], cw[:, ch, 0:1], None, ALU.mult)
                    for i in range(1, CONV):
                        dve.drain()
                        vec.scalar_tensor_tensor(out=conv[:], in0=xbc[:, ch, i:i + T], scalar=cw[:, ch, i:i + 1],
                                                 in1=conv[:], op0=ALU.mult, op1=ALU.add)
                    dve.drain().then_inc(conv_ready, 1)
                dve.wait_ge(dt_done, 1).then_inc(dt_done, -1)
                vec.tensor_copy(dt_raw[:], BC[:, 0:NT * SSD_HEADS])
                dve.drain().then_inc(bc_free, 1)
                dve.wait_ge(trig_ready, 1).then_inc(trig_ready, -1)
                dve.sem_inc(roped_free, 2)
                vec.memset(state[:], 0.0).then_inc(state_for_pe, 1)
                dve.sem_inc(l_in_free, 1)
                dve.sem_inc(chunk_free, 1)
                dve.sem_inc(y_banks_free, 1)
                dve.wait_ge(vecs_in, 64)
                raw = dt_raw[:].rearrange("p (c h) -> p c h", h=SSD_HEADS)
                vec.tensor_tensor(raw, raw, bias_dt[:].unsqueeze(1).broadcast_to(per_head), ALU.add)
                dve.drain()
                vec.tensor_scalar(u_dt[:], raw, -1.0, None, ALU.mult)
                dve.drain()
                vec.tensor_tensor(e_dt[:], raw, u_dt[:], ALU.min)
                dve.drain().then_inc(prep_act, 1)
                dve.wait_ge(exp_done, 1).then_inc(exp_done, -1)
                vec.tensor_scalar(u_dt[:], e_dt[:], 1.0, None, ALU.add)
                dve.drain().then_inc(prep_act, 1)
                vec.tensor_scalar(dt[:], u_dt[:], -1.0, None, ALU.add)
                dve.drain()
                vec.tensor_tensor(e_dt[:], e_dt[:], dt[:], ALU.subtract)
                dve.wait_ge(exp_done, 1).then_inc(exp_done, -1)
                vec.reciprocal(u_dt[:], u_dt[:])
                dve.drain()
                vec.tensor_tensor(e_dt[:], e_dt[:], u_dt[:], ALU.mult)
                vec.tensor_scalar(dt[:], raw, 0.0, None, ALU.max)
                dve.drain()
                vec.tensor_tensor(dt[:], dt[:], e_dt[:], ALU.add)
                dve.drain()
                vec.tensor_tensor(dt[:], dt[:], l_dt[:], ALU.add)
                vec.tensor_scalar(log_a[:], log_a[:], -1.0, None, ALU.mult)
                dve.drain()
                vec.tensor_tensor(a[:], dt[:], log_a[:].unsqueeze(1).broadcast_to(per_head), ALU.mult)
                dve.drain().then_inc(prep, 1)
                dve.sem_inc(prep_pe, 1)
                dve.wait_ge(cs_done, 1).then_inc(cs_done, -1)
                both = YD[:, 0:128].rearrange("p (k c h) -> p k c h", k=2, h=SSD_HEADS)
                vec.tensor_copy(cs[:], both[:, 0])
                vec.tensor_copy(etot[:], both[:, 1])
                dve.drain()
                vec.tensor_tensor(dec[:], etot[:], cs[:], ALU.subtract)
                dve.drain().then_inc(prep_act, 1)
                dve.wait_ge(exp_done, 1).then_inc(exp_done, -1)
                vec.tensor_scalar(cs[:], cs[:], -1.0, None, ALU.mult)
                dve.drain().then_inc(prep_act, 1)

                def rope(n):
                    t, b = n % NT, n % 2
                    dve.wait_ge(dve_group, 1).then_inc(dve_group, -1)
                    src = bank[b][:].rearrange("p (g two n) -> p g two n", two=2, n=HALF)
                    dst = roped[:, n % 2, :].rearrange("p (g two n) -> p g two n", two=2, n=HALF)
                    part = [P, 2 * DA_HEADS, HALF]
                    cos = trig[:, 0, t, :].unsqueeze(1).broadcast_to(part)
                    sin = trig[:, 1, t, :].unsqueeze(1).broadcast_to(part)
                    p0, p1 = (prod[:, i, :].rearrange("p (g n) -> p g n", n=HALF) for i in range(2))
                    dve.wait_ge(roped_free, 1).then_inc(roped_free, -1)
                    vec.tensor_tensor(p0, src[:, :, 1, :], sin, ALU.mult)
                    vec.tensor_tensor(p1, src[:, :, 0, :], sin, ALU.mult)
                    vec.tensor_tensor(dst[:, :, 0, :], src[:, :, 0, :], cos, ALU.mult)
                    vec.tensor_tensor(dst[:, :, 1, :], src[:, :, 1, :], cos, ALU.mult)
                    dve.drain().then_inc(bank_free[b], 1)
                    vec.tensor_tensor(dst[:, :, 0, :], dst[:, :, 0, :], p0, ALU.subtract)
                    vec.tensor_tensor(dst[:, :, 1, :], dst[:, :, 1, :], p1, ALU.add)
                    dve.drain().then_inc(roped_ready, 1)

                for s in range(steps):
                    if (c := stage(s, 3)) is not None:
                        dve.wait_ge(y_done, 1).then_inc(y_done, -1)
                        vec.tensor_tensor(heads(ys), YO[:].rearrange("p (h d) -> p h d", d=SSD_DIM), by_head(ecs[:, c, :]), ALU.mult)
                        vec.tensor_tensor(heads(sq), heads(xs), by_head(skip[:]), ALU.mult)
                        dve.drain()
                        vec.tensor_tensor(ys[:], ys[:], YD[:], ALU.add)
                        dve.drain().then_inc(y_banks_free, 1)
                        dve.sem_inc(chunk_free, 1)
                        vec.tensor_tensor(ys[:], ys[:], sq[:], ALU.add)
                        dve.drain()
                        dve.wait_ge(z_ready, 1).then_inc(z_ready, -1)
                        vec.tensor_tensor(ys[:], ys[:], z[:, c, :], ALU.mult)
                        dve.drain()
                        for g in range(2):
                            part = slice(g * 256, (g + 1) * 256)
                            vec.tensor_tensor_reduce(sq[:, part], ys[:, part], ys[:, part], 1.0, 0.0, ALU.mult, ALU.add, ss[:, g:g + 1])
                        dve.drain()
                        vec.tensor_scalar(ss[:], ss[:], 1.0 / 256, RMS_EPS, ALU.mult, ALU.add)
                        dve.drain().then_inc(ss_ready, 1)
                    if (c := stage(s, 0)) is not None:
                        dve.wait_ge(xs_ready, 1).then_inc(xs_ready, -1)
                        vec.tensor_tensor(heads(xd), heads(xs), by_head(dt[:, c, :]), ALU.mult)
                        dve.drain()
                        vec.tensor_tensor(heads(xd_end), heads(xd), by_head(dec[:, c, :]), ALU.mult)
                        dve.drain().then_inc(xd_ready, 1)
                    for g in range(2):
                        if (c := stage(s, 1 + g)) is not None:
                            dve.wait_ge(decays_ready, 1).then_inc(decays_ready, -1)
                            vec.tensor_tensor(decays[:, 4 * g:4 * g + 4, :], decays[:, 4 * g:4 * g + 4, :],
                                              bcs[:, (2 + g) * P:(3 + g) * P].unsqueeze(1).broadcast_to([P, 4, P]), ALU.mult)
                            if g:
                                dve.drain().then_inc(mixed_ready, 1)
                    if (c := stage(s, 2)) is not None:
                        dve.wait_ge(st_done, 1).then_inc(st_done, -1)
                        vec.tensor_tensor(heads(state), heads(state), by_head(etot[:, c, :]), ALU.mult)
                        dve.drain()
                        vec.tensor_tensor(state[:], state[:], ST[:], ALU.add)
                        dve.drain().then_inc(state_for_pe, 1)
                    if (c := stage(s, 4)) is not None:
                        dve.wait_ge(rs_ready, 1).then_inc(rs_ready, -1)
                        for g in range(2):
                            part = slice(g * 256, (g + 1) * 256)
                            vec.scalar_tensor_tensor(out=z[:, c, part], in0=ys[:, part], scalar=rs[:, g:g + 1], in1=norm_g[:, part],
                                                     op0=ALU.mult, op1=ALU.mult)
                        dve.drain()
                    if s >= 2 * NT:
                        rope(s - 2 * NT)
        scan.close()

        probs = sb("probs", [P, 3, 2, T])
        wt = sb("wt", [P, 2, NT, P])
        xtile = sb("xtile", [P, D])
        res = sb("res", [P, D])
        x1 = sb("x1", [P, D])
        x1t = sb("x1t_out", [P, KC, P])
        g1 = sb("g1", [P, D])
        b1 = sb("b1", [P, D])
        att = sb("att", [P, ATT])
        att_sq = sb("att_sq", [P, ATT])
        sub_g = sb("sub_g", [P, DA_V])
        mx = sb("mx", [P, 2, 2])
        rsum = sb("rsum1", [P, 3, 2])
        rinv = sb("rinv", [P, 2])
        av = sb("av", [P, DA_HEADS])
        ar = sb("ar", [P, DA_HEADS])
        stats = sb("stats1", [P, 2, 6])
        mv = sb("mv1", [P, 2])
        var = sb("var1", [P, 1])
        rstd = sb("rstd1", [P, 1])

        norm_in = sem("norm_in")
        sc_done = [sem(f"sc_done{i}") for i in range(2)]
        sc_free = [sem(f"sc_free{i}1") for i in range(2)]
        mx_ready = [sem(f"mx_ready{i}") for i in range(2)]
        probs_ready = sem("probs_ready")
        w_ready = sem("w_ready")
        t_done = [sem(f"t_done{i}") for i in range(2)]
        t_free = [sem(f"t_free{i}") for i in range(2)]
        wt_ready = sem("wt_ready")
        pv_done = sem("pv_done")
        pv_free = sem("pv_free")
        att_copied = sem("att_copied")
        av_ready = sem("av_ready")
        ar_ready = sem("ar_ready")
        att_ready = sem("att_ready")
        mix_ready = sem("mix_ready")
        op_done = sem("op_done")
        op_free = sem("op_free")
        xtile_in = sem("xtile_in")
        xtile_free = sem("xtile_free")
        var_ready = sem("var_ready1")
        rstd_ready = sem("rstd_ready1")
        x1_ready = sem("x1_ready")
        x1_turn = sem("x1_turn")
        x1_free = sem("x1_free")
        x1_landed = sem("x1_landed")
        x1t_ready = sem("x1t_ready")
        x1t_landed = sem("x1t_landed")
        SC, TP, PV, OP = wide, bank[0:2], bank[2], bank[3]
        items = NT * DA_HEADS
        last_step = items - 1 + 12

        def tail(n, lag):
            t, rest = divmod(n - lag, DA_HEADS)
            return t if rest == 0 and 0 <= t < NT else None

        with nc.Block() as block:
            @block.sync
            def _(sp):
                for dst, src in ((g1, ln1_g), (b1, ln1_b), (sub_g, subln_g)):
                    sp.dma_start(dst[:], src.partition_broadcast(P)).then_inc(norm_in, 16)
                for t in range(NT):
                    sp.wait_ge(xtile_free, 1).then_inc(xtile_free, -1)
                    sp.dma_start(xtile[:], x[t * P:(t + 1) * P, :]).then_inc(xtile_in, 16)
                    sp.wait_ge(x1_ready, 1).then_inc(x1_ready, -1)
                    sp.dma_start(x1_dram[t * P:(t + 1) * P, :], x1[:]).then_inc(x1_landed, 16)
                    sp.wait_ge(x1t_ready, 1).then_inc(x1t_ready, -1)
                    sp.dma_start(x1t_dram[t * P:(t + 1) * P, :], x1t[:].rearrange("p c n -> p (c n)")).then_inc(x1t_landed, 16)
                sp.wait_ge(x1_landed, 16).then_inc(x1_landed, -16)
                sp.wait_ge(x1t_landed, 16).then_inc(x1t_landed, -16)

            @block.gpsimd
            def _(pool):
                for n in range(last_step + 1):
                    if tail(n, 7) is not None:
                        pool.wait_ge(av_ready, 1).then_inc(av_ready, -1)
                        pool.tensor_tensor(ar[:], av[:], half_neg[:], ALU.pow).then_inc(ar_ready, 1)
                    if tail(n, 10) is not None:
                        pool.wait_ge(var_ready, 1).then_inc(var_ready, -1)
                        pool.tensor_tensor(rstd[:], var[:], half_neg[:, 0:1], ALU.pow).then_inc(rstd_ready, 1)

            @block.tensor
            def _(pe):
                pe.wait_ge(w_out_in, 32)

                def scores(n):
                    t, h = divmod(n, DA_HEADS)
                    keys = (t + 1) * P
                    for c in range(2):
                        rows = slice(c * DA_DIM, (c + 1) * DA_DIM)
                        pe.wait_ge(sc_free[c], 1).then_inc(sc_free[c], -1)
                        for k0 in range(0, keys, 512):
                            k1 = min(keys, k0 + 512)
                            diagonal = k1 == keys
                            last = mm.matmul(SC[c][:, k0:k1], q_t[rows, h, t * P:(t + 1) * P], k_t[rows, h, k0:k1],
                                             start=True, stop=not diagonal)
                            if diagonal:
                                last = mm.matmul(SC[c][:, k1 - P:k1], ident[:], mask_qk[:], start=False, stop=True)
                        last.then_inc(sc_done[c], 1)

                def turn(n):
                    t = n // DA_HEADS
                    pe.wait_ge(w_ready, 1).then_inc(w_ready, -1)
                    for b in range(t // 4 + 1):
                        pe.wait_ge(t_free[b], 1).then_inc(t_free[b], -1)
                        for k in range(4 * b, min(4 * b + 4, t + 1)):
                            last = mm.transpose(TP[b][:, (k % 4) * P:(k % 4 + 1) * P], probs[:, n % 3, 0, k * P:(k + 1) * P], ident[:])
                        last.then_inc(t_done[b], 1)

                def weigh(n):
                    t, h = divmod(n, DA_HEADS)
                    if h == 0:
                        pe.wait_ge(pv_free, 1).then_inc(pv_free, -1)
                    pe.wait_ge(wt_ready, 1).then_inc(wt_ready, -1)
                    for k in range(t + 1):
                        last = mm.matmul(PV[:, h * P:(h + 1) * P], wt[:, n % 2, k, :], val[:, k, h * P:(h + 1) * P],
                                         start=(k == 0), stop=(k == t))
                    if h == DA_HEADS - 1:
                        last.then_inc(pv_done, 1)

                for n in range(last_step + 1):
                    if n < items:
                        scores(n)
                    if 2 <= n < items + 2:
                        turn(n - 2)
                    if 3 <= n < items + 3:
                        weigh(n - 3)
                    if tail(n, 9) is not None:
                        pe.wait_ge(att_ready, 1).then_inc(att_ready, -1)
                        for b, src in ((0, att[:]), (1, z[:, tail(n, 9), :])):
                            pe.wait_ge(t_free[b], 1).then_inc(t_free[b], -1)
                            for i in range(4):
                                last = mm.transpose(TP[b][:, i * P:(i + 1) * P], src[:, i * P:(i + 1) * P], ident[:])
                            last.then_inc(t_done[b], 1)
                    if (t := tail(n, 10)) is not None:
                        pe.wait_ge(mix_ready, 1).then_inc(mix_ready, -1)
                        for half in range(2):
                            pe.wait_ge(op_free, 1).then_inc(op_free, -1)
                            for c in range(KC):
                                last = mm.matmul(OP[:], xt[:, c, t * P:(t + 1) * P], w_ring[:, half, c, :],
                                                 start=(c == 0), stop=(c == KC - 1))
                            last.then_inc(op_done, 1)
                    if tail(n, 12) is not None:
                        pe.wait_ge(x1_turn, 1).then_inc(x1_turn, -1)
                        for b in range(2):
                            pe.wait_ge(t_free[b], 1).then_inc(t_free[b], -1)
                            for i in range(4):
                                at = (4 * b + i) * P
                                last = mm.transpose(TP[b][:, i * P:(i + 1) * P], x1[:, at:at + P], ident[:])
                            last.then_inc(t_done[b], 1)

            @block.scalar
            def _(act):
                for s in (*t_free, *sc_free, pv_free):
                    act.sem_inc(s, 1)
                act.sem_inc(x1t_landed, 16)
                for n in range(last_step + 1):
                    if n < items:
                        keys = (n // DA_HEADS + 1) * P
                        for c in range(2):
                            act.wait_ge(mx_ready[c], 1).then_inc(mx_ready[c], -1)
                            act_.activation(probs[:, n % 3, c, 0:keys], SC[c][:, 0:keys], ACT.Exp, bias=mx[:, n % 2, c:c + 1],
                                            scale=DA_DIM ** -0.5, accum_out=rsum[:, n % 3, c:c + 1])
                            act.drain().then_inc(sc_free[c], 1)
                        act.sem_inc(probs_ready, 1)
                    if 2 <= n < items + 2:
                        m = n - 2
                        t = m // DA_HEADS
                        for b in range(t // 4 + 1):
                            k0, k1 = 4 * b, min(4 * b + 4, t + 1)
                            act.wait_ge(t_done[b], 1).then_inc(t_done[b], -1)
                            act_.activation(wt[:, m % 2, k0:k1, :].rearrange("p k n -> p (k n)"), TP[b][:, 0:(k1 - k0) * P], ACT.Copy)
                            act.drain().then_inc(t_free[b], 1)
                        act.sem_inc(wt_ready, 1)
                    if tail(n, 6) is not None:
                        act.wait_ge(pv_done, 1).then_inc(pv_done, -1)
                        act_.activation(att[:], PV[:], ACT.Copy)
                        act.drain().then_inc(pv_free, 1)
                        act.sem_inc(att_copied, 1)
                    if (t := tail(n, 9)) is not None:
                        for b in range(2):
                            act.wait_ge(t_done[b], 1).then_inc(t_done[b], -1)
                            act_.activation(xt[:, 4 * b:4 * b + 4, t * P:(t + 1) * P], TP[b][:].rearrange("p (i n) -> p i n", i=4),
                                            ACT.Copy)
                            act.drain().then_inc(t_free[b], 1)
                        act.sem_inc(mix_ready, 1)
                    if tail(n, 12) is not None:
                        act.wait_ge(x1t_landed, 16).then_inc(x1t_landed, -16)
                        for b in range(2):
                            act.wait_ge(t_done[b], 1).then_inc(t_done[b], -1)
                            act_.activation(x1t[:, 4 * b:4 * b + 4, :].rearrange("p i n -> p (i n)"), TP[b][:], ACT.Copy)
                            act.drain().then_inc(t_free[b], 1)
                        act.sem_inc(x1t_ready, 1)
                        act.sem_inc(x1_free, 1)

            @block.vector
            def _(dve):
                dve.sem_inc(op_free, 1)
                dve.sem_inc(xtile_free, 1)
                dve.sem_inc(x1_free, 1)
                dve.sem_inc(x1_landed, 16)
                dve.wait_ge(norm_in, 48)
                vec.tensor_scalar(sub_g[:], sub_g[:], 1.0 - LAMBDA_INIT, None, ALU.mult)
                dve.drain()
                for n in range(last_step + 1):
                    if n < items:
                        keys = (n // DA_HEADS + 1) * P
                        for c in range(2):
                            dve.wait_ge(sc_done[c], 1).then_inc(sc_done[c], -1)
                            vec.tensor_reduce(mx[:, n % 2, c:c + 1], SC[c][:, 0:keys], AX.X, ALU.max)
                            dve.drain()
                            vec.tensor_scalar(mx[:, n % 2, c:c + 1], mx[:, n % 2, c:c + 1], -DA_DIM ** -0.5, None, ALU.mult)
                            dve.drain().then_inc(mx_ready[c], 1)
                    if 1 <= n < items + 1:
                        m = n - 1
                        keys = (m // DA_HEADS + 1) * P
                        p0, p1 = (probs[:, m % 3, c, 0:keys] for c in range(2))
                        dve.wait_ge(probs_ready, 1).then_inc(probs_ready, -1)
                        vec.reciprocal(rinv[:], rsum[:, m % 3, :])
                        dve.drain()
                        vec.tensor_tensor(rinv[:, 1:2], rinv[:, 1:2], minus_lam[:], ALU.mult)
                        vec.tensor_scalar(p0, p0, rinv[:, 0:1], None, ALU.mult)
                        dve.drain()
                        vec.scalar_tensor_tensor(out=p0, in0=p1, scalar=rinv[:, 1:2], in1=p0, op0=ALU.mult, op1=ALU.add)
                        dve.drain().then_inc(w_ready, 1)
                    if tail(n, 7) is not None:
                        dve.wait_ge(att_copied, 1).then_inc(att_copied, -1)
                        vec.tensor_tensor(att_sq[:], att[:], att[:], ALU.mult)
                        dve.drain()
                        vec.tensor_reduce(av[:], att_sq[:].rearrange("p (h n) -> p h n", h=DA_HEADS), AX.X, ALU.add)
                        dve.drain()
                        vec.tensor_scalar(av[:], av[:], 1.0 / DA_V, RMS_EPS, ALU.mult, ALU.add)
                        dve.drain().then_inc(av_ready, 1)
                    if tail(n, 8) is not None:
                        full = [P, DA_HEADS, DA_V]
                        by_head_ = att[:].rearrange("p (h n) -> p h n", h=DA_HEADS)
                        dve.wait_ge(ar_ready, 1).then_inc(ar_ready, -1)
                        vec.tensor_tensor(by_head_, by_head_, ar[:].unsqueeze(2).broadcast_to(full), ALU.mult)
                        dve.drain()
                        vec.tensor_tensor(by_head_, by_head_, sub_g[:].unsqueeze(1).broadcast_to(full), ALU.mult)
                        dve.drain().then_inc(att_ready, 1)
                    if tail(n, 10) is not None:
                        dve.wait_ge(xtile_in, 16).then_inc(xtile_in, -16)
                        for half in range(2):
                            part = slice(half * 512, (half + 1) * 512)
                            dve.wait_ge(op_done, 1).then_inc(op_done, -1)
                            vec.scalar_tensor_tensor(out=res[:, part], in0=xtile[:, part], scalar=ALPHA, in1=OP[:],
                                                     op0=ALU.mult, op1=ALU.add)
                            dve.drain().then_inc(op_free, 1)
                            vec.bn_stats(stats[:, half, :], res[:, part])
                        dve.drain().then_inc(xtile_free, 1)
                        vec.bn_aggr(mv[:], stats[:].rearrange("p a b -> p (a b)"))
                        dve.drain()
                        vec.tensor_scalar(var[:], mv[:, 1:2], LN_EPS, None, ALU.add)
                        dve.drain().then_inc(var_ready, 1)
                    if tail(n, 11) is not None:
                        dve.wait_ge(rstd_ready, 1).then_inc(rstd_ready, -1)
                        dve.wait_ge(x1_landed, 16).then_inc(x1_landed, -16)
                        dve.wait_ge(x1_free, 1).then_inc(x1_free, -1)
                        vec.tensor_scalar(x1[:], res[:], mv[:, 0:1], rstd[:, 0:1], ALU.subtract, ALU.mult)
                        dve.drain()
                        vec.tensor_tensor(x1[:], x1[:], g1[:], ALU.mult)
                        dve.drain()
                        vec.tensor_tensor(x1[:], x1[:], b1[:], ALU.add)
                        dve.drain().then_inc(x1_ready, 1)
                        dve.sem_inc(x1_turn, 1)


def refine_rsqrt(nc, dve, out, var, std, tmp):
    vec = nc.vector
    vec.reciprocal(out, std)
    dve.drain()
    vec.tensor_tensor(tmp, out, out, ALU.mult)
    dve.drain()
    vec.tensor_tensor(tmp, tmp, var, ALU.mult)
    dve.drain()
    vec.tensor_scalar(tmp, tmp, -0.5, 1.5, ALU.mult, ALU.add)
    dve.drain()
    vec.tensor_tensor(out, out, tmp, ALU.mult)
    dve.drain()


def build_experts(nc, x1_dram, x1t_dram, peer_wq, keys_t, peer_u, peer_v, ln2_g, ln2_b, out):
    with ExitStack() as ctx:
        def sb(name, shape, dt=F32):
            return ctx.enter_context(nc.sbuf_tensor(name, shape, dt))

        def ps(name, shape):
            return ctx.enter_context(nc.psum_tensor(name, shape, F32))

        def sem(name):
            return ctx.enter_context(nc.semaphore(name))

        wq = sb("wq", [P, KC, HEADS * DKEY])
        keys = sb("keys", [P, HEADS * 2 * NKEYS])
        u_ring = sb("u_ring", [P, RING, D])
        v_ring = sb("v_ring", [P, RING, D])
        x1t_sel = sb("x1t_sel", [P, KC, P])
        x1_u = sb("x1_u", [P, D])
        g2 = sb("g2", [P, D])
        b2 = sb("b2", [P, D])
        y = sb("y", [P, D])
        ids_all = sb("ids_all", [P, NT * SLOTS], U32)
        exp_all = sb("exp_all", [P, NT * SLOTS])
        sum_all = sb("sum_all", [P, NT * HEADS])
        coef_all = sb("coef_all", [P, NT * SLOTS])
        ids_u = sb("ids_u", [P, 2, TOPK], U32)
        ids_v = sb("ids_v", [P, 2, TOPK], U32)
        coef_v = sb("coef_v", [P, 2, TOPK])
        dots = sb("dots", [P, 2, TOPK])
        gelu = sb("gelu", [P, 2, TOPK])
        rsum = sb("rsum", [P, 1])
        zero = sb("zero2", [P, 512])
        diag = sb("diag", [P, DIAGS, P])
        ident = sb("ident2", [P, P])
        alpha_ident = sb("alpha_ident", [P, P])
        q_sb = sb("q_sb", [P, DKEY])
        qt_sb = sb("qt_sb", [P, 2, P])
        val = sb("val", [P, 2, TOPK])
        idx = sb("idx", [P, 2, TOPK], U32)
        idx_f = sb("idx_f", [P, 2, TOPK])
        work = sb("work", [P, 2, NKEYS])
        cand = sb("cand", [P, TOPK, TOPK])
        cand2 = sb("cand2", [P, TOPK * TOPK])
        top = sb("top", [P, TOPK])
        neg_max = sb("neg_max", [P, 1])
        pos = sb("pos", [P, TOPK], U32)
        ab = sb("ab", [P, 2, TOPK], U32)
        ab_f = sb("ab_f", [P, 2, TOPK])
        onehot = sb("onehot", [P, 2, TOPK, TOPK])
        picked = sb("picked", [P, 2, TOPK])
        iota16 = sb("iota16", [P, TOPK])
        iota_i = sb("iota_i", [P, TOPK], I32)
        stats = sb("stats", [P, 2, 6])
        mv = sb("mv", [P, 2])
        rstd = sb("rstd", [P, 1])
        var = sb("var2", [P, 1])
        std = sb("std2", [P, 1])
        tmp = sb("tmp2", [P, 1])

        acc = [ps(f"acc{i}", [P, 512]) for i in range(2)]
        q_ps = ps("q_ps", [P, 512])
        qt_ps = ps("qt_ps", [P, 512])
        sc_ps = ps("sc_ps", [P, 512])

        weights_in = sem("weights_in2")
        ln2_in = sem("ln2_in")
        sel_in = sem("sel_in")
        sel_free = sem("sel_free")
        xu_in = sem("xu_in")
        xu_free = sem("xu_free")
        xu_for_pe = sem("xu_for_pe")
        opened = sem("opened")
        u_landed = [sem(f"u_landed{i}") for i in range(RING)]
        v_landed = [sem(f"v_landed{i}") for i in range(RING)]
        u_free = sem("u_free")
        v_free = sem("v_free")
        ids_ready = sem("ids_ready")
        q_done = sem("q_done")
        q_copied = sem("q_copied")
        qt_done = sem("qt_done")
        qt_copied = sem("qt_copied")
        sc_done = sem("sc_done")
        sc_free = sem("sc_free")
        top_ready = sem("top_ready")
        top_free = sem("top_free")
        dots_ready = sem("dots_ready")
        gelu_ready = sem("gelu_ready")
        coef_ready = sem("coef_ready")
        diag_ready = sem("diag_ready")
        diag_free = sem("diag_free")
        acc_done = sem("acc_done")
        acc_free = sem("acc_free")
        y_ready = sem("y_ready")
        y_free = sem("y_free")
        y_out = sem("y_out")
        var_ready = sem("var_ready2")
        std_ready = sem("std_ready2")
        consts = sem("consts2")
        zero_ready = sem("zero_ready")
        pool_step = sem("pool_step")

        def rounds(eng, body):
            body(0, True, False, False)
            body(1, True, True, False)
            with eng.Fori(2, NT) as r:
                body(r, True, True, True)
            body(NT, False, True, True)
            body(NT + 1, False, False, True)

        def groups(eng, more, ended, sums, group, turn):
            for par in range(2):
                group(par, par, ended)
            turn()
            if more:
                with eng.Fori(1, HEADS // 2) as half:
                    for par in range(2):
                        group(half * 2 + par, par, sums)

        block = ctx.enter_context(nc.Block())

        @block.sync
        def _(sp):
            sp.dma_start(keys[:], keys_t).then_inc(weights_in, 16)
            for c in range(KC):
                sp.dma_start(wq[:, c, :], peer_wq[c * P:(c + 1) * P, :]).then_inc(weights_in, 16)

            def round_(r, sel, u, ended):
                if sel:
                    sp.wait_ge(sel_free, 1).then_inc(sel_free, -1)
                    sp.dma_start(x1t_sel[:].rearrange("p c n -> p (c n)"),
                                 x1t_dram[bass.ds(r * P, P), :]).then_inc(sel_in, 16)
                if u:
                    sp.wait_ge(xu_free, 1).then_inc(xu_free, -1)
                    sp.dma_start(x1_u[:], x1_dram[bass.ds((r - 1) * P, P), :]).then_inc(xu_in, 16)
                if ended:
                    sp.wait_ge(y_ready, 1).then_inc(y_ready, -1)
                    sp.dma_start(out[bass.ds((r - 2) * P, P), :], y[:]).then_inc(y_free, 16)

            round_(0, True, False, False)
            sp.dma_start(g2[:], ln2_g.partition_broadcast(P)).then_inc(ln2_in, 16)
            sp.dma_start(b2[:], ln2_b.partition_broadcast(P)).then_inc(ln2_in, 16)
            round_(1, True, True, False)
            with sp.Fori(2, NT) as r:
                round_(r, True, True, True)
            round_(NT, False, True, True)
            round_(NT + 1, False, False, True)
            sp.wait_ge(y_free, 16)

        @block.gpsimd
        def _(pool):
            pool.iota(iota_i[:], [[1, TOPK]], base=0, channel_multiplier=0).then_inc(consts, 1)
            pool.memset(ident[:], 0.0).then_inc(pool_step, 1)
            pool.memset(alpha_ident[:], 0.0).then_inc(pool_step, 1)
            pool.wait_ge(pool_step, 2).then_inc(pool_step, -2)
            for m, diagonal in ((ident, 1.0), (alpha_ident, ALPHA)):
                pool.affine_select(out=m[:], in_=m[:], compare_op=ALU.not_equal, fill=diagonal, base=0,
                                   pattern=[[-1, P]], channel_multiplier=1).then_inc(consts, 1)

            def gather(ring, slot, table, ids, par, j, landed):
                pool.indirect_dma_start(ring[:, slot, :], None, table,
                                        bass.IndirectOffsetOnAxis(ap=ids[:, par, j:j + 1], axis=0))\
                    .then_inc(landed[slot], 16)

            def round_(r, sel, u, ended):
                def group(g, par, v):
                    if u:
                        pool.wait_ge(ids_ready, 1).then_inc(ids_ready, -1)
                        pool.tensor_copy(ids_u[:, par, :], ids_all[:, bass.ds(((r - 1) * HEADS + g) * TOPK, TOPK)])\
                            .then_inc(pool_step, 1)
                        pool.wait_ge(pool_step, 1).then_inc(pool_step, -1)
                    if v:
                        pool.tensor_copy(ids_v[:, par, :], ids_all[:, bass.ds(((r - 1) * HEADS + g - LAG) * TOPK, TOPK)])\
                            .then_inc(pool_step, 1)
                        pool.wait_ge(pool_step, 1).then_inc(pool_step, -1)
                    for j in range(TOPK):
                        slot = j % RING
                        if u:
                            pool.wait_ge(u_free, 1).then_inc(u_free, -1)
                            gather(u_ring, slot, peer_u, ids_u, par, j, u_landed)
                        if v:
                            pool.wait_ge(v_free, 1).then_inc(v_free, -1)
                            gather(v_ring, slot, peer_v, ids_v, par, j, v_landed)
                if u or ended:
                    groups(pool, u, ended, u, group, lambda: None)
            rounds(pool, round_)

        @block.tensor
        def _(pe):
            pe.sem_inc(v_free, RING)
            pe.wait_ge(consts, 3)
            pe.wait_ge(zero_ready, 1)
            pe.wait_ge(weights_in, 16 * (KC + 1))

            def round_(r, sel, u, ended):
                if sel:
                    pe.wait_ge(sel_in, 16).then_inc(sel_in, -16)

                def turn():
                    if ended:
                        for c in range(2):
                            last = nc.tensor.matmul(acc[c][:], zero[:, 0:P], zero[:], start=False, stop=True, skip_group_check=True)
                        last.then_inc(acc_done, 1)
                    if u:
                        pe.wait_ge(xu_for_pe, 1).then_inc(xu_for_pe, -1)
                        pe.wait_ge(acc_free, 1).then_inc(acc_free, -1)
                        for c in range(2):
                            last = nc.tensor.matmul(acc[c][:], alpha_ident[:], x1_u[:, c * 512:(c + 1) * 512],
                                                    start=True, stop=False, skip_group_check=True)
                        last.then_inc(opened, 1)

                def group(g, par, v):
                    def add_rows(j0, j1):
                        for j in range(j0, j1):
                            slot = j % RING
                            pe.wait_ge(diag_ready, 1).then_inc(diag_ready, -1)
                            pe.wait_ge(v_landed[slot], (((r - 1) * HEADS + g - LAG) * (TOPK // RING) + j // RING + 1) * 16)
                            nc.tensor.matmul(acc[0][:], diag[:, j % DIAGS, :], v_ring[:, slot, 0:512],
                                             start=False, stop=False, skip_group_check=True)\
                                .then_inc(diag_free, 1)
                            nc.tensor.matmul(acc[1][:], diag[:, j % DIAGS, :], v_ring[:, slot, 512:1024],
                                             start=False, stop=False, skip_group_check=True)\
                                .then_inc(v_free, 1)

                    if v:
                        add_rows(0, 4)
                    if sel:
                        for c in range(KC):
                            last = nc.tensor.matmul(q_ps[:, 0:DKEY], x1t_sel[:, c, :], wq[:, c, bass.ds(g * DKEY, DKEY)],
                                                    start=(c == 0), stop=(c == KC - 1))
                        last.then_inc(q_done, 1)
                    if v:
                        add_rows(4, 8)
                    if sel:
                        pe.wait_ge(q_copied, 1).then_inc(q_copied, -1)
                        for c in range(2):
                            last = nc.tensor.transpose(qt_ps[:, c * P:(c + 1) * P], q_sb[:, c * P:(c + 1) * P], ident[:])
                        last.then_inc(qt_done, 1)
                    if v:
                        add_rows(8, 12)
                    if sel:
                        pe.wait_ge(qt_copied, 1).then_inc(qt_copied, -1)
                        pe.wait_ge(sc_free, 1).then_inc(sc_free, -1)
                        for c in range(2):
                            last = nc.tensor.matmul(sc_ps[:, c * NKEYS:(c + 1) * NKEYS], qt_sb[:, c, :],
                                                    keys[:, bass.ds(g * 2 * NKEYS + c * NKEYS, NKEYS)], start=True, stop=True)
                        last.then_inc(sc_done, 1)
                    if v:
                        add_rows(12, 16)
                groups(pe, sel or u, ended, u, group, turn)
            rounds(pe, round_)

        @block.scalar
        def _(act):
            act.sem_inc(sel_free, 1)
            act.sem_inc(top_free, 1)
            act.wait_ge(consts, 3)

            def round_(r, sel, u, ended):
                def turn():
                    if ended:
                        act.wait_ge(var_ready, 1).then_inc(var_ready, -1)
                        nc.scalar.activation(std[:], var[:], ACT.Sqrt).then_inc(std_ready, 1)

                def group(g, par, v):
                    def diagonals(j0, j1):
                        for j in range(j0, j1):
                            act.wait_ge(diag_free, 1).then_inc(diag_free, -1)
                            nc.scalar.activation(diag[:, j % DIAGS, :], ident[:], ACT.Copy,
                                                 scale=coef_v[:, par, j:j + 1]).then_inc(diag_ready, 1)
                    if v:
                        act.wait_ge(coef_ready, 1).then_inc(coef_ready, -1)
                        nc.scalar.activation(coef_v[:, par, :], coef_all[:, bass.ds(((r - 1) * HEADS + g - LAG) * TOPK, TOPK)], ACT.Copy)
                        act.drain()
                        diagonals(0, 8)
                    if sel:
                        act.wait_ge(q_done, 1).then_inc(q_done, -1)
                        nc.scalar.activation(q_sb[:], q_ps[:, 0:DKEY], ACT.Copy).then_inc(q_copied, 1)
                    if v:
                        diagonals(8, 12)
                    if sel:
                        act.wait_ge(qt_done, 1).then_inc(qt_done, -1)
                        nc.scalar.activation(qt_sb[:].rearrange("p c n -> p (c n)"), qt_ps[:, 0:2 * P], ACT.Copy).then_inc(qt_copied, 1)
                    if v:
                        diagonals(12, 16)
                    if sel:
                        act.wait_ge(top_ready, 1).then_inc(top_ready, -1)
                        nc.scalar.activation(exp_all[:, bass.ds((r * HEADS + g) * TOPK, TOPK)], top[:], ACT.Exp,
                                             bias=neg_max[:, 0:1]).then_inc(top_free, 1)
                    if u:
                        act.wait_ge(dots_ready, 1).then_inc(dots_ready, -1)
                        nc.scalar.activation(gelu[:, par, :], dots[:, par, :], ACT.Gelu).then_inc(gelu_ready, 1)
                groups(act, sel or u, ended, u, group, turn)
                if sel:
                    act.sem_inc(sel_free, 1)
            rounds(act, round_)

        @block.vector
        def _(dve):
            vec = nc.vector
            dve.sem_inc(u_free, RING)
            dve.sem_inc(sc_free, 1)
            dve.sem_inc(xu_free, 1)
            dve.sem_inc(acc_free, 1)
            dve.sem_inc(diag_free, DIAGS - 1)
            dve.sem_inc(y_free, 16)
            vec.memset(zero[:], 0.0).then_inc(zero_ready, 1)
            dve.wait_ge(consts, 3)
            vec.tensor_copy(iota16[:], iota_i[:])
            dve.drain()

            def choose(r, g):
                dve.wait_ge(sc_done, 1).then_inc(sc_done, -1)
                for c in range(2):
                    s = sc_ps[:, c * NKEYS:(c + 1) * NKEYS]
                    vec.max(val[:, c, 0:8], s)
                dve.drain()
                for c in range(2):
                    s = sc_ps[:, c * NKEYS:(c + 1) * NKEYS]
                    vec.max_index(idx[:, c, 0:8], val[:, c, 0:8], s)
                    vec.match_replace(work[:, c, :], val[:, c, 0:8], s, NEG)
                dve.drain().then_inc(sc_free, 1)
                for c in range(2):
                    vec.max(val[:, c, 8:16], work[:, c, :])
                dve.drain()
                for c in range(2):
                    vec.max_index(idx[:, c, 8:16], val[:, c, 8:16], work[:, c, :])
                vec.tensor_tensor(cand[:], val[:, 0, :].unsqueeze(2).broadcast_to([P, TOPK, TOPK]),
                                  val[:, 1, :].unsqueeze(1).broadcast_to([P, TOPK, TOPK]), ALU.add)
                dve.drain()
                vec.tensor_copy(idx_f[:], idx[:])
                dve.wait_ge(top_free, 1).then_inc(top_free, -1)
                flat = cand[:].rearrange("p a b -> p (a b)")
                vec.max(top[:, 0:8], flat)
                dve.drain()
                vec.max_index(pos[:, 0:8], top[:, 0:8], flat)
                vec.match_replace(cand2[:], top[:, 0:8], flat, NEG)
                dve.drain()
                vec.max(top[:, 8:16], cand2[:])
                vec.tensor_scalar(neg_max[:], top[:, 0:1], -1.0, None, ALU.mult)
                dve.drain().then_inc(top_ready, 1)
                vec.max_index(pos[:, 8:16], top[:, 8:16], cand2[:])
                dve.drain()
                vec.tensor_scalar(ab[:, 0, :], pos[:], 4, None, ALU.logical_shift_right)
                vec.tensor_scalar(ab[:, 1, :], pos[:], TOPK - 1, None, ALU.bitwise_and)
                dve.drain()
                vec.tensor_copy(ab_f[:], ab[:])
                dve.drain()
                full = [P, 2, TOPK, TOPK]
                vec.tensor_tensor(onehot[:], ab_f[:].unsqueeze(3).broadcast_to(full),
                                  iota16[:].unsqueeze(1).unsqueeze(1).broadcast_to(full), ALU.is_equal)
                dve.drain()
                vec.tensor_tensor(onehot[:], onehot[:], idx_f[:].unsqueeze(2).broadcast_to(full), ALU.mult)
                dve.drain()
                vec.tensor_reduce(picked[:], onehot[:], AX.X, ALU.add)
                dve.drain()
                vec.scalar_tensor_tensor(out=ids_all[:, bass.ds((r * HEADS + g) * TOPK, TOPK)], in0=picked[:, 0, :],
                                         scalar=float(NKEYS), in1=picked[:, 1, :], op0=ALU.mult, op1=ALU.add)\
                    .then_inc(ids_ready, 1)

            def round_(r, sel, u, ended):
                if u:
                    dve.wait_ge(xu_in, 16).then_inc(xu_in, -16)
                    dve.sem_inc(xu_for_pe, 1)
                if isinstance(r, int) and r == NT:
                    dve.wait_ge(top_free, 1).then_inc(top_free, -1)

                def group(g, par, v):
                    for j in range(TOPK):
                        slot = j % RING
                        if sel and j == 13:
                            choose(r, g)
                        if u:
                            dve.wait_ge(u_landed[slot], (((r - 1) * HEADS + g) * (TOPK // RING) + j // RING + 1) * 16)
                            vec.tensor_tensor_reduce(u_ring[:, slot, :], u_ring[:, slot, :], x1_u[:], 1.0, 0.0,
                                                     ALU.mult, ALU.add, dots[:, par, j:j + 1]).then_inc(u_free, 1)
                    if u:
                        dve.drain().then_inc(dots_ready, 1)
                        at = bass.ds(((r - 1) * HEADS + g) * TOPK, TOPK)
                        vec.tensor_reduce(rsum[:], exp_all[:, at], AX.X, ALU.add)
                        dve.drain()
                        vec.reciprocal(rsum[:], rsum[:])
                        dve.drain()
                        dve.wait_ge(gelu_ready, 1).then_inc(gelu_ready, -1)
                        vec.scalar_tensor_tensor(out=coef_all[:, at], in0=gelu[:, par, :], scalar=rsum[:, 0:1],
                                                 in1=exp_all[:, at], op0=ALU.mult, op1=ALU.mult).then_inc(coef_ready, 1)
                def turn():
                    if ended:
                        dve.wait_ge(acc_done, 1).then_inc(acc_done, -1)
                        for c in range(2):
                            vec.bn_stats(stats[:, c, :], acc[c][:])
                        dve.drain()
                        vec.bn_aggr(mv[:], stats[:].rearrange("p a b -> p (a b)"))
                        dve.drain()
                        vec.tensor_scalar(var[:], mv[:, 1:2], LN_EPS, None, ALU.add).then_inc(var_ready, 1)
                        dve.wait_ge(std_ready, 1).then_inc(std_ready, -1)
                        refine_rsqrt(nc, dve, rstd[:], var[:], std[:], tmp[:])
                        dve.wait_ge(y_free, 16).then_inc(y_free, -16)
                        for c in range(2):
                            vec.tensor_scalar(y[:, c * 512:(c + 1) * 512], acc[c][:], mv[:, 0:1], rstd[:, 0:1],
                                              ALU.subtract, ALU.mult)
                        dve.drain().then_inc(acc_free, 1)
                        dve.wait_ge(ln2_in, 32)
                        vec.tensor_tensor(y[:], y[:], g2[:], ALU.mult)
                        dve.drain()
                        vec.tensor_tensor(y[:], y[:], b2[:], ALU.add)
                        dve.drain().then_inc(y_ready, 1)
                groups(dve, sel or u, ended, u, group, turn)
                if u:
                    dve.wait_ge(opened, 1).then_inc(opened, -1)
                    dve.sem_inc(xu_free, 1)
            rounds(dve, round_)


_INS = ['x', 'x_t', 'positions', 'w_in', 'w_out', 'lambda_q1', 'lambda_k1', 'lambda_q2', 'lambda_k2', 'subln_g', 'conv_w',
        'conv_b', 'dt_bias', 'a_log', 'd_skip', 'ssd_norm_g', 'ln1_g', 'ln1_b', 'peer_wq', 'peer_keys', 'peer_u', 'peer_v',
        'ln2_g', 'ln2_b']


def build(nc, x, x_t, positions, w_in, w_out, lambda_q1, lambda_k1, lambda_q2, lambda_k2, subln_g, conv_w, conv_b, dt_bias,
          a_log, d_skip, ssd_norm_g, ln1_g, ln1_b, peer_wq, peer_keys, peer_u, peer_v, ln2_g, ln2_b, out):
    x1_dram = nc.dram_tensor("x1_rows", (T, D), F32).ap()
    x1t_dram = nc.dram_tensor("x1_tiles_t", (T, D), F32).ap()
    build_mixer(nc, x, x_t, positions, w_in, w_out, (lambda_q1, lambda_k1, lambda_q2, lambda_k2), subln_g, conv_w, conv_b,
                dt_bias, a_log, d_skip, ssd_norm_g, ln1_g, ln1_b, x1_dram, x1t_dram)
    build_experts(nc, x1_dram, x1t_dram, peer_wq, peer_keys, peer_u, peer_v, ln2_g, ln2_b, out)


def kernel(**inputs):
    import concourse.bacc as _bacc
    from concourse.bass_utils import run_bass_kernel_spmd as _run

    a = {name: np.asarray(v)[0] for name, v in inputs.items()}
    a["x_t"] = a["x"].T
    a["positions"] = a["positions"].reshape(NT, P).T
    a["conv_w"] = a["conv_w"].reshape(CONV, KC, P).transpose(2, 1, 0)
    a["conv_b"] = a["conv_b"].reshape(KC, P).T
    a["peer_keys"] = a["peer_keys"].transpose(3, 0, 1, 2).reshape(P, HEADS * 2 * NKEYS)

    nc = _bacc.Bacc("TRN2", target_bir_lowering=False, num_devices=1)
    arrays, args = {}, []
    for name in _INS:
        arrays[f"in_{name}_dram"] = np.ascontiguousarray(a[name])
        args.append(nc.dram_tensor(f"in_{name}_dram", a[name].shape, mybir.dt.from_np(a[name].dtype), kind="ExternalInput").ap())
    args.append(nc.dram_tensor("out_0_dram", (T, D), F32, kind="ExternalOutput").ap())
    build(nc, *args)
    r = _run(nc, [arrays], core_ids=[0])
    return r.results[0]["out_0_dram"].reshape(1, T, D)
```

```python
import math
from contextlib import ExitStack

import numpy as np

import concourse.bass as bass
from concourse import mybir

F32 = mybir.dt.float32
U32 = mybir.dt.uint32
I32 = mybir.dt.int32
ALU = mybir.AluOpType
ACT = mybir.ActivationFunctionType
AX = mybir.AxisListType

P = 128
ATT = SSD = 512
DA_HEADS = 4
DA_DIM = 64
DA_V = 128
HALF = DA_DIM // 2
SSD_HEADS = 8
SSD_DIM = 64
CONV = 4
LAMBDA_INIT = 0.8 - 0.6 * math.exp(-0.3 * 0)
RMS_EPS = 1e-5
FAR = -1.0e30
INV_FREQ = np.float32(10000.0) ** (-np.arange(0, DA_DIM, 2, dtype=np.float32) / np.float32(DA_DIM))
TURN = 2 * math.pi
TURN_PARTS = (6.28125, 2029 * 2.0 ** -20, TURN - 6.28125 - 2029 * 2.0 ** -20)
PI_BELOW = 3.1415925
ROUND = 1.5 * 2.0 ** 23
D = 1024
T = 1024
NT = T // P
KC = D // P
HEADS = 8
NKEYS = 128
DKEY = 256
TOPK = 16
SLOTS = HEADS * TOPK
RING = 8
DIAGS = 8
LAG = 6
FIRST_HEADS = HEADS - LAG
FIRST_SLOTS = FIRST_HEADS * TOPK
U_FIRST_RING = 4
NORM_AT = 4
ALPHA = 2.0 ** 0.25
LN_EPS = 1e-5
NEG = -3.0e38



class Choice:
    def __init__(self, sb, tag):
        def buf(name, shape, dt=F32):
            return sb(name + tag, shape, dt)
        self.val = buf("val", [P, 2, TOPK])
        self.idx = buf("idx", [P, 2, TOPK], U32)
        self.idx_f = buf("idx_f", [P, 2, TOPK])
        self.work = buf("work", [P, 2, NKEYS])
        self.cand = buf("cand", [P, TOPK, TOPK])
        self.top = buf("top", [P, TOPK])
        self.neg_max = buf("neg_max", [P, 1])
        self.pos = buf("pos", [P, TOPK], U32)
        self.ab = buf("ab", [P, 2, TOPK], U32)
        self.ab_f = buf("ab_f", [P, 2, TOPK])
        self.onehot = buf("onehot", [P, 2, TOPK, TOPK])
        self.picked = buf("picked", [P, 2, TOPK])
        self.iota16 = buf("iota16", [P, TOPK])
        self.iota_i = buf("iota_i", [P, TOPK], I32)


def choose_experts(vec, dve, b, scores, ids, sc_done, sc_free, top_free, top_ready):
    dve.wait_ge(sc_done, 1).then_inc(sc_done, -1)
    for c in range(2):
        s = scores[:, c * NKEYS:(c + 1) * NKEYS]
        vec.max(b.val[:, c, 0:8], s)
    dve.drain()
    for c in range(2):
        s = scores[:, c * NKEYS:(c + 1) * NKEYS]
        vec.max_index(b.idx[:, c, 0:8], b.val[:, c, 0:8], s)
        vec.match_replace(b.work[:, c, :], b.val[:, c, 0:8], s, NEG)
    dve.drain().then_inc(sc_free, 1)
    for c in range(2):
        vec.max(b.val[:, c, 8:16], b.work[:, c, :])
    dve.drain()
    for c in range(2):
        vec.max_index(b.idx[:, c, 8:16], b.val[:, c, 8:16], b.work[:, c, :])
    vec.tensor_tensor(b.cand[:], b.val[:, 0, :].unsqueeze(2).broadcast_to([P, TOPK, TOPK]),
                      b.val[:, 1, :].unsqueeze(1).broadcast_to([P, TOPK, TOPK]), ALU.add)
    dve.drain()
    vec.tensor_copy(b.idx_f[:], b.idx[:])
    dve.wait_ge(top_free, 1).then_inc(top_free, -1)
    flat = b.cand[:].rearrange("p a b -> p (a b)")
    rest = b.work[:].rearrange("p c n -> p (c n)")
    vec.max(b.top[:, 0:8], flat)
    dve.drain()
    vec.max_index(b.pos[:, 0:8], b.top[:, 0:8], flat)
    vec.match_replace(rest, b.top[:, 0:8], flat, NEG)
    dve.drain()
    vec.max(b.top[:, 8:16], rest)
    vec.tensor_scalar(b.neg_max[:], b.top[:, 0:1], -1.0, None, ALU.mult)
    dve.drain().then_inc(top_ready, 1)
    vec.max_index(b.pos[:, 8:16], b.top[:, 8:16], rest)
    dve.drain()
    vec.tensor_scalar(b.ab[:, 0, :], b.pos[:], 4, None, ALU.logical_shift_right)
    vec.tensor_scalar(b.ab[:, 1, :], b.pos[:], TOPK - 1, None, ALU.bitwise_and)
    dve.drain()
    vec.tensor_copy(b.ab_f[:], b.ab[:])
    dve.drain()
    full = [P, 2, TOPK, TOPK]
    vec.tensor_tensor(b.onehot[:], b.ab_f[:].unsqueeze(3).broadcast_to(full),
                      b.iota16[:].unsqueeze(1).unsqueeze(1).broadcast_to(full), ALU.is_equal)
    dve.drain()
    vec.tensor_tensor(b.onehot[:], b.onehot[:], b.idx_f[:].unsqueeze(2).broadcast_to(full), ALU.mult)
    dve.drain()
    vec.tensor_reduce(b.picked[:], b.onehot[:], AX.X, ALU.add)
    dve.drain()
    return vec.scalar_tensor_tensor(out=ids, in0=b.picked[:, 0, :],
                                    scalar=float(NKEYS), in1=b.picked[:, 1, :], op0=ALU.mult, op1=ALU.add)


def build_mixer(nc, x, x_t, positions, w_in, w_out, lambdas, subln_g, conv_w, conv_b, dt_bias, a_log,
                d_skip, ssd_norm_g, ln1_g, ln1_b, x1_dram, x1t_dram, peer_wq, keys_t, peer_u,
                ids_first, exp_first, coef_first, kept):
    vec, act_, mm = nc.vector, nc.scalar, nc.tensor
    with ExitStack() as ctx:
        def sb(name, shape, dt=F32, to=None):
            return (to or ctx).enter_context(nc.sbuf_tensor(name, shape, dt))

        def sem(name):
            return kept.enter_context(nc.semaphore(name))

        def handshake(name):
            return ctx.enter_context(nc.semaphore(name))

        bank = [ctx.enter_context(nc.psum_tensor(f"bank{i}", [P, 512], F32)) for i in range(4)]
        wide = [ctx.enter_context(nc.psum_tensor(f"wide{i}", [P, 1024], F32)) for i in range(2)]
        bank += [w[:, i * 512:(i + 1) * 512] for w in wide for i in range(2)]

        ident = sb("ident", [P, P])
        mask_qk = sb("mask_qk", [P, P])
        q_t = sb("q_t", [P, DA_HEADS, T])
        k_t = sb("k_t", [P, DA_HEADS, T])
        val = sb("val1", [P, NT, ATT])
        w_ring = sb("w_ring", [P, 2, KC, 512])
        half_neg = sb("half_neg", [P, 4])
        lam = sb("lam", [P, 1])
        minus_lam = sb("minus_lam", [P, 1])

        const_ready = sem("const_ready")
        w_out_in = sem("w_out_in")
        z = sb("z", [P, NT, SSD])
        step = sem("pool_step1")

        scan = ExitStack()
        ones = sb("ones", [P, P], to=scan)
        upper = sb("upper", [P, P], to=scan)
        mask_sl = sb("mask_sl", [P, 4, P], to=scan)
        xt = sb("xt", [P, KC, T], to=scan)
        xbc = sb("xbc", [P, KC, CONV - 1 + T], to=scan)
        dt_raw = sb("dt_raw", [P, NT * SSD_HEADS], to=scan)
        w_dt = sb("w_dt", [P, KC, SSD_HEADS], to=scan)
        cw = sb("cw", [P, KC, CONV], to=scan)
        cb = sb("cb", [P, KC], to=scan)
        conv = sb("conv", [P, T], to=scan)
        lam_in = sb("lam_in", [P, 4, DA_DIM], to=scan)
        lam_dot = sb("lam_dot", [P, 2], to=scan)
        lam_exp = sb("lam_exp", [P, 2], to=scan)
        pos_i = sb("pos_i", [P, NT], I32, to=scan)
        pos_f = sb("pos_f", [P, NT], to=scan)
        freq = sb("freq", [P, HALF], to=scan)
        ang = sb("ang", [P, NT, HALF], to=scan)
        whole = sb("whole", [P, NT, HALF], to=scan)
        trig = sb("trig", [P, 2, NT, HALF], to=scan)
        roped = sb("roped", [P, 2, ATT], to=scan)
        prod = sb("prod", [P, 2, ATT // 2], to=scan)

        per_head = [P, NT, SSD_HEADS]
        xs = sb("xs", [P, SSD], to=scan)
        bcs = sb("bcs", [P, 4 * P], to=scan)
        xd = sb("xd", [P, SSD], to=scan)
        xd_end = sb("xd_end", [P, SSD], to=scan)
        decay_in = sb("decay_in", [P, SSD_HEADS, P], to=scan)
        decays = sb("decays", [P, SSD_HEADS, P], to=scan)
        state = sb("state", [P, SSD], to=scan)
        ys = sb("ys", [P, SSD], to=scan)
        sq = sb("sq", [P, SSD], to=scan)
        ss = sb("ss", [P, 2], to=scan)
        rs = sb("rs", [P, 2], to=scan)
        norm_g = sb("norm_g", [P, SSD], to=scan)
        bias_dt = sb("bias_dt", [P, SSD_HEADS], to=scan)
        log_a = sb("log_a", [P, SSD_HEADS], to=scan)
        skip = sb("skip", [P, SSD_HEADS], to=scan)
        e_dt, u_dt, l_dt, dt, a, cs, ecs, dec, etot = (
            sb(n, per_head, to=scan) for n in ("e_dt", "u_dt", "l_dt", "dt", "a", "cs", "ecs", "dec", "etot"))


        chunk_in = [sem(f"chunk_in{i}") for i in range(KC)]
        w_landed = [sem(f"w_landed{i}") for i in range(2)]
        w_free = sem("w_free")
        dt_in = sem("dt_in")
        small_in = sem("small_in")
        act_group = sem("act_group")
        dve_group = sem("dve_group")
        bank_free = [sem(f"bank_free{i}") for i in range(2)]
        xbc_smooth = sem("xbc_smooth")
        dt_by_heads = sem("dt_by_heads")
        dt_copied = sem("dt_copied")
        dt_done = sem("dt_done")
        xbc_ready = sem("xbc_ready")
        conv_ready = sem("conv_ready")
        conv_free = sem("conv_free")
        turns_ready = sem("turns_ready")
        trig_ready = sem("trig_ready")
        lam_ready = sem("lam_ready")
        lam_exped = sem("lam_exped")
        roped_ready = sem("roped_ready")
        roped_free = sem("roped_free")

        vecs_in = sem("vecs_in")
        prep = sem("prep")
        prep_pe = sem("prep_pe")
        exp_done = sem("exp_done")
        prep_act = sem("prep_act")
        cs_done = sem("cs_done")
        xt_done = sem("xt_done")
        xt_free = sem("xt_free")
        z_ready = sem("z_ready")
        state_for_pe = sem("state_for_pe")
        bc_done = sem("bc_done")
        bc_free = sem("bc_free")
        l_in_ready = sem("l_in_ready")
        l_in_free = sem("l_in_free")
        l_done = sem("l_done")
        l_free = sem("l_free")
        xs_ready = sem("xs_ready")
        bcs_for_pe = sem("bcs_for_pe")
        decays_ready = sem("decays_ready")
        chunk_free = sem("chunk_free")
        xd_ready = sem("xd_ready")
        mixed_ready = sem("mixed_ready")
        st_done = sem("st_done")
        y_done = sem("y_done")
        y_banks_free = sem("y_banks_free")
        ss_ready = sem("ss_ready")
        rs_ready = sem("rs_ready")
        XT, BC, L, YO, ST, YD = bank[2], bank[3], bank[4], bank[5], bank[6], bank[7]
        flat = "p c h -> p (c h)"
        dt_t = decay_in[0:SSD_HEADS, :, :].rearrange("p h l -> p (h l)")

        def by_head(v):
            return v.unsqueeze(2).broadcast_to([P, SSD_HEADS, SSD_DIM])

        def heads(v):
            return v[:].rearrange("p (h d) -> p h d", d=SSD_DIM)

        blocks = [("xbc", 2048), ("xbc", 2560), ("z", 1536), ("v", 1024), ("k", 512), ("q", 0)]
        steps = 4 * NT

        def stage(step, lag):
            c, rest = divmod(step - 2 - lag, 3)
            return c if rest == 0 and 0 <= c < NT else None

        with nc.Block() as block:
            @block.sync
            def _(sp):
                def load(dst, n, c):
                    return sp.dma_start(dst, w_in[c * P:(c + 1) * P, blocks[n][1]:blocks[n][1] + 512])
                for c in range(KC):
                    sp.dma_start(xt[:, c, :], x_t[c * P:(c + 1) * P, :]).then_inc(chunk_in[c], 16)
                    load(w_ring[:, 0, c, :], 0, c).then_inc(chunk_in[c], 16)
                for n in range(1, len(blocks)):
                    if n >= 2:
                        sp.wait_ge(w_free, 1).then_inc(w_free, -1)
                    at = blocks[n][1]
                    sp.dma_start(w_ring[:, n % 2, :, :], w_in[:, at:at + 512].rearrange("(c p) n -> p c n", p=P))\
                        .then_inc(w_landed[n % 2], 16)
                for h in range(2):
                    sp.wait_ge(w_free, 1).then_inc(w_free, -1)
                    sp.dma_start(w_ring[:, h, :, :], w_out[:, h * 512:(h + 1) * 512].rearrange("(c p) n -> p c n", p=P))\
                        .then_inc(w_out_in, 16)

            @block.gpsimd
            def _(pool):
                pool.memset(ident[:], 0.0).then_inc(step, 1)
                pool.memset(upper[:], 1.0).then_inc(step, 1)
                pool.memset(ones[:], 1.0).then_inc(step, 1)
                pool.memset(mask_sl[:], 0.0).then_inc(step, 1)
                pool.memset(mask_qk[:], 0.0).then_inc(step, 1)
                pool.wait_ge(step, 5).then_inc(step, -5)
                pool.affine_select(out=ident[:], in_=ident[:], compare_op=ALU.not_equal, fill=1.0, base=0,
                                   pattern=[[-1, P]], channel_multiplier=1).then_inc(const_ready, 1)
                pool.affine_select(out=upper[:], in_=upper[:], compare_op=ALU.is_ge, fill=0.0, base=0,
                                   pattern=[[1, P]], channel_multiplier=-1).then_inc(const_ready, 1)
                pool.affine_select(out=mask_sl[:], in_=mask_sl[:], compare_op=ALU.is_ge, fill=FAR, base=0,
                                   pattern=[[0, 4], [1, P]], channel_multiplier=-1).then_inc(const_ready, 1)
                pool.affine_select(out=mask_qk[:], in_=mask_qk[:], compare_op=ALU.is_ge, fill=-FAR, base=0,
                                   pattern=[[-1, P]], channel_multiplier=1).then_inc(const_ready, 1)
                pool.memset(half_neg[:], -0.5).then_inc(step, 1)
                pool.wait_ge(step, 1).then_inc(step, -1)
                pool.wait_ge(prep, 1).then_inc(prep, -1)
                for c in range(NT):
                    pool.wait_ge(l_in_free, 1).then_inc(l_in_free, -1)
                    pool.tensor_tensor(decay_in[:], a[:, c, :].unsqueeze(2).broadcast_to([P, SSD_HEADS, P]),
                                       upper[:].unsqueeze(1).broadcast_to([P, SSD_HEADS, P]), ALU.mult).then_inc(l_in_ready, 1)
                    if c:
                        pool.wait_ge(ss_ready, 1).then_inc(ss_ready, -1)
                        pool.tensor_tensor(rs[:], ss[:], half_neg[:, 0:2], ALU.pow).then_inc(rs_ready, 1)
                pool.wait_ge(ss_ready, 1).then_inc(ss_ready, -1)
                pool.tensor_tensor(rs[:], ss[:], half_neg[:, 0:2], ALU.pow).then_inc(rs_ready, 1)

            @block.tensor
            def _(pe):
                pe.wait_ge(const_ready, 4)

                def channels(c, i):
                    return xbc[:, i, CONV - 1 + c * P:CONV - 1 + (c + 1) * P]

                def turn(n):
                    pe.wait_ge(roped_ready, 1).then_inc(roped_ready, -1)
                    pe.wait_ge(xt_free, 1).then_inc(xt_free, -1)
                    for h in range(DA_HEADS):
                        last = mm.transpose(XT[:, h * P:(h + 1) * P], roped[:, n % 2, h * P:(h + 1) * P], ident[:])
                    last.then_inc(xt_done, 1)

                def decay_half(i):
                    pe.wait_ge(l_free, 1).then_inc(l_free, -1)
                    mm.matmul(L[:], ones[:], decay_in[:, 4 * i:4 * i + 4, :].rearrange("p h l -> p (h l)"), start=True, stop=False)
                    mm.matmul(L[:], ident[:], mask_sl[:].rearrange("p h l -> p (h l)"), start=False, stop=True).then_inc(l_done, 1)

                def scan_stages(s):
                    if (c := stage(s, 3)) is not None:
                        pe.wait_ge(mixed_ready, 1).then_inc(mixed_ready, -1)
                        for h in range(SSD_HEADS):
                            last = mm.matmul(YD[:, h * SSD_DIM:(h + 1) * SSD_DIM], decays[:, h, :], xd[:, h * SSD_DIM:(h + 1) * SSD_DIM],
                                             start=True, stop=True)
                        last.then_inc(y_done, 1)
                    if (c := stage(s, 0)) is not None:
                        pe.wait_ge(xt_free, 1).then_inc(xt_free, -1)
                        for i in range(4):
                            last = mm.transpose(XT[:, i * P:(i + 1) * P], channels(c, i), ident[:])
                        last.then_inc(xt_done, 1)
                        pe.wait_ge(bc_free, 1).then_inc(bc_free, -1)
                        for g in range(2):
                            mm.transpose(BC[:, g * P:(g + 1) * P], channels(c, 4 + g), ident[:])
                        for g in range(2):
                            last = mm.matmul(BC[:, (2 + g) * P:(3 + g) * P], channels(c, 4 + g), channels(c, 6 + g), start=True, stop=True)
                        last.then_inc(bc_done, 1)
                        pe.wait_ge(l_in_ready, 1).then_inc(l_in_ready, -1)
                        decay_half(0)
                    if (c := stage(s, 1)) is not None:
                        decay_half(1)
                        pe.wait_ge(y_banks_free, 1).then_inc(y_banks_free, -1)
                        pe.wait_ge(state_for_pe, 1).then_inc(state_for_pe, -1)
                        for g in range(2):
                            mm.matmul(YO[:, g * 256:(g + 1) * 256], channels(c, 6 + g), state[:, g * 256:(g + 1) * 256], start=True, stop=True)
                    if (c := stage(s, 2)) is not None:
                        pe.wait_ge(xd_ready, 1).then_inc(xd_ready, -1)
                        pe.wait_ge(bcs_for_pe, 1).then_inc(bcs_for_pe, -1)
                        for g in range(2):
                            last = mm.matmul(ST[:, g * 256:(g + 1) * 256], bcs[:, g * P:(g + 1) * P], xd_end[:, g * 256:(g + 1) * 256],
                                             start=True, stop=True)
                        last.then_inc(st_done, 1)

                group = 0
                for n, (kind, _) in enumerate(blocks):
                    slot = n % 2
                    if n:
                        pe.wait_ge(w_landed[slot], 16).then_inc(w_landed[slot], -16)
                    for i in range(8):
                        s = group - 2 * NT
                        if n == 1 and i == 4:
                            pe.wait_ge(dt_copied, 1).then_inc(dt_copied, -1)
                            for t in range(NT):
                                last = mm.transpose(BC[:, t * SSD_HEADS:(t + 1) * SSD_HEADS], dt_t[:, t * P:(t + 1) * P],
                                                    ident[0:SSD_HEADS, 0:SSD_HEADS])
                            last.then_inc(dt_done, 1)
                        if s == 1:
                            pe.wait_ge(prep_pe, 1).then_inc(prep_pe, -1)
                            mm.matmul(YD[:, 0:64], upper[:], a[:].rearrange(flat), start=True, stop=True)
                            mm.matmul(YD[:, 64:128], ones[:], a[:].rearrange(flat), start=True, stop=True).then_inc(cs_done, 1)
                            pe.wait_ge(xbc_smooth, 1)
                        scan_stages(s)
                        b = group % 2
                        pe.wait_ge(bank_free[b], 1).then_inc(bank_free[b], -1)
                        for c in range(KC):
                            if n == 0 and i == 0:
                                pe.wait_ge(chunk_in[c], 32)
                            if kind == "xbc":
                                lhs = w_ring[:, slot, c, (i // 2) * P:(i // 2 + 1) * P]
                                rhs = xt[:, c, (i % 2) * 512:(i % 2 + 1) * 512]
                            else:
                                lhs, rhs = xt[:, c, i * P:(i + 1) * P], w_ring[:, slot, c, :]
                            last = mm.matmul(bank[b][:], lhs, rhs, start=(c == 0), stop=(c == KC - 1))
                            if n and i == 0 and c == 0:
                                last.then_inc(w_free, 1)
                        last.then_inc(dve_group if kind in "kq" else act_group, 1)
                        group += 1
                        if kind in "kq" and (kind == "q" or i):
                            turn((kind == "q") * 8 + i - 1)
                    if n == 0:
                        pe.wait_ge(dt_in, 16).then_inc(dt_in, -16)
                        for half, out in enumerate((BC, L)):
                            for c in range(KC):
                                last = mm.matmul(out[0:SSD_HEADS, :], w_dt[:, c, :], xt[:, c, half * 512:(half + 1) * 512],
                                                 start=(c == 0), stop=(c == KC - 1))
                        last.then_inc(dt_by_heads, 1)
                turn(15)
                pe.drain().then_inc(w_free, 1)

            @block.scalar
            def _(act):
                act.dma_start(pos_i[:], positions).then_inc(small_in, 16)
                for i in range(4):
                    act.dma_start(lam_in[:, i, :], lambdas[i].partition_broadcast(P)).then_inc(small_in, 16)
                act.dma_start(cw[:], conv_w).then_inc(small_in, 16)
                act.dma_start(cb[:], conv_b).then_inc(small_in, 16)
                act.dma_start(w_dt[:], w_in[:, 3072:3072 + SSD_HEADS].rearrange("(c p) n -> p c n", p=P)).then_inc(dt_in, 16)
                for dst, src in ((bias_dt, dt_bias), (log_a, a_log), (skip, d_skip), (norm_g, ssd_norm_g)):
                    act.dma_start(dst[:], src.partition_broadcast(P)).then_inc(vecs_in, 16)
                for free in (*bank_free, xt_free, l_free):
                    act.sem_inc(free, 1)
                act.wait_ge(small_in, 16 * 7)
                act.wait_ge(vecs_in, 64)
                act.wait_ge(turns_ready, 1).then_inc(turns_ready, -1)
                act_.activation(trig[:], trig[:], ACT.Sin).then_inc(trig_ready, 1)
                act.wait_ge(lam_ready, 1).then_inc(lam_ready, -1)
                act_.activation(lam_exp[:], lam_dot[:], ACT.Exp).then_inc(lam_exped, 1)

                def smooth(ch):
                    act.wait_ge(conv_ready, 1).then_inc(conv_ready, -1)
                    act_.activation(xbc[:, ch, CONV - 1:], conv[:], ACT.Silu, bias=cb[:, ch:ch + 1])
                    act.drain().then_inc(conv_free, 1)

                def evacuate(dst, func, group):
                    act.wait_ge(act_group, 1).then_inc(act_group, -1)
                    act_.activation(dst, bank[group % 2][:], func).then_inc(bank_free[group % 2], 1)

                def dt_exponentials():
                    act.wait_ge(prep_act, 1).then_inc(prep_act, -1)
                    act_.activation(e_dt[:], e_dt[:], ACT.Exp)
                    act_.activation(log_a[:], log_a[:], ACT.Exp)
                    act.drain().then_inc(exp_done, 1)
                    act.wait_ge(prep_act, 1).then_inc(prep_act, -1)
                    act_.activation(l_dt[:], u_dt[:], ACT.Ln).then_inc(exp_done, 1)

                for ch in range(KC):
                    for half in range(2):
                        if ch == KC - 1 and half:
                            dt_exponentials()
                        at = CONV - 1 + half * 512
                        evacuate(xbc[:, ch, at:at + 512], ACT.Copy, 2 * ch + half)
                    act.drain().then_inc(xbc_ready, 1)
                    if ch == KC // 2 - 1:
                        act.wait_ge(dt_by_heads, 1).then_inc(dt_by_heads, -1)
                        for half, src in enumerate((BC, L)):
                            act_.activation(dt_t[:, half * 512:(half + 1) * 512], src[0:SSD_HEADS, :], ACT.Copy)
                        act.drain().then_inc(dt_copied, 1)
                    if ch:
                        smooth(ch - 1)
                smooth(KC - 1)
                act.sem_inc(xbc_smooth, 1)

                def keep_turned(n):
                    act.wait_ge(xt_done, 1).then_inc(xt_done, -1)
                    act.sem_inc(roped_free, 1)
                    dst = (k_t if n < NT else q_t)[:, :, (n % NT) * P:(n % NT + 1) * P]
                    act_.activation(dst, XT[:].rearrange("p (h n) -> p h n", h=DA_HEADS), ACT.Copy,
                                    scale=1.0 if n < NT else -DA_DIM ** -0.5).then_inc(xt_free, 1)

                def decay_exponentials(c, i):
                    act.wait_ge(l_done, 1).then_inc(l_done, -1)
                    for h in range(4 * i, 4 * i + 4):
                        act_.activation(decays[:, h, :], L[:, (h % 4) * P:(h % 4 + 1) * P], ACT.Exp, bias=cs[:, c, h:h + 1])
                    act.drain().then_inc(l_free, 1)
                    act.sem_inc(decays_ready, 1)

                for s in range(steps):
                    if s == 1:
                        act.wait_ge(prep_act, 1).then_inc(prep_act, -1)
                        act_.activation(ecs[:], cs[:], ACT.Exp)
                        act_.activation(dec[:], dec[:], ACT.Exp)
                        act_.activation(etot[:], etot[:], ACT.Exp)
                        act.drain().then_inc(exp_done, 1)
                        act.wait_ge(prep_act, 1).then_inc(prep_act, -1)
                    if (c := stage(s, 0)) is not None:
                        act.wait_ge(xt_done, 1).then_inc(xt_done, -1)
                        act.wait_ge(chunk_free, 1).then_inc(chunk_free, -1)
                        act_.activation(xs[:], XT[:], ACT.Copy)
                        act.drain().then_inc(xt_free, 1)
                        act.sem_inc(xs_ready, 1)
                        act.wait_ge(bc_done, 1).then_inc(bc_done, -1)
                        act_.activation(bcs[:], BC[:], ACT.Copy)
                        act.drain().then_inc(bc_free, 1)
                        act.sem_inc(bcs_for_pe, 1)
                        decay_exponentials(c, 0)
                    if (c := stage(s, 1)) is not None:
                        decay_exponentials(c, 1)
                        act.sem_inc(l_in_free, 1)
                    if s < NT:
                        evacuate(z[:, s, :], ACT.Silu, s)
                        act.drain().then_inc(z_ready, 1)
                    elif s < 2 * NT:
                        evacuate(val[:, s - NT, :], ACT.Copy, s)
                    n = s - 2 * NT - 1
                    if n >= 0:
                        keep_turned(n)
                keep_turned(2 * NT - 1)

            @block.vector
            def _(dve):
                dve.sem_inc(conv_free, 1)
                for i in range(HALF):
                    vec.memset(freq[:, i:i + 1], float(INV_FREQ[i]))
                vec.memset(xbc[:, :, 0:CONV - 1], 0.0)
                dve.wait_ge(small_in, 16 * 7)
                vec.tensor_copy(pos_f[:], pos_i[:])
                for i in range(2):
                    vec.tensor_tensor_reduce(lam_in[:, 2 * i, :], lam_in[:, 2 * i, :], lam_in[:, 2 * i + 1, :], 1.0, 0.0,
                                             ALU.mult, ALU.add, lam_dot[:, i:i + 1])
                dve.drain().then_inc(lam_ready, 1)
                full = [P, NT, HALF]
                vec.tensor_tensor(ang[:], pos_f[:].unsqueeze(2).broadcast_to(full), freq[:].unsqueeze(1).broadcast_to(full), ALU.mult)
                dve.drain()
                for i, quarter in enumerate((0.25, 0.0)):
                    t, n = trig[:, i], whole[:]
                    vec.tensor_scalar(n, ang[:], 1 / TURN, quarter, ALU.mult, ALU.add)
                    dve.drain()
                    vec.tensor_scalar(n, n, ROUND, None, ALU.add)
                    dve.drain()
                    vec.tensor_scalar(n, n, ROUND, None, ALU.subtract)
                    dve.drain()
                    vec.tensor_copy(t, ang[:])
                    for part in TURN_PARTS:
                        dve.drain()
                        vec.scalar_tensor_tensor(out=t, in0=n, scalar=-part, in1=t, op0=ALU.mult, op1=ALU.add)
                    dve.drain()
                    vec.tensor_scalar(t, t, quarter * TURN, PI_BELOW, ALU.add, ALU.min)
                    dve.drain()
                    vec.tensor_scalar(t, t, -PI_BELOW, None, ALU.max)
                dve.drain().then_inc(turns_ready, 1)
                dve.wait_ge(lam_exped, 1).then_inc(lam_exped, -1)
                vec.tensor_tensor(lam[:], lam_exp[:, 0:1], lam_exp[:, 1:2], ALU.subtract)
                dve.drain()
                vec.tensor_scalar(minus_lam[:], lam[:], LAMBDA_INIT, -1.0, ALU.add, ALU.mult)

                def prepare_steps():
                    dve.wait_ge(dt_done, 1).then_inc(dt_done, -1)
                    vec.tensor_copy(dt_raw[:], BC[:, 0:NT * SSD_HEADS])
                    dve.drain().then_inc(bc_free, 1)
                    dve.wait_ge(trig_ready, 1).then_inc(trig_ready, -1)
                    dve.sem_inc(roped_free, 2)
                    vec.memset(state[:], 0.0).then_inc(state_for_pe, 1)
                    dve.sem_inc(l_in_free, 1)
                    dve.sem_inc(chunk_free, 1)
                    dve.sem_inc(y_banks_free, 1)
                    dve.wait_ge(vecs_in, 64)
                    raw = dt_raw[:].rearrange("p (c h) -> p c h", h=SSD_HEADS)
                    vec.tensor_tensor(raw, raw, bias_dt[:].unsqueeze(1).broadcast_to(per_head), ALU.add)
                    dve.drain()
                    vec.tensor_scalar(u_dt[:], raw, -1.0, None, ALU.mult)
                    dve.drain()
                    vec.tensor_tensor(e_dt[:], raw, u_dt[:], ALU.min)
                    dve.drain().then_inc(prep_act, 1)
                    dve.wait_ge(exp_done, 1).then_inc(exp_done, -1)
                    vec.tensor_scalar(u_dt[:], e_dt[:], 1.0, None, ALU.add)
                    dve.drain().then_inc(prep_act, 1)
                    vec.tensor_scalar(dt[:], u_dt[:], -1.0, None, ALU.add)
                    dve.drain()
                    vec.tensor_tensor(e_dt[:], e_dt[:], dt[:], ALU.subtract)
                    dve.wait_ge(exp_done, 1).then_inc(exp_done, -1)
                    vec.reciprocal(u_dt[:], u_dt[:])
                    dve.drain()
                    vec.tensor_tensor(e_dt[:], e_dt[:], u_dt[:], ALU.mult)
                    vec.tensor_scalar(dt[:], raw, 0.0, None, ALU.max)
                    dve.drain()
                    vec.tensor_tensor(dt[:], dt[:], e_dt[:], ALU.add)
                    dve.drain()
                    vec.tensor_tensor(dt[:], dt[:], l_dt[:], ALU.add)
                    vec.tensor_scalar(log_a[:], log_a[:], -1.0, None, ALU.mult)
                    dve.drain()
                    vec.tensor_tensor(a[:], dt[:], log_a[:].unsqueeze(1).broadcast_to(per_head), ALU.mult)
                    dve.drain().then_inc(prep, 1)
                    dve.sem_inc(prep_pe, 1)

                for ch in range(KC):
                    if ch == KC - 1:
                        prepare_steps()
                    dve.wait_ge(xbc_ready, 1).then_inc(xbc_ready, -1)
                    dve.wait_ge(conv_free, 1).then_inc(conv_free, -1)
                    vec.tensor_scalar(conv[:], xbc[:, ch, 0:T], cw[:, ch, 0:1], None, ALU.mult)
                    for i in range(1, CONV):
                        dve.drain()
                        vec.scalar_tensor_tensor(out=conv[:], in0=xbc[:, ch, i:i + T], scalar=cw[:, ch, i:i + 1],
                                                 in1=conv[:], op0=ALU.mult, op1=ALU.add)
                    dve.drain().then_inc(conv_ready, 1)
                dve.wait_ge(cs_done, 1).then_inc(cs_done, -1)
                both = YD[:, 0:128].rearrange("p (k c h) -> p k c h", k=2, h=SSD_HEADS)
                vec.tensor_copy(cs[:], both[:, 0])
                vec.tensor_copy(etot[:], both[:, 1])
                dve.drain()
                vec.tensor_tensor(dec[:], etot[:], cs[:], ALU.subtract)
                dve.drain().then_inc(prep_act, 1)
                dve.wait_ge(exp_done, 1).then_inc(exp_done, -1)
                vec.tensor_scalar(cs[:], cs[:], -1.0, None, ALU.mult)
                dve.drain().then_inc(prep_act, 1)

                def rope(n):
                    t, b = n % NT, n % 2
                    dve.wait_ge(dve_group, 1).then_inc(dve_group, -1)
                    src = bank[b][:].rearrange("p (g two n) -> p g two n", two=2, n=HALF)
                    dst = roped[:, n % 2, :].rearrange("p (g two n) -> p g two n", two=2, n=HALF)
                    part = [P, 2 * DA_HEADS, HALF]
                    cos = trig[:, 0, t, :].unsqueeze(1).broadcast_to(part)
                    sin = trig[:, 1, t, :].unsqueeze(1).broadcast_to(part)
                    p0, p1 = (prod[:, i, :].rearrange("p (g n) -> p g n", n=HALF) for i in range(2))
                    dve.wait_ge(roped_free, 1).then_inc(roped_free, -1)
                    vec.tensor_tensor(p0, src[:, :, 1, :], sin, ALU.mult)
                    vec.tensor_tensor(p1, src[:, :, 0, :], sin, ALU.mult)
                    vec.tensor_tensor(dst[:, :, 0, :], src[:, :, 0, :], cos, ALU.mult)
                    vec.tensor_tensor(dst[:, :, 1, :], src[:, :, 1, :], cos, ALU.mult)
                    dve.drain().then_inc(bank_free[b], 1)
                    vec.tensor_tensor(dst[:, :, 0, :], dst[:, :, 0, :], p0, ALU.subtract)
                    vec.tensor_tensor(dst[:, :, 1, :], dst[:, :, 1, :], p1, ALU.add)
                    dve.drain().then_inc(roped_ready, 1)

                for s in range(steps):
                    if (c := stage(s, 3)) is not None:
                        dve.wait_ge(y_done, 1).then_inc(y_done, -1)
                        vec.tensor_tensor(heads(ys), YO[:].rearrange("p (h d) -> p h d", d=SSD_DIM), by_head(ecs[:, c, :]), ALU.mult)
                        vec.tensor_tensor(heads(sq), heads(xs), by_head(skip[:]), ALU.mult)
                        dve.drain()
                        vec.tensor_tensor(ys[:], ys[:], YD[:], ALU.add)
                        dve.drain().then_inc(y_banks_free, 1)
                        dve.sem_inc(chunk_free, 1)
                        vec.tensor_tensor(ys[:], ys[:], sq[:], ALU.add)
                        dve.drain()
                        dve.wait_ge(z_ready, 1).then_inc(z_ready, -1)
                        vec.tensor_tensor(ys[:], ys[:], z[:, c, :], ALU.mult)
                        dve.drain()
                        for g in range(2):
                            part = slice(g * 256, (g + 1) * 256)
                            vec.tensor_tensor_reduce(sq[:, part], ys[:, part], ys[:, part], 1.0, 0.0, ALU.mult, ALU.add, ss[:, g:g + 1])
                        dve.drain()
                        vec.tensor_scalar(ss[:], ss[:], 1.0 / 256, RMS_EPS, ALU.mult, ALU.add)
                        dve.drain().then_inc(ss_ready, 1)
                    if (c := stage(s, 0)) is not None:
                        dve.wait_ge(xs_ready, 1).then_inc(xs_ready, -1)
                        vec.tensor_tensor(heads(xd), heads(xs), by_head(dt[:, c, :]), ALU.mult)
                        dve.drain()
                        vec.tensor_tensor(heads(xd_end), heads(xd), by_head(dec[:, c, :]), ALU.mult)
                        dve.drain().then_inc(xd_ready, 1)
                    for g in range(2):
                        if (c := stage(s, 1 + g)) is not None:
                            dve.wait_ge(decays_ready, 1).then_inc(decays_ready, -1)
                            vec.tensor_tensor(decays[:, 4 * g:4 * g + 4, :], decays[:, 4 * g:4 * g + 4, :],
                                              bcs[:, (2 + g) * P:(3 + g) * P].unsqueeze(1).broadcast_to([P, 4, P]), ALU.mult)
                            if g:
                                dve.drain().then_inc(mixed_ready, 1)
                    if (c := stage(s, 2)) is not None:
                        dve.wait_ge(st_done, 1).then_inc(st_done, -1)
                        vec.tensor_tensor(heads(state), heads(state), by_head(etot[:, c, :]), ALU.mult)
                        dve.drain()
                        vec.tensor_tensor(state[:], state[:], ST[:], ALU.add)
                        dve.drain().then_inc(state_for_pe, 1)
                    if (c := stage(s, 4)) is not None:
                        dve.wait_ge(rs_ready, 1).then_inc(rs_ready, -1)
                        for g in range(2):
                            part = slice(g * 256, (g + 1) * 256)
                            vec.scalar_tensor_tensor(out=z[:, c, part], in0=ys[:, part], scalar=rs[:, g:g + 1], in1=norm_g[:, part],
                                                     op0=ALU.mult, op1=ALU.mult)
                        dve.drain()
                    if s >= 2 * NT:
                        rope(s - 2 * NT)
        scan.close()

        probs0 = sb("probs0", [P, 3, T])
        probs1 = sb("probs1", [P, 2, T])
        wt = sb("wt", [P, 2, NT, P])
        x1 = sb("x1", [P, 2, D])
        x1t = sb("x1t_out", [P, KC, P])
        g1 = sb("g1", [P, D])
        b1 = sb("b1", [P, D])
        att = sb("att", [P, ATT])
        sub_g = sb("sub_g", [P, DA_V])
        mix_t = sb("mix_t", [P, KC, P])
        neg_mx = sb("neg_mx", [P, 2, 2])
        rsum = sb("rsum1", [P, 3, 2])
        rinv = sb("rinv", [P, 2, DA_HEADS, 2])
        ratio = sb("ratio", [P, 1])
        av = sb("av", [P, DA_HEADS])
        ar = sb("ar", [P, DA_HEADS])
        stats = sb("stats1", [P, 2, 6])
        mv = sb("mv1", [P, 2])
        var = sb("var1", [P, 1])
        rstd = sb("rstd1", [P, 1])

        b = Choice(sb, "_first")
        x1t_first = sb("x1t_first", [P, KC, P])
        x1_first = sb("x1_first", [P, D])
        wq_pair = sb("wq_pair", [P, KC, 2 * DKEY])
        keys_pair = sb("keys_pair", [P, 2 * DKEY])
        q_pair = sb("q_pair", [P, 2 * DKEY])
        qt_pair = sb("qt_pair", [P, 2 * DKEY])
        sc_pair = sb("sc_pair", [P, 2 * DKEY])
        u_rows = sb("u_rows", [P, U_FIRST_RING, D])
        dots_first = sb("dots_first", [P, FIRST_SLOTS])
        sums_first = sb("sums_first", [P, FIRST_HEADS])
        wq_in = sem("wq_in")
        wq_free = sem("wq_free")
        x1t_first_ready = sem("x1t_first_ready")
        q_done = handshake("q_done1")
        q_copied = handshake("q_copied1")
        qt_done = handshake("qt_done1")
        qt_copied = handshake("qt_copied1")
        pair_scored = handshake("pair_scored")
        pair_for_pe = handshake("pair_for_pe")
        pair_for_dve = sem("pair_for_dve")
        pair_free = sem("pair_free")
        pair_seen = sem("pair_seen")
        top_free = sem("top_free1")
        top_ready = sem("top_ready1")
        iota_ready = sem("iota_ready")
        ids_ready = sem("ids_ready1")
        rows_landed = [sem(f"rows_landed{i}") for i in range(U_FIRST_RING)]
        rows_free = sem("rows_free")
        dots_ready = handshake("dots_ready1")
        gelu_ready = handshake("gelu_ready1")

        norm_in = sem("norm_in")
        sc_done = [sem(f"sc_done{i}") for i in range(2)]
        sc_free = [sem(f"sc_free{i}1") for i in range(2)]
        mx_ready = [sem(f"mx_ready{i}") for i in range(2)]
        probs_ready = handshake("probs_ready")
        w_ready = handshake("w_ready")
        t_done = [sem(f"t_done{i}") for i in range(2)]
        t_free = [sem(f"t_free{i}") for i in range(2)]
        wt_ready = handshake("wt_ready")
        pv_done = handshake("pv_done")
        pv_free = sem("pv_free")
        att_copied = handshake("att_copied")
        av_ready = handshake("av_ready")
        ar_ready = handshake("ar_ready")
        att_ready = handshake("att_ready")
        mix_ready = handshake("mix_ready")
        op_done = handshake("op_done")
        op_free = sem("op_free")
        xtile_in = sem("xtile_in")
        var_ready = handshake("var_ready1")
        rstd_ready = handshake("rstd_ready1")
        normed = sem("normed")
        x1_first_ready = sem("x1_first_ready")
        x1_ready = handshake("x1_ready")
        x1_turn = handshake("x1_turn")
        x1_free = sem("x1_free")
        x1_landed = [sem(f"x1_landed{i}") for i in range(2)]
        x1t_ready = handshake("x1t_ready")
        x1t_landed = sem("x1t_landed")
        SC, TP, PV, OP = wide, bank[0:2], bank[2], bank[3]
        items = NT * DA_HEADS
        CHOICE = 15
        last_step = items - 1 + 12

        def choice(n, lag):
            g, rest = divmod(n - CHOICE - lag, DA_HEADS)
            return g if rest == 0 and 0 <= g < HEADS // 2 else None

        def products(n):
            def count(k):
                if k < CHOICE + 7:
                    return 0
                return (2, 2, 3, 4)[k % DA_HEADS]
            done = sum(count(k) for k in range(n))
            return range(min(done, FIRST_SLOTS), min(done + count(n), FIRST_SLOTS))

        def tail(n, lag):
            t, rest = divmod(n - lag, DA_HEADS)
            return t if rest == 0 and 0 <= t < NT else None

        with nc.Block() as block:
            @block.sync
            def _(sp):
                for dst, src in ((g1, ln1_g), (b1, ln1_b), (sub_g, subln_g)):
                    sp.dma_start(dst[:], src.partition_broadcast(P)).then_inc(norm_in, 16)

                def load_pair(g):
                    part = slice(g * 2 * DKEY, (g + 1) * 2 * DKEY)
                    sp.dma_start(wq_pair[:], peer_wq[:, part].rearrange("(c p) n -> p c n", p=P)).then_inc(wq_in, 16)
                    sp.dma_start(keys_pair[:], keys_t[:, part]).then_inc(wq_in, 16)
                load_pair(0)
                for t in range(NT):
                    if t >= 2:
                        sp.wait_ge(x1_landed[t % 2], 16).then_inc(x1_landed[t % 2], -16)
                        sp.wait_ge(x1_free, 1).then_inc(x1_free, -1)
                    sp.dma_start(x1[:, t % 2, :], x[t * P:(t + 1) * P, :]).then_inc(xtile_in, 16)
                    if 1 <= t - 1 < HEADS // 2:
                        sp.wait_ge(wq_free, 1).then_inc(wq_free, -1)
                        load_pair(t - 1)
                    sp.wait_ge(x1_ready, 1).then_inc(x1_ready, -1)
                    sp.dma_start(x1_dram[t * P:(t + 1) * P, :], x1[:, t % 2, :]).then_inc(x1_landed[t % 2], 16)
                    sp.wait_ge(x1t_ready, 1).then_inc(x1t_ready, -1)
                    sp.dma_start(x1t_dram[t * P:(t + 1) * P, :], x1t[:].rearrange("p c n -> p (c n)")).then_inc(x1t_landed, 16)
                for i in range(2):
                    sp.wait_ge(x1_landed[i], 16).then_inc(x1_landed[i], -16)
                sp.wait_ge(x1t_landed, 16).then_inc(x1t_landed, -16)

            @block.gpsimd
            def _(pool):
                pool.iota(b.iota_i[:], [[1, TOPK]], base=0, channel_multiplier=0).then_inc(iota_ready, 1)
                for n in range(last_step + 1):
                    if tail(n, 7) is not None:
                        pool.wait_ge(av_ready, 1).then_inc(av_ready, -1)
                        pool.tensor_tensor(ar[:], av[:], half_neg[:], ALU.pow).then_inc(ar_ready, 1)
                    if tail(n, 10) is not None:
                        pool.wait_ge(var_ready, 1).then_inc(var_ready, -1)
                        pool.tensor_tensor(rstd[:], var[:], half_neg[:, 0:1], ALU.pow).then_inc(rstd_ready, 1)
                    if (t := tail(n, 11)) is not None:
                        tile = x1[:, t % 2, :]
                        if t == 0:
                            pool.wait_ge(norm_in, 48)
                        pool.wait_ge(normed, 1).then_inc(normed, -1)
                        if t < NT - 1:
                            pool.tensor_tensor(tile, tile, g1[:], ALU.mult).then_inc(step, 1)
                            pool.wait_ge(step, 1).then_inc(step, -1)
                            pool.tensor_tensor(tile, tile, b1[:], ALU.add).then_inc(step, 1)
                            pool.wait_ge(step, 1).then_inc(step, -1)
                        pool.sem_inc(x1_ready, 1)
                        pool.sem_inc(x1_turn, 1)
                        if t == 0:
                            pool.tensor_copy(x1_first[:], tile).then_inc(x1_first_ready, 1)
                    for k in products(n + 1):
                        if k % TOPK == 0:
                            pool.wait_ge(ids_ready, 1).then_inc(ids_ready, -1)
                        pool.wait_ge(rows_free, 1).then_inc(rows_free, -1)
                        pool.indirect_dma_start(u_rows[:, k % U_FIRST_RING, :], None, peer_u,
                                                bass.IndirectOffsetOnAxis(ap=ids_first[:, k:k + 1], axis=0))\
                            .then_inc(rows_landed[k % U_FIRST_RING], 16)

            @block.tensor
            def _(pe):

                def scores(n):
                    t, h = divmod(n, DA_HEADS)
                    keys = (t + 1) * P
                    for c in range(2):
                        rows = slice(c * DA_DIM, (c + 1) * DA_DIM)
                        pe.wait_ge(sc_free[c], 1).then_inc(sc_free[c], -1)
                        for k0 in range(0, keys, 512):
                            k1 = min(keys, k0 + 512)
                            diagonal = k1 == keys
                            last = mm.matmul(SC[c][:, k0:k1], q_t[rows, h, t * P:(t + 1) * P], k_t[rows, h, k0:k1],
                                             start=True, stop=not diagonal)
                            if diagonal:
                                last = mm.matmul(SC[c][:, k1 - P:k1], ident[:], mask_qk[:], start=False, stop=True)
                        last.then_inc(sc_done[c], 1)

                def turn(n):
                    t = n // DA_HEADS
                    pe.wait_ge(w_ready, 1).then_inc(w_ready, -1)
                    for piece in range(t // 4 + 1):
                        pe.wait_ge(t_free[piece], 1).then_inc(t_free[piece], -1)
                        for k in range(4 * piece, min(4 * piece + 4, t + 1)):
                            last = mm.transpose(TP[piece][:, (k % 4) * P:(k % 4 + 1) * P], probs0[:, n % 3, k * P:(k + 1) * P], ident[:])
                        last.then_inc(t_done[piece], 1)

                def weigh(n):
                    t, h = divmod(n, DA_HEADS)
                    if h == 0:
                        pe.wait_ge(pv_free, 1).then_inc(pv_free, -1)
                    pe.wait_ge(wt_ready, 1).then_inc(wt_ready, -1)
                    for k in range(t + 1):
                        last = mm.matmul(PV[:, h * P:(h + 1) * P], wt[:, n % 2, k, :], val[:, k, h * P:(h + 1) * P],
                                         start=(k == 0), stop=(k == t))
                    if h == DA_HEADS - 1:
                        last.then_inc(pv_done, 1)

                for n in range(last_step + 1):
                    if n < items:
                        scores(n)
                    if choice(n, 0) is not None:
                        if choice(n, 0) == 0:
                            pe.wait_ge(x1t_first_ready, 1).then_inc(x1t_first_ready, -1)
                        pe.wait_ge(wq_in, 32).then_inc(wq_in, -32)
                        pe.wait_ge(op_free, 1).then_inc(op_free, -1)
                        for c in range(KC):
                            last = mm.matmul(OP[:], x1t_first[:, c, :], wq_pair[:, c, :], start=(c == 0), stop=(c == KC - 1))
                        last.then_inc(q_done, 1)
                    if choice(n, 1) is not None:
                        pe.wait_ge(q_copied, 1).then_inc(q_copied, -1)
                        for c in range(4):
                            last = mm.transpose(OP[:, c * P:(c + 1) * P], q_pair[:, c * P:(c + 1) * P], ident[:])
                        last.then_inc(qt_done, 1)
                    if choice(n, 2) is not None:
                        pe.wait_ge(qt_copied, 1).then_inc(qt_copied, -1)
                        for c in range(4):
                            at = slice(c * P, (c + 1) * P)
                            last = mm.matmul(OP[:, at], qt_pair[:, at], keys_pair[:, at], start=True, stop=True)
                        last.then_inc(pair_scored, 1)
                    if 2 <= n < items + 2:
                        turn(n - 2)
                    if 3 <= n < items + 3:
                        weigh(n - 3)
                    if tail(n, 9) is not None:
                        pe.wait_ge(att_ready, 1).then_inc(att_ready, -1)
                        for piece, src in ((0, att[:]), (1, z[:, tail(n, 9), :])):
                            pe.wait_ge(t_free[piece], 1).then_inc(t_free[piece], -1)
                            for i in range(4):
                                last = mm.transpose(TP[piece][:, i * P:(i + 1) * P], src[:, i * P:(i + 1) * P], ident[:])
                            last.then_inc(t_done[piece], 1)
                    if (t := tail(n, 10)) is not None:
                        if t == 0:
                            pe.wait_ge(w_out_in, 32)
                        pe.wait_ge(mix_ready, 1).then_inc(mix_ready, -1)
                        for half in range(2):
                            if half == 0 and choice(n, 3) is not None:
                                pe.wait_ge(pair_for_pe, 1).then_inc(pair_for_pe, -1)
                            else:
                                pe.wait_ge(op_free, 1).then_inc(op_free, -1)
                            for c in range(KC):
                                last = mm.matmul(OP[:], mix_t[:, c, :], w_ring[:, half, c, :],
                                                 start=(c == 0), stop=(c == KC - 1))
                            last.then_inc(op_done, 1)
                    if tail(n, 12) is not None:
                        pe.wait_ge(x1_turn, 1).then_inc(x1_turn, -1)
                        for piece in range(2):
                            pe.wait_ge(t_free[piece], 1).then_inc(t_free[piece], -1)
                            for i in range(4):
                                at = (4 * piece + i) * P
                                last = mm.transpose(TP[piece][:, i * P:(i + 1) * P], x1[:, tail(n, 12) % 2, at:at + P], ident[:])
                            last.then_inc(t_done[piece], 1)

            @block.scalar
            def _(act):
                for s in (*t_free, *sc_free, pv_free):
                    act.sem_inc(s, 1)
                act.sem_inc(x1t_landed, 16)
                act.sem_inc(top_free, 1)
                for n in range(last_step + 1):
                    if n < items:
                        keys = (n // DA_HEADS + 1) * P
                        for c in range(2):
                            act.wait_ge(mx_ready[c], 1).then_inc(mx_ready[c], -1)
                            act_.activation((probs0[:, n % 3] if c == 0 else probs1[:, n % 2])[:, 0:keys], SC[c][:, 0:keys], ACT.Exp, bias=neg_mx[:, n % 2, c:c + 1],
                                            scale=-1.0, accum_out=rsum[:, n % 3, c:c + 1])
                            act.drain().then_inc(sc_free[c], 1)
                        act.sem_inc(probs_ready, 1)
                    for which in range(2):
                        if (g := choice(n, 6 + which)) is not None:
                            act.wait_ge(top_ready, 1).then_inc(top_ready, -1)
                            act_.activation(exp_first[:, (2 * g + which) * TOPK:(2 * g + which + 1) * TOPK], b.top[:], ACT.Exp,
                                            bias=b.neg_max[:, 0:1]).then_inc(top_free, 1)
                    if 2 <= n < items + 2:
                        m = n - 2
                        t = m // DA_HEADS
                        for piece in range(t // 4 + 1):
                            k0, k1 = 4 * piece, min(4 * piece + 4, t + 1)
                            act.wait_ge(t_done[piece], 1).then_inc(t_done[piece], -1)
                            act_.activation(wt[:, m % 2, k0:k1, :].rearrange("p k n -> p (k n)"), TP[piece][:, 0:(k1 - k0) * P], ACT.Copy)
                            act.drain().then_inc(t_free[piece], 1)
                        act.sem_inc(wt_ready, 1)
                    if tail(n, 6) is not None:
                        act.wait_ge(pv_done, 1).then_inc(pv_done, -1)
                        for h in range(DA_HEADS):
                            part = slice(h * DA_V, (h + 1) * DA_V)
                            factor = rinv[:, tail(n, 6) % 2, h, 0:1]
                            act_.activation(att[:, part], PV[:, part], ACT.Copy, scale=factor)
                            act_.activation(PV[:, part], PV[:, part], ACT.Square, scale=factor, accum_out=av[:, h:h + 1])
                        act.drain().then_inc(pv_free, 1)
                        act.sem_inc(att_copied, 1)
                    if (t := tail(n, 9)) is not None:
                        for piece in range(2):
                            act.wait_ge(t_done[piece], 1).then_inc(t_done[piece], -1)
                            act_.activation(mix_t[:, 4 * piece:4 * piece + 4, :].rearrange("p i n -> p (i n)"), TP[piece][:], ACT.Copy)
                            act.drain().then_inc(t_free[piece], 1)
                        act.sem_inc(mix_ready, 1)
                    if tail(n, 12) is not None:
                        act.wait_ge(x1t_landed, 16).then_inc(x1t_landed, -16)
                        for piece in range(2):
                            act.wait_ge(t_done[piece], 1).then_inc(t_done[piece], -1)
                            act_.activation(x1t[:, 4 * piece:4 * piece + 4, :].rearrange("p i n -> p (i n)"), TP[piece][:], ACT.Copy)
                            if n == 12:
                                act_.activation(x1t_first[:, 4 * piece:4 * piece + 4, :].rearrange("p i n -> p (i n)"), TP[piece][:], ACT.Copy)
                            act.drain().then_inc(t_free[piece], 1)
                        if n == 12:
                            act.sem_inc(x1t_first_ready, 1)
                        act.sem_inc(x1t_ready, 1)
                        act.sem_inc(x1_free, 1)
                    if choice(n, 0) is not None:
                        act.wait_ge(q_done, 1).then_inc(q_done, -1)
                        act_.activation(q_pair[:], OP[:], ACT.Copy).then_inc(q_copied, 1)
                    if choice(n, 1) is not None:
                        act.wait_ge(qt_done, 1).then_inc(qt_done, -1)
                        act_.activation(qt_pair[:], OP[:], ACT.Copy).then_inc(qt_copied, 1)
                    if choice(n, 2) is not None:
                        act.wait_ge(pair_scored, 1).then_inc(pair_scored, -1)
                        act.sem_inc(wq_free, 1)
                        act.wait_ge(pair_free, 1).then_inc(pair_free, -1)
                        act_.activation(sc_pair[:], OP[:], ACT.Copy)
                        act.drain().then_inc(pair_for_pe, 1)
                        act.sem_inc(pair_for_dve, 2)
                act.wait_ge(dots_ready, 1).then_inc(dots_ready, -1)
                act_.activation(dots_first[:], dots_first[:], ACT.Gelu).then_inc(gelu_ready, 1)

            @block.vector
            def _(dve):
                dve.sem_inc(op_free, 1)
                dve.sem_inc(pair_free, 1)
                dve.sem_inc(rows_free, U_FIRST_RING)
                dve.wait_ge(iota_ready, 1)
                vec.tensor_copy(b.iota16[:], b.iota_i[:])
                for n in range(last_step + 1):
                    if n < items:
                        keys = (n // DA_HEADS + 1) * P
                        for c in range(2):
                            dve.wait_ge(sc_done[c], 1).then_inc(sc_done[c], -1)
                            vec.tensor_reduce(neg_mx[:, n % 2, c:c + 1], SC[c][:, 0:keys], AX.X, ALU.min)
                            dve.drain().then_inc(mx_ready[c], 1)
                    if 1 <= n < items + 1:
                        m = n - 1
                        keys = (m // DA_HEADS + 1) * P
                        p0, p1 = probs0[:, m % 3, 0:keys], probs1[:, m % 2, 0:keys]
                        inv = rinv[:, m // DA_HEADS % 2, m % DA_HEADS, :]
                        dve.wait_ge(probs_ready, 1).then_inc(probs_ready, -1)
                        vec.reciprocal(inv, rsum[:, m % 3, :])
                        dve.drain()
                        vec.scalar_tensor_tensor(out=ratio[:], in0=inv[:, 1:2], scalar=minus_lam[:, 0:1],
                                                 in1=rsum[:, m % 3, 0:1], op0=ALU.mult, op1=ALU.mult)
                        dve.drain()
                        vec.scalar_tensor_tensor(out=p0, in0=p1, scalar=ratio[:, 0:1], in1=p0, op0=ALU.mult, op1=ALU.add)
                        dve.drain().then_inc(w_ready, 1)
                    if tail(n, 7) is not None:
                        dve.wait_ge(att_copied, 1).then_inc(att_copied, -1)
                        vec.tensor_scalar(av[:], av[:], 1.0 / DA_V, RMS_EPS, ALU.mult, ALU.add)
                        dve.drain().then_inc(av_ready, 1)
                    if tail(n, 8) is not None:
                        if n == 8:
                            dve.wait_ge(norm_in, 48)
                            vec.tensor_scalar(sub_g[:], sub_g[:], 1.0 - LAMBDA_INIT, None, ALU.mult)
                            dve.drain()
                        dve.wait_ge(ar_ready, 1).then_inc(ar_ready, -1)
                        for h in range(DA_HEADS):
                            part = att[:, h * DA_V:(h + 1) * DA_V]
                            vec.scalar_tensor_tensor(out=part, in0=part, scalar=ar[:, h:h + 1], in1=sub_g[:],
                                                     op0=ALU.mult, op1=ALU.mult)
                        dve.drain().then_inc(att_ready, 1)
                    if (t := tail(n, 10)) is not None:
                        dve.wait_ge(xtile_in, 16).then_inc(xtile_in, -16)
                        for half in range(2):
                            part = x1[:, t % 2, half * 512:(half + 1) * 512]
                            dve.wait_ge(op_done, 1).then_inc(op_done, -1)
                            vec.scalar_tensor_tensor(out=part, in0=part, scalar=ALPHA, in1=OP[:],
                                                     op0=ALU.mult, op1=ALU.add)
                            dve.drain().then_inc(op_free, 1)
                            vec.bn_stats(stats[:, half, :], part)
                        dve.drain()
                        vec.bn_aggr(mv[:], stats[:].rearrange("p a b -> p (a b)"))
                        dve.drain()
                        vec.tensor_scalar(var[:], mv[:, 1:2], LN_EPS, None, ALU.add)
                        dve.drain().then_inc(var_ready, 1)
                    if (t := tail(n, 11)) is not None:
                        tile = x1[:, t % 2, :]
                        dve.wait_ge(rstd_ready, 1).then_inc(rstd_ready, -1)
                        vec.tensor_scalar(tile, tile, mv[:, 0:1], rstd[:, 0:1], ALU.subtract, ALU.mult)
                        dve.drain()
                        if t == NT - 1:
                            vec.tensor_tensor(tile, tile, g1[:], ALU.mult)
                            dve.drain()
                            vec.tensor_tensor(tile, tile, b1[:], ALU.add)
                            dve.drain()
                        dve.sem_inc(normed, 1)
                    for which in range(2):
                        if (g := choice(n, 5 + which)) is not None:
                            at = slice(which * DKEY, (which + 1) * DKEY)
                            head = 2 * g + which
                            choose_experts(vec, dve, b, sc_pair[:, at], ids_first[:, head * TOPK:(head + 1) * TOPK],
                                           pair_for_dve, pair_seen, top_free, top_ready).then_inc(ids_ready, 1)
                            if which:
                                dve.wait_ge(pair_seen, 2).then_inc(pair_seen, -2)
                                dve.sem_inc(pair_free, 1)
                    for k in products(n):
                        if k == 0:
                            dve.wait_ge(x1_first_ready, 1)
                        slot = k % U_FIRST_RING
                        dve.wait_ge(rows_landed[slot], (k // U_FIRST_RING + 1) * 16)
                        vec.tensor_tensor_reduce(u_rows[:, slot, :], u_rows[:, slot, :], x1_first[:], 1.0, 0.0, ALU.mult, ALU.add,
                                                 dots_first[:, k:k + 1]).then_inc(rows_free, 1)
                dve.drain().then_inc(dots_ready, 1)
                dve.wait_ge(top_free, 1).then_inc(top_free, -1)
                by_slot = "p (h k) -> p h k"
                gates = coef_first[:].rearrange(by_slot, k=TOPK)
                exps = exp_first[:, 0:FIRST_SLOTS].rearrange(by_slot, k=TOPK)
                vec.tensor_reduce(sums_first[:], exps, AX.X, ALU.add)
                dve.drain()
                vec.reciprocal(sums_first[:], sums_first[:])
                dve.drain()
                vec.tensor_tensor(gates, exps, sums_first[:].unsqueeze(2).broadcast_to([P, FIRST_HEADS, TOPK]), ALU.mult)
                dve.drain()
                dve.wait_ge(gelu_ready, 1).then_inc(gelu_ready, -1)
                vec.tensor_tensor(coef_first[:], coef_first[:], dots_first[:], ALU.mult)


def refine_rsqrt(nc, dve, out, var, std, tmp):
    vec = nc.vector
    vec.reciprocal(out, std)
    dve.drain()
    vec.tensor_tensor(tmp, out, out, ALU.mult)
    dve.drain()
    vec.tensor_tensor(tmp, tmp, var, ALU.mult)
    dve.drain()
    vec.tensor_scalar(tmp, tmp, -0.5, 1.5, ALU.mult, ALU.add)
    dve.drain()
    vec.tensor_tensor(out, out, tmp, ALU.mult)
    dve.drain()


def build_experts(nc, x1_dram, x1t_dram, ids_first, exp_first, coef_first, peer_wq, keys_t, peer_u, peer_v, ln2_g, ln2_b, out):
    with ExitStack() as ctx:
        def sb(name, shape, dt=F32):
            return ctx.enter_context(nc.sbuf_tensor(name, shape, dt))

        def ps(name, shape):
            return ctx.enter_context(nc.psum_tensor(name, shape, F32))

        def sem(name):
            return ctx.enter_context(nc.semaphore(name))

        wq = sb("wq", [P, KC, HEADS * DKEY])
        keys = sb("keys", [P, HEADS * 2 * NKEYS])
        u_ring = sb("u_ring", [P, RING, D])
        v_ring = sb("v_ring", [P, RING, D])
        x1t_sel = sb("x1t_sel", [P, KC, P])
        x1_u = sb("x1_u", [P, D])
        g2 = sb("g2", [P, D])
        b2 = sb("b2", [P, D])
        y = sb("y", [P, D])
        ids_all = sb("ids_all", [P, NT * SLOTS], U32)
        exp_all = sb("exp_all", [P, NT * SLOTS])
        coef_all = sb("coef_all", [P, NT * SLOTS])
        ids_u = sb("ids_u", [P, 2, TOPK], U32)
        ids_v = sb("ids_v", [P, 2, TOPK], U32)
        coef_v = sb("coef_v", [P, 2, TOPK])
        dots = sb("dots", [P, 2, TOPK])
        gelu = sb("gelu", [P, 2, TOPK])
        rsum = sb("rsum", [P, 1])
        zero = sb("zero2", [P, 512])
        diag = sb("diag", [P, DIAGS, P])
        ident = sb("ident2", [P, P])
        alpha_ident = sb("alpha_ident", [P, P])
        q_sb = sb("q_sb", [P, DKEY])
        qt_sb = sb("qt_sb", [P, 2, P])
        b = Choice(sb, "_later")
        stats = sb("stats", [P, 2, 6])
        mv = sb("mv", [P, 2])
        rstd = sb("rstd", [P, 1])
        var = sb("var2", [P, 1])
        std = sb("std2", [P, 1])
        tmp = sb("tmp2", [P, 1])

        acc = [ps(f"acc{i}", [P, 512]) for i in range(2)]
        q_ps = ps("q_ps", [P, 512])
        qt_ps = ps("qt_ps", [P, 512])
        sc_ps = ps("sc_ps", [P, 512])

        weights_in = sem("weights_in2")
        keys_in = sem("keys_in")
        head_weights = sem("head_weights")
        ln2_in = sem("ln2_in")
        sel_in = sem("sel_in")
        sel_free = sem("sel_free")
        xu_in = sem("xu_in")
        xu_free = sem("xu_free")
        xu_for_pe = sem("xu_for_pe")
        opened = sem("opened")
        u_landed = [sem(f"u_landed{i}") for i in range(RING)]
        v_landed = [sem(f"v_landed{i}") for i in range(RING)]
        u_free = sem("u_free")
        v_free = sem("v_free")
        first_copied = sem("first_copied")
        ids_ready = sem("ids_ready")
        q_done = sem("q_done")
        q_copied = sem("q_copied")
        qt_done = sem("qt_done")
        qt_copied = sem("qt_copied")
        sc_done = sem("sc_done")
        sc_free = sem("sc_free")
        top_ready = sem("top_ready")
        top_free = sem("top_free")
        dots_ready = sem("dots_ready")
        gelu_ready = sem("gelu_ready")
        coef_ready = sem("coef_ready")
        diag_ready = sem("diag_ready")
        diag_free = sem("diag_free")
        acc_done = sem("acc_done")
        acc_free = sem("acc_free")
        y_ready = sem("y_ready")
        y_free = sem("y_free")
        var_ready = sem("var_ready2")
        std_ready = sem("std_ready2")
        consts = sem("consts2")
        zero_ready = sem("zero_ready")
        pool_step = sem("pool_step")

        def rounds(eng, body):
            body(1, True, True, False)
            with eng.Fori(2, NT) as r:
                body(r, True, True, True)
            body(NT, False, True, True)
            body(NT + 1, False, False, True)

        def groups(r, eng, group, turn):
            for g in range(LAG):
                group(g, g % 2, True)
            turn()
            with eng.Fori(LAG // 2, HEADS // 2) as half:
                for par in range(2):
                    group(half * 2 + par, par, not (isinstance(r, int) and r == NT))

        block = ctx.enter_context(nc.Block())

        @block.sync
        def _(sp):
            def round_(r, sel, v, ended):
                if sel:
                    sp.wait_ge(sel_free, 1).then_inc(sel_free, -1)
                    sp.dma_start(x1t_sel[:].rearrange("p c n -> p (c n)"),
                                 x1t_dram[bass.ds(r * P, P), :]).then_inc(sel_in, 16)
                if ended:
                    sp.wait_ge(y_ready, 1).then_inc(y_ready, -1)
                    sp.dma_start(out[bass.ds((r - 2) * P, P), :], y[:]).then_inc(y_free, 16)
                if sel:
                    sp.wait_ge(xu_free, 1).then_inc(xu_free, -1)
                    sp.dma_start(x1_u[:], x1_dram[bass.ds(r * P, P), :]).then_inc(xu_in, 16)

            sp.dma_start(x1_u[:], x1_dram[0:P, :]).then_inc(xu_in, 16)
            sp.wait_ge(sel_free, 1).then_inc(sel_free, -1)
            sp.dma_start(x1t_sel[:].rearrange("p c n -> p (c n)"), x1t_dram[P:2 * P, :]).then_inc(sel_in, 16)
            sp.dma_start(keys[:], keys_t).then_inc(keys_in, 16)
            for g in range(HEADS):
                part = slice(g * DKEY, (g + 1) * DKEY)
                sp.dma_start(wq[:, :, part], peer_wq[:, part].rearrange("(c p) n -> p c n", p=P)).then_inc(weights_in, 16)
                sp.wait_ge(weights_in, 16).then_inc(weights_in, -16)
                sp.sem_inc(head_weights, 1)
            sp.wait_ge(xu_free, 1).then_inc(xu_free, -1)
            sp.dma_start(x1_u[:], x1_dram[P:2 * P, :]).then_inc(xu_in, 16)
            sp.dma_start(g2[:], ln2_g.partition_broadcast(P)).then_inc(ln2_in, 16)
            sp.dma_start(b2[:], ln2_b.partition_broadcast(P)).then_inc(ln2_in, 16)
            with sp.Fori(2, NT) as r:
                round_(r, True, True, True)
            round_(NT, False, True, True)
            round_(NT + 1, False, False, True)
            sp.wait_ge(y_free, 16)

        @block.gpsimd
        def _(pool):
            pool.iota(b.iota_i[:], [[1, TOPK]], base=0, channel_multiplier=0).then_inc(consts, 1)
            pool.memset(ident[:], 0.0).then_inc(pool_step, 1)
            pool.memset(alpha_ident[:], 0.0).then_inc(pool_step, 1)
            pool.wait_ge(pool_step, 2).then_inc(pool_step, -2)
            for m, diagonal in ((ident, 1.0), (alpha_ident, ALPHA)):
                pool.affine_select(out=m[:], in_=m[:], compare_op=ALU.not_equal, fill=diagonal, base=0,
                                   pattern=[[-1, P]], channel_multiplier=1).then_inc(consts, 1)

            def gather(ring, slot, table, ids, par, j, landed):
                pool.indirect_dma_start(ring[:, slot, :], None, table,
                                        bass.IndirectOffsetOnAxis(ap=ids[:, par, j:j + 1], axis=0))\
                    .then_inc(landed[slot], 16)

            pool.wait_ge(first_copied, 1).then_inc(first_copied, -1)

            def round_(r, sel, v, ended):
                def group(g, par, u):
                    if u:
                        pool.wait_ge(ids_ready, 1).then_inc(ids_ready, -1)
                        pool.tensor_copy(ids_u[:, par, :], ids_all[:, bass.ds((r * HEADS + g - LAG) * TOPK, TOPK)])\
                            .then_inc(pool_step, 1)
                        pool.wait_ge(pool_step, 1).then_inc(pool_step, -1)
                    pool.tensor_copy(ids_v[:, par, :], ids_all[:, bass.ds(((r - 1) * HEADS + g) * TOPK, TOPK)])\
                        .then_inc(pool_step, 1)
                    pool.wait_ge(pool_step, 1).then_inc(pool_step, -1)
                    for j in range(TOPK):
                        slot = j % RING
                        if u:
                            pool.wait_ge(u_free, 1).then_inc(u_free, -1)
                            gather(u_ring, slot, peer_u, ids_u, par, j, u_landed)
                        pool.wait_ge(v_free, 1).then_inc(v_free, -1)
                        gather(v_ring, slot, peer_v, ids_v, par, j, v_landed)
                if v:
                    groups(r, pool, group, lambda: None)
            rounds(pool, round_)

        @block.tensor
        def _(pe):
            pe.sem_inc(v_free, RING)
            pe.wait_ge(consts, 3)
            pe.wait_ge(zero_ready, 1)

            def round_(r, sel, v, ended):
                if ended:
                    for c in range(2):
                        last = nc.tensor.matmul(acc[c][:], zero[:, 0:P], zero[:], start=False, stop=True, skip_group_check=True)
                    last.then_inc(acc_done, 1)
                if v:
                    pe.wait_ge(xu_for_pe, 1).then_inc(xu_for_pe, -1)
                    pe.wait_ge(acc_free, 1).then_inc(acc_free, -1)
                    for c in range(2):
                        last = nc.tensor.matmul(acc[c][:], alpha_ident[:], x1_u[:, c * 512:(c + 1) * 512],
                                                start=True, stop=False, skip_group_check=True)
                    last.then_inc(opened, 1)

                def group(g, par, u):
                    def add_rows(j0, j1):
                        for j in range(j0, j1):
                            slot = j % RING
                            pe.wait_ge(diag_ready, 1).then_inc(diag_ready, -1)
                            pe.wait_ge(v_landed[slot], (((r - 1) * HEADS + g) * (TOPK // RING) + j // RING + 1) * 16)
                            nc.tensor.matmul(acc[0][:], diag[:, j % DIAGS, :], v_ring[:, slot, 0:512],
                                             start=False, stop=False, skip_group_check=True)\
                                .then_inc(diag_free, 1)
                            nc.tensor.matmul(acc[1][:], diag[:, j % DIAGS, :], v_ring[:, slot, 512:1024],
                                             start=False, stop=False, skip_group_check=True)\
                                .then_inc(v_free, 1)

                    add_rows(0, 4)
                    if sel:
                        if isinstance(g, int) and g == 0:
                            if isinstance(r, int):
                                pe.wait_ge(keys_in, 16)
                            pe.wait_ge(sel_in, 16).then_inc(sel_in, -16)
                        if isinstance(r, int):
                            pe.wait_ge(head_weights, 1).then_inc(head_weights, -1)
                        for c in range(KC):
                            last = nc.tensor.matmul(q_ps[:, 0:DKEY], x1t_sel[:, c, :], wq[:, c, bass.ds(g * DKEY, DKEY)],
                                                    start=(c == 0), stop=(c == KC - 1))
                        last.then_inc(q_done, 1)
                    add_rows(4, 8)
                    if sel:
                        pe.wait_ge(q_copied, 1).then_inc(q_copied, -1)
                        for c in range(2):
                            last = nc.tensor.transpose(qt_ps[:, c * P:(c + 1) * P], q_sb[:, c * P:(c + 1) * P], ident[:])
                        last.then_inc(qt_done, 1)
                    add_rows(8, 12)
                    if sel:
                        pe.wait_ge(qt_copied, 1).then_inc(qt_copied, -1)
                        pe.wait_ge(sc_free, 1).then_inc(sc_free, -1)
                        for c in range(2):
                            last = nc.tensor.matmul(sc_ps[:, c * NKEYS:(c + 1) * NKEYS], qt_sb[:, c, :],
                                                    keys[:, bass.ds(g * 2 * NKEYS + c * NKEYS, NKEYS)], start=True, stop=True)
                        last.then_inc(sc_done, 1)
                    add_rows(12, 16)
                if v:
                    groups(r, pe, group, lambda: None)
            rounds(pe, round_)

        @block.scalar
        def _(act):
            act.sem_inc(sel_free, 1)
            act.sem_inc(top_free, 1)
            act.wait_ge(consts, 3)

            def round_(r, sel, v, ended):
                if ended:
                    act.wait_ge(var_ready, 1).then_inc(var_ready, -1)
                    nc.scalar.activation(std[:], var[:], ACT.Sqrt).then_inc(std_ready, 1)

                def group(g, par, u):
                    def diagonals(j0, j1):
                        for j in range(j0, j1):
                            act.wait_ge(diag_free, 1).then_inc(diag_free, -1)
                            nc.scalar.activation(diag[:, j % DIAGS, :], ident[:], ACT.Copy,
                                                 scale=coef_v[:, par, j:j + 1]).then_inc(diag_ready, 1)
                    act.wait_ge(coef_ready, 1).then_inc(coef_ready, -1)
                    nc.scalar.activation(coef_v[:, par, :], coef_all[:, bass.ds(((r - 1) * HEADS + g) * TOPK, TOPK)], ACT.Copy)
                    act.drain()
                    diagonals(0, 8)
                    if sel:
                        act.wait_ge(q_done, 1).then_inc(q_done, -1)
                        nc.scalar.activation(q_sb[:], q_ps[:, 0:DKEY], ACT.Copy).then_inc(q_copied, 1)
                    diagonals(8, 12)
                    if sel:
                        act.wait_ge(qt_done, 1).then_inc(qt_done, -1)
                        nc.scalar.activation(qt_sb[:].rearrange("p c n -> p (c n)"), qt_ps[:, 0:2 * P], ACT.Copy).then_inc(qt_copied, 1)
                    diagonals(12, 16)
                    if sel:
                        act.wait_ge(top_ready, 1).then_inc(top_ready, -1)
                        nc.scalar.activation(exp_all[:, bass.ds((r * HEADS + g) * TOPK, TOPK)], b.top[:], ACT.Exp,
                                             bias=b.neg_max[:, 0:1]).then_inc(top_free, 1)
                    if u:
                        act.wait_ge(dots_ready, 1).then_inc(dots_ready, -1)
                        nc.scalar.activation(gelu[:, par, :], dots[:, par, :], ACT.Gelu).then_inc(gelu_ready, 1)
                if v:
                    groups(r, act, group, lambda: None)
                if sel:
                    act.sem_inc(sel_free, 1)
            rounds(act, round_)

        @block.vector
        def _(dve):
            vec = nc.vector
            dve.sem_inc(u_free, RING)
            dve.sem_inc(sc_free, 1)
            dve.sem_inc(acc_free, 1)
            dve.sem_inc(diag_free, DIAGS - 1)
            dve.sem_inc(y_free, 16)
            vec.memset(zero[:], 0.0).then_inc(zero_ready, 1)
            dve.wait_ge(consts, 3)
            vec.tensor_copy(b.iota16[:], b.iota_i[:])
            vec.tensor_copy(ids_all[:, 0:SLOTS], ids_first[:])
            vec.tensor_copy(exp_all[:, 0:SLOTS], exp_first[:])
            vec.tensor_copy(coef_all[:, 0:FIRST_SLOTS], coef_first[:])
            dve.drain()
            dve.sem_inc(first_copied, 1)
            dve.sem_inc(coef_ready, FIRST_HEADS)
            dve.sem_inc(ids_ready, HEADS - FIRST_HEADS)
            dve.wait_ge(xu_in, 16).then_inc(xu_in, -16)
            dve.sem_inc(xu_for_pe, 1)

            def round_(r, sel, v, ended):
                if isinstance(r, int) and r == NT:
                    dve.wait_ge(top_free, 1).then_inc(top_free, -1)

                def norm():
                    dve.wait_ge(acc_done, 1).then_inc(acc_done, -1)
                    for c in range(2):
                        vec.bn_stats(stats[:, c, :], acc[c][:])
                    dve.drain()
                    vec.bn_aggr(mv[:], stats[:].rearrange("p a b -> p (a b)"))
                    dve.drain()
                    vec.tensor_scalar(var[:], mv[:, 1:2], LN_EPS, None, ALU.add).then_inc(var_ready, 1)
                    dve.wait_ge(std_ready, 1).then_inc(std_ready, -1)
                    refine_rsqrt(nc, dve, rstd[:], var[:], std[:], tmp[:])
                    dve.wait_ge(y_free, 16).then_inc(y_free, -16)
                    for c in range(2):
                        vec.tensor_scalar(y[:, c * 512:(c + 1) * 512], acc[c][:], mv[:, 0:1], rstd[:, 0:1],
                                          ALU.subtract, ALU.mult)
                    dve.drain().then_inc(acc_free, 1)
                    dve.wait_ge(ln2_in, 32)
                    vec.tensor_tensor(y[:], y[:], g2[:], ALU.mult)
                    dve.drain()
                    vec.tensor_tensor(y[:], y[:], b2[:], ALU.add)
                    dve.drain().then_inc(y_ready, 1)

                def group(g, par, u):
                    for j in range(TOPK):
                        slot = j % RING
                        if ended and isinstance(g, int) and g == 0 and j == NORM_AT:
                            norm()
                        if sel and j == 13:
                            choose_experts(vec, dve, b, sc_ps, ids_all[:, bass.ds((r * HEADS + g) * TOPK, TOPK)],
                                           sc_done, sc_free, top_free, top_ready).then_inc(ids_ready, 1)
                        if u:
                            dve.wait_ge(u_landed[slot], (((r - 1) * HEADS + g) * (TOPK // RING) + j // RING + 1) * 16)
                            vec.tensor_tensor_reduce(u_ring[:, slot, :], u_ring[:, slot, :], x1_u[:], 1.0, 0.0,
                                                     ALU.mult, ALU.add, dots[:, par, j:j + 1]).then_inc(u_free, 1)
                    if u:
                        dve.drain().then_inc(dots_ready, 1)
                        at = bass.ds((r * HEADS + g - LAG) * TOPK, TOPK)
                        vec.tensor_reduce(rsum[:], exp_all[:, at], AX.X, ALU.add)
                        dve.drain()
                        vec.reciprocal(rsum[:], rsum[:])
                        dve.drain()
                        dve.wait_ge(gelu_ready, 1).then_inc(gelu_ready, -1)
                        vec.scalar_tensor_tensor(out=coef_all[:, at], in0=gelu[:, par, :], scalar=rsum[:, 0:1],
                                                 in1=exp_all[:, at], op0=ALU.mult, op1=ALU.mult).then_inc(coef_ready, 1)

                def turn():
                    dve.wait_ge(opened, 1).then_inc(opened, -1)
                    if sel:
                        dve.sem_inc(xu_free, 1)
                        dve.wait_ge(xu_in, 16).then_inc(xu_in, -16)
                        dve.sem_inc(xu_for_pe, 1)
                if v:
                    groups(r, dve, group, turn)
                else:
                    norm()
            rounds(dve, round_)


_INS = ['x', 'x_t', 'positions', 'w_in', 'w_out', 'lambda_q1', 'lambda_k1', 'lambda_q2', 'lambda_k2', 'subln_g', 'conv_w',
        'conv_b', 'dt_bias', 'a_log', 'd_skip', 'ssd_norm_g', 'ln1_g', 'ln1_b', 'peer_wq', 'peer_keys', 'peer_u', 'peer_v',
        'ln2_g', 'ln2_b']


def build(nc, x, x_t, positions, w_in, w_out, lambda_q1, lambda_k1, lambda_q2, lambda_k2, subln_g, conv_w, conv_b, dt_bias,
          a_log, d_skip, ssd_norm_g, ln1_g, ln1_b, peer_wq, peer_keys, peer_u, peer_v, ln2_g, ln2_b, out):
    x1_dram = nc.dram_tensor("x1_rows", (T, D), F32).ap()
    x1t_dram = nc.dram_tensor("x1_tiles_t", (T, D), F32).ap()
    with ExitStack() as kept:
        ids_first = kept.enter_context(nc.sbuf_tensor("ids_first", [P, SLOTS], U32))
        exp_first = kept.enter_context(nc.sbuf_tensor("exp_first", [P, SLOTS], F32))
        coef_first = kept.enter_context(nc.sbuf_tensor("coef_first", [P, FIRST_SLOTS], F32))
        build_mixer(nc, x, x_t, positions, w_in, w_out, (lambda_q1, lambda_k1, lambda_q2, lambda_k2), subln_g, conv_w, conv_b,
                    dt_bias, a_log, d_skip, ssd_norm_g, ln1_g, ln1_b, x1_dram, x1t_dram, peer_wq, peer_keys, peer_u,
                    ids_first, exp_first, coef_first, kept)
        build_experts(nc, x1_dram, x1t_dram, ids_first, exp_first, coef_first, peer_wq, peer_keys, peer_u, peer_v, ln2_g, ln2_b, out)


def kernel(**inputs):
    import concourse.bacc as _bacc
    from concourse.bass_utils import run_bass_kernel_spmd as _run

    a = {name: np.asarray(v)[0] for name, v in inputs.items()}
    a["x_t"] = a["x"].T
    a["positions"] = a["positions"].reshape(NT, P).T
    a["conv_w"] = a["conv_w"].reshape(CONV, KC, P).transpose(2, 1, 0)
    a["conv_b"] = a["conv_b"].reshape(KC, P).T
    a["peer_keys"] = a["peer_keys"].transpose(3, 0, 1, 2).reshape(P, HEADS * 2 * NKEYS)

    nc = _bacc.Bacc("TRN2", target_bir_lowering=False, num_devices=1)
    arrays, args = {}, []
    for name in _INS:
        arrays[f"in_{name}_dram"] = np.ascontiguousarray(a[name])
        args.append(nc.dram_tensor(f"in_{name}_dram", a[name].shape, mybir.dt.from_np(a[name].dtype), kind="ExternalInput").ap())
    args.append(nc.dram_tensor("out_0_dram", (T, D), F32, kind="ExternalOutput").ap())
    build(nc, *args)
    r = _run(nc, [arrays], core_ids=[0])
    return r.results[0]["out_0_dram"].reshape(1, T, D)
```
